# Optimizing a Trainium2 kernel written in Bass

```python
import math
import jax, jax.numpy as jnp
from jax import lax
import numpy as np

D_MODEL = 1024
BATCH = 1
SEQ = 512
DEPTH = 1

CTX_LEN = 256
GRID_W = 64
A_HEADS = 4
A_DK = 128
A_DV = 128
A_KW = A_HEADS * A_DK
A_VW = A_HEADS * A_DV
A_CHUNK = 64
B_WIDTH = 512
HYENA_ORDER = 2
HYENA_SHORT = 3
HYENA_EMB = 33
HYENA_BANDS = (HYENA_EMB - 1) // 2
HYENA_FFN = 64
HYENA_FAST_DECAY = 0.3
HYENA_SLOW_DECAY = 1.5
HYENA_TARGET = 1e-2
HYENA_SHIFT = 0.05
HYENA_L1_EPS = 1e-6
D_FF = 2816
N_MOD = 9
RMS_EPS = 1e-6
COL_V = 0
COL_FFW = COL_V + A_VW
COL_FBW = COL_FFW + A_KW
COL_Q = COL_FBW + A_KW
COL_G = COL_Q + A_KW
COL_HY = COL_G + A_VW
COL_MERGE = COL_HY + 3 * B_WIDTH
IN_COLS = COL_MERGE + 2 * D_MODEL


def rms_norm(x):
    xf = x.astype(jnp.float32)
    return (xf * lax.rsqrt(jnp.mean(xf * xf, axis=-1, keepdims=True) + RMS_EPS)).astype(x.dtype)

def modulate(x, shift, scale):
    return x * (1.0 + scale) + shift

def swiglu(x, wg, wu, wd):
    return (jax.nn.silu(x @ wg) * (x @ wu)) @ wd

def half_ffn(h, shift, scale, gate, wg, wu, wd):
    return h + 0.5 * gate * swiglu(modulate(rms_norm(h), shift, scale), wg, wu, wd)

def grid_pos_embed(n_tokens):
    rows = n_tokens // GRID_W
    quarter = D_MODEL // 4
    omega = 1.0 / (10000.0 ** (jnp.arange(quarter, dtype=jnp.float32) / quarter))
    ar = jnp.arange(rows, dtype=jnp.float32)[:, None] * omega
    ac = jnp.arange(GRID_W, dtype=jnp.float32)[:, None] * omega
    er = jnp.concatenate([jnp.sin(ar), jnp.cos(ar)], axis=-1)
    ec = jnp.concatenate([jnp.sin(ac), jnp.cos(ac)], axis=-1)
    emb = jnp.concatenate([jnp.broadcast_to(er[:, None, :], (rows, GRID_W, D_MODEL // 2)),
                           jnp.broadcast_to(ec[None, :, :], (rows, GRID_W, D_MODEL // 2))], axis=-1)
    return emb.reshape(rows * GRID_W, D_MODEL)

def to_heads(a):
    b, l, w = a.shape
    return a.reshape(b, l, A_HEADS, w // A_HEADS).transpose(0, 2, 1, 3)

def hgrn2_forget(z, lb):
    f = lb + (1.0 - lb) * jax.nn.sigmoid(z.astype(jnp.float32))
    return to_heads(jnp.log(f)), to_heads(1.0 - f)

def hgrn2_chunk_scan(q, k, v, logf, s0):
    b, h, l, dk = q.shape
    n_chunks = l // A_CHUNK

    def to_chunks(a):
        return a.reshape(b, h, n_chunks, A_CHUNK, a.shape[-1]).transpose(2, 0, 1, 3, 4)

    within_scan = jnp.tril(jnp.ones((A_CHUNK, A_CHUNK), dtype=bool))[:, :, None]

    def step(s, inp):
        qb, kb, vb, gb = inp
        cum = jnp.cumsum(gb, axis=2)
        diff = cum[:, :, :, None, :] - cum[:, :, None, :, :]
        decay = jnp.exp(jnp.where(within_scan, diff, -jnp.inf))
        scores = jnp.einsum('bhtsd,bhsd->bhts', qb[:, :, :, None, :] * decay, kb)
        o = scores @ vb + (qb * jnp.exp(cum)) @ s
        last = cum[:, :, -1:, :]
        s_new = jnp.exp(last[:, :, 0, :])[..., None] * s + jnp.einsum('bhsd,bhse->bhde', kb * jnp.exp(last - cum), vb)
        return s_new, o

    s_final, oc = lax.scan(step, s0, (to_chunks(q), to_chunks(k), to_chunks(v), to_chunks(logf)))
    o = oc.transpose(1, 2, 0, 3, 4).reshape(b, h, l, v.shape[-1])
    return o, s_final

def hgrn2_final_state(k, v, logf):
    cum = jnp.cumsum(logf, axis=2)
    return jnp.einsum('bhld,bhle->bhde', k * jnp.exp(cum[:, :, -1:, :] - cum), v)

def flip_seq(a):
    return jnp.flip(a, axis=2)

def hgrn2_bidir(q, v, logf_fw, k_fw, logf_bw, k_bw, s0_fw, s0_bw):
    o_fw, s_fw = hgrn2_chunk_scan(q, k_fw, v, logf_fw, s0_fw)
    o_bw, s_bw = hgrn2_chunk_scan(flip_seq(q), flip_seq(k_bw), flip_seq(v), flip_seq(logf_bw), s0_bw)
    return o_fw + flip_seq(o_bw), s_fw, s_bw

def context_states(nc, w_in, lb):
    p = nc @ w_in[:, :COL_Q]
    v = to_heads(p[..., COL_V:COL_FFW]).astype(jnp.float32)
    logf_fw, k_fw = hgrn2_forget(p[..., COL_FFW:COL_FBW], lb[0])
    logf_bw, k_bw = hgrn2_forget(p[..., COL_FBW:COL_Q], lb[1])
    s_fw = hgrn2_final_state(k_fw, v, logf_fw)
    s_bw = hgrn2_final_state(flip_seq(k_bw), flip_seq(v), flip_seq(logf_bw))
    return s_fw, s_bw

def short_conv(u, w, bias):
    l = u.shape[1]
    pad = HYENA_SHORT // 2
    up = jnp.pad(u, ((0, 0), (pad, pad), (0, 0)))
    out = bias
    for j in range(HYENA_SHORT):
        out = out + up[:, j:j + l] * w[j]
    return out

def hyena_pos_features(l):
    p = jnp.arange(l, dtype=jnp.float32)
    t = p / (l - 1)
    w = 2.0 * math.pi * p / l
    f = jnp.linspace(1e-4, HYENA_BANDS - 1, HYENA_BANDS, dtype=jnp.float32)
    ang = w[:, None] * f[None, :]
    z = jnp.concatenate([t[:, None], jnp.cos(ang), -jnp.sin(ang)], axis=-1)
    return t, z

def hyena_kernels(l, w1, b1, fr1, w2, b2, fr2, w3):
    t, z = hyena_pos_features(l)
    h = jnp.sin(fr1 * (z @ w1 + b1))
    h = jnp.sin(fr2 * (h @ w2 + b2))
    h = (h @ w3).astype(jnp.float32).reshape(l, HYENA_ORDER, 2, B_WIDTH)
    max_decay = math.log(HYENA_TARGET) / HYENA_FAST_DECAY
    min_decay = math.log(HYENA_TARGET) / HYENA_SLOW_DECAY
    deltas = jnp.abs(jnp.linspace(min_decay, max_decay, B_WIDTH, dtype=jnp.float32))
    window = jnp.exp(-t[:, None] * deltas[None, :]) + HYENA_SHIFT
    h = h * window[:, None, None, :]
    kern = jnp.concatenate([h[:, :, 0], jnp.flip(h[:, :, 1], axis=0)], axis=0)
    return kern / (jnp.sum(jnp.abs(kern), axis=0, keepdims=True) + HYENA_L1_EPS)

def fft_conv(u, kern):
    l = u.shape[1]
    uf = jnp.fft.rfft(u.astype(jnp.float32), n=2 * l, axis=1)
    kf = jnp.fft.rfft(kern, n=2 * l, axis=0)
    return jnp.fft.irfft(uf * kf[None], n=2 * l, axis=1)[:, :l]

def hyena(u3, kern, hy_bias):
    v, x1, x2 = jnp.split(u3, 3, axis=-1)
    z = v
    for o, gate in enumerate((x1, x2)):
        z = gate * (fft_conv(z, kern[:, o]).astype(z.dtype) + hy_bias[o] * z)
    return z

def token_mixers(n, s0_fw, s0_bw, kern, w_in, lb, a_norm_w, conv_w, conv_b, hy_bias, w_pa, w_pb, w_out):
    b, l, _ = n.shape
    p = n @ w_in
    v = to_heads(p[..., COL_V:COL_FFW]).astype(jnp.float32)
    logf_fw, k_fw = hgrn2_forget(p[..., COL_FFW:COL_FBW], lb[0])
    logf_bw, k_bw = hgrn2_forget(p[..., COL_FBW:COL_Q], lb[1])
    q = to_heads(jax.nn.silu(p[..., COL_Q:COL_G])).astype(jnp.float32)
    o, s_fw, s_bw = hgrn2_bidir(q, v, logf_fw, k_fw, logf_bw, k_bw, s0_fw, s0_bw)
    o = rms_norm(o.transpose(0, 2, 1, 3)) * a_norm_w
    o_a = o.reshape(b, l, A_VW).astype(n.dtype) * jax.nn.silu(p[..., COL_G:COL_HY])
    u3 = short_conv(p[..., COL_HY:COL_MERGE], conv_w, conv_b)
    o_b = hyena(u3, kern, hy_bias)
    g_a, g_b = jnp.split(p[..., COL_MERGE:], 2, axis=-1)
    y = jax.nn.sigmoid(g_a) * (o_a @ w_pa) + jax.nn.sigmoid(g_b) * (o_b @ w_pb)
    return y @ w_out, s_fw, s_bw

def first_inputs(seed: int = 0) -> dict:
    key = jax.random.key(seed)
    ks = jax.random.split(key, 32)
    nrm = jax.random.normal
    f32 = jnp.float32
    d = D_MODEL
    return {
        'x': nrm(ks[0], (BATCH, SEQ, d), f32),
        'c': nrm(ks[1], (BATCH, d), f32),
        'ctx': nrm(ks[2], (BATCH, CTX_LEN, d), f32),
        'c_ctx': nrm(ks[3], (d,), f32),
        'mod_w': nrm(ks[4], (DEPTH, d, N_MOD * d), f32) * d ** -0.5,
        'mod_b': nrm(ks[5], (DEPTH, N_MOD * d), f32) * 0.01,
        'ffn_w_gate': nrm(ks[6], (DEPTH, 2, d, D_FF), f32) * d ** -0.5,
        'ffn_w_up': nrm(ks[7], (DEPTH, 2, d, D_FF), f32) * d ** -0.5,
        'ffn_w_down': nrm(ks[8], (DEPTH, 2, D_FF, d), f32) * D_FF ** -0.5,
        'w_in': nrm(ks[9], (DEPTH, d, IN_COLS), f32) * d ** -0.5,
        'hgrn_lb_logits': nrm(ks[10], (DEPTH + 1, 2, A_KW), f32) * 0.1,
        'hgrn_norm_w': 1.0 + 0.1 * nrm(ks[11], (DEPTH, A_DV), f32),
        'hyena_conv_w': nrm(ks[12], (DEPTH, HYENA_SHORT, 3 * B_WIDTH), f32) * HYENA_SHORT ** -0.5,
        'hyena_conv_b': nrm(ks[13], (DEPTH, 3 * B_WIDTH), f32) * 0.01,
        'hyena_w1': nrm(ks[14], (DEPTH, HYENA_EMB, HYENA_FFN), f32) * HYENA_EMB ** -0.5,
        'hyena_b1': nrm(ks[15], (DEPTH, HYENA_FFN), f32) * 0.1,
        'hyena_freq1': 1.0 + 0.1 * nrm(ks[16], (DEPTH, HYENA_FFN), f32),
        'hyena_w2': nrm(ks[17], (DEPTH, HYENA_FFN, HYENA_FFN), f32) * HYENA_FFN ** -0.5,
        'hyena_b2': nrm(ks[18], (DEPTH, HYENA_FFN), f32) * 0.1,
        'hyena_freq2': 1.0 + 0.1 * nrm(ks[19], (DEPTH, HYENA_FFN), f32),
        'hyena_w3': nrm(ks[20], (DEPTH, HYENA_FFN, HYENA_ORDER * 2 * B_WIDTH), f32) * HYENA_FFN ** -0.5,
        'hyena_bias': nrm(ks[21], (DEPTH, HYENA_ORDER, B_WIDTH), f32),
        'w_proj_a': nrm(ks[22], (DEPTH, A_VW, d), f32) * A_VW ** -0.5,
        'w_proj_b': nrm(ks[23], (DEPTH, B_WIDTH, d), f32) * B_WIDTH ** -0.5,
        'w_out': nrm(ks[24], (DEPTH, d, d), f32) * d ** -0.5,
        'final_norm_w': 1.0 + 0.1 * nrm(ks[25], (d,), f32),
    }

def first_block(x, c, ctx, c_ctx, mod_w, mod_b, ffn_w_gate, ffn_w_up, ffn_w_down, w_in, hgrn_lb_logits,
              hgrn_norm_w, hyena_conv_w, hyena_conv_b, hyena_w1, hyena_b1, hyena_freq1, hyena_w2, hyena_b2,
              hyena_freq2, hyena_w3, hyena_bias, w_proj_a, w_proj_b, w_out, final_norm_w):
    n_lat = x.shape[1]
    n_ctx = ctx.shape[1]
    h = x + grid_pos_embed(n_lat).astype(x.dtype)[None]
    hc = ctx
    lb_all = jnp.cumsum(jax.nn.softmax(hgrn_lb_logits.astype(jnp.float32), axis=0), axis=0)
    for l in range(DEPTH):
        last = l == DEPTH - 1
        m = jnp.split((jax.nn.silu(c) @ mod_w[l] + mod_b[l])[:, None, :], N_MOD, axis=-1)
        mc = jnp.split((jax.nn.silu(c_ctx) @ mod_w[l] + mod_b[l])[None, None, :], N_MOD, axis=-1)
        h = half_ffn(h, m[0], m[1], m[2], ffn_w_gate[l, 0], ffn_w_up[l, 0], ffn_w_down[l, 0])
        hc = half_ffn(hc, mc[0], mc[1], mc[2], ffn_w_gate[l, 0], ffn_w_up[l, 0], ffn_w_down[l, 0])
        n = modulate(rms_norm(h), m[3], m[4])
        nc = modulate(rms_norm(hc), mc[3], mc[4])
        mix_w = (w_in[l], lb_all[l], hgrn_norm_w[l], hyena_conv_w[l], hyena_conv_b[l], hyena_bias[l],
                 w_proj_a[l], w_proj_b[l], w_out[l])
        filt_w = (hyena_w1[l], hyena_b1[l], hyena_freq1[l], hyena_w2[l], hyena_b2[l], hyena_freq2[l], hyena_w3[l])
        if last:
            s_fw, s_bw = context_states(nc, w_in[l], lb_all[l])
        else:
            zeros = jnp.zeros((hc.shape[0], A_HEADS, A_DK, A_DV), jnp.float32)
            out_c, s_fw, s_bw = token_mixers(nc, zeros, zeros, hyena_kernels(n_ctx, *filt_w), *mix_w)
            hc = hc + mc[5] * out_c
            hc = half_ffn(hc, mc[6], mc[7], mc[8], ffn_w_gate[l, 1], ffn_w_up[l, 1], ffn_w_down[l, 1])
        out, _, _ = token_mixers(n, s_fw, s_bw, hyena_kernels(n_lat, *filt_w), *mix_w)
        h = h + m[5] * out
        h = half_ffn(h, m[6], m[7], m[8], ffn_w_gate[l, 1], ffn_w_up[l, 1], ffn_w_down[l, 1])
    return rms_norm(h) * final_norm_w


DEPTH_2 = 2

D_MIX = D_MODEL
HEAD_DIM = 64
CONV_CH = D_MIX // 4
CONV_K = 3
ATT_HEADS = D_MIX // 2 // HEAD_DIM
ATT_KV_HEADS = 2
ATT_GROUP = ATT_HEADS // ATT_KV_HEADS
WINDOW = 128
BLOCK = 128
GLA_HEADS = D_MIX // 4 // HEAD_DIM
GLA_DK = HEAD_DIM
GLA_DV = HEAD_DIM
GLA_RANK = 16
GLA_NORMALIZER = 16.0
GLA_CHUNK = 32
D_FF_2 = ((8 * D_MODEL + 3 * 256 - 1) // (3 * 256)) * 256
N_MOD_2 = 6
ROPE_BASE = 10000.0
EPS = 1e-6
COL_SIZES = (CONV_CH, CONV_CH, CONV_CH,
             ATT_HEADS * HEAD_DIM, ATT_KV_HEADS * HEAD_DIM, ATT_KV_HEADS * HEAD_DIM,
             GLA_HEADS * GLA_DK, GLA_HEADS * GLA_DK, GLA_HEADS * GLA_DV, GLA_HEADS * GLA_DV,
             2 * GLA_RANK)
N_IN = sum(COL_SIZES)
COL_SPLITS = tuple(int(v) for v in np.cumsum(COL_SIZES)[:-1])


def rmsnorm(x, g):
    x32 = x.astype(jnp.float32)
    y = x32 * lax.rsqrt(jnp.mean(x32 * x32, axis=-1, keepdims=True) + EPS)
    return (y * g.astype(jnp.float32)).astype(x.dtype)

def heads(a, n):
    return a.reshape(a.shape[:-1] + (n, a.shape[-1] // n))

def axial_rope_tables(rows):
    t = jnp.arange(rows * GRID_W)
    row = (t // GRID_W).astype(jnp.float32)
    col = (t % GRID_W).astype(jnp.float32)
    n_freq = HEAD_DIM // 4
    inv_freq = ROPE_BASE ** (-jnp.arange(n_freq, dtype=jnp.float32) / n_freq)
    ang = jnp.stack([row[:, None] * inv_freq, col[:, None] * inv_freq], axis=1)
    return jnp.cos(ang), jnp.sin(ang)

def apply_rope(x, cos, sin):
    B, S, H, D = x.shape
    xs = x.astype(jnp.float32).reshape(B, S, H, 2, D // 2)
    half = D // 4
    x1, x2 = xs[..., :half], xs[..., half:]
    c = cos[None, :, None]
    s = sin[None, :, None]
    out = jnp.concatenate([x1 * c - x2 * s, x2 * c + x1 * s], axis=-1)
    return out.reshape(B, S, H, D).astype(x.dtype)

def short_conv_2(x_in, b_gate, c_gate, w):
    T = x_in.shape[1]
    u = c_gate * x_in
    up = jnp.pad(u, ((0, 0), (CONV_K // 2, CONV_K // 2), (0, 0)))
    y = sum(w[j] * up[:, j:j + T] for j in range(CONV_K))
    return b_gate * y

def softmax_with_sink(scores, sink):
    s = jnp.broadcast_to(sink.astype(jnp.float32).reshape(ATT_KV_HEADS, ATT_GROUP, 1, 1),
                         scores.shape[:-1] + (1,))
    p = jax.nn.softmax(jnp.concatenate([s, scores], axis=-1), axis=-1)
    return p[..., 1:]

def context_attention(q, k, v, sink):
    B, L = q.shape[:2]
    qg = q.reshape(B, L, ATT_KV_HEADS, ATT_GROUP, HEAD_DIM)
    s = jnp.einsum('bqhgd,bkhd->bhgqk', qg, k).astype(jnp.float32) * HEAD_DIM ** -0.5
    p = softmax_with_sink(s, sink).astype(v.dtype)
    o = jnp.einsum('bhgqk,bkhd->bqhgd', p, v)
    return o.reshape(B, L, ATT_HEADS * HEAD_DIM)

def window_attention(q, k, v, k_ctx, v_ctx, sink):
    B, S = q.shape[:2]
    L = k_ctx.shape[1]
    nb = S // BLOCK
    qb = q.reshape(B, nb, BLOCK, ATT_KV_HEADS, ATT_GROUP, HEAD_DIM).transpose(1, 0, 2, 3, 4, 5)
    pad = ((0, 0), (BLOCK, BLOCK), (0, 0), (0, 0))
    kp = jnp.pad(k, pad)
    vp = jnp.pad(v, pad)
    r = jnp.arange(BLOCK)
    j = jnp.arange(3 * BLOCK)
    scale = HEAD_DIM ** -0.5

    def one_block(args):
        qi, i = args
        start = i * BLOCK
        ks = lax.dynamic_slice_in_dim(kp, start, 3 * BLOCK, axis=1)
        vs = lax.dynamic_slice_in_dim(vp, start, 3 * BLOCK, axis=1)
        s_ctx = jnp.einsum('bqhgd,bkhd->bhgqk', qi, k_ctx).astype(jnp.float32)
        s_loc = jnp.einsum('bqhgd,bkhd->bhgqk', qi, ks).astype(jnp.float32)
        tq = start + r
        tk = start - BLOCK + j
        valid = (jnp.abs(tq[:, None] - tk[None, :]) <= WINDOW) & (tk[None, :] >= 0) & (tk[None, :] < S)
        s_loc = jnp.where(valid, s_loc, -jnp.inf)
        p = softmax_with_sink(jnp.concatenate([s_ctx, s_loc], axis=-1) * scale, sink).astype(v.dtype)
        o = (jnp.einsum('bhgqk,bkhd->bqhgd', p[..., :L], v_ctx)
             + jnp.einsum('bhgqk,bkhd->bqhgd', p[..., L:], vs))
        return o.reshape(B, BLOCK, ATT_HEADS * HEAD_DIM)

    out = lax.map(one_block, (qb, jnp.arange(nb)))
    return out.transpose(1, 0, 2, 3).reshape(B, S, ATT_HEADS * HEAD_DIM)

def gla_chunk_scan(q, k, v, log_g, state0, with_output):
    B, T, H, _ = q.shape
    n = T // GLA_CHUNK

    def to_chunks(a):
        return a.reshape(B, n, GLA_CHUNK, H, a.shape[-1]).transpose(1, 0, 3, 2, 4)

    lower_tri = jnp.tril(jnp.ones((GLA_CHUNK, GLA_CHUNK), dtype=bool))[:, :, None]

    def step(state, inp):
        qc, kc, vc, gc = inp
        b = jnp.cumsum(gc.astype(jnp.float32), axis=2)
        b_last = b[:, :, -1:, :]
        new_state = (jnp.exp(b_last[:, :, 0, :])[..., None] * state
                     + jnp.einsum('bhsk,bhsv->bhkv', kc * jnp.exp(b_last - b), vc))
        if not with_output:
            return new_state, None
        diff = jnp.where(lower_tri, b[:, :, :, None, :] - b[:, :, None, :, :], -jnp.inf)
        a = jnp.einsum('bhtk,bhsk,bhtsk->bhts', qc, kc, jnp.exp(diff))
        o = (jnp.einsum('bhts,bhsv->bhtv', a, vc)
             + jnp.einsum('bhtk,bhkv->bhtv', qc * jnp.exp(b), state))
        return new_state, o

    state, o = lax.scan(step, state0, (to_chunks(q), to_chunks(k), to_chunks(v), to_chunks(log_g)))
    if not with_output:
        return None, state
    return o.transpose(1, 0, 3, 2, 4).reshape(B, T, H, v.shape[-1]), state

def gla_output(o, g, norm_g):
    o32 = o.astype(jnp.float32)
    o32 = o32 * lax.rsqrt(jnp.mean(o32 * o32, axis=-1, keepdims=True) + EPS) * norm_g.astype(jnp.float32)
    B, T = o.shape[:2]
    return (o32.reshape(B, T, GLA_HEADS * GLA_DV) * jax.nn.silu(g.astype(jnp.float32))).astype(g.dtype)

def gla_bidir(q, k, v, lr, g, q_c, k_c, v_c, lr_c, g_c, w_gate, b_gate, norm_g, ctx_out):
    B = q.shape[0]
    q = heads(q, GLA_HEADS) * GLA_DK ** -0.5
    k = heads(k, GLA_HEADS)
    v = heads(v, GLA_HEADS)
    q_c = heads(q_c, GLA_HEADS) * GLA_DK ** -0.5
    k_c = heads(k_c, GLA_HEADS)
    v_c = heads(v_c, GLA_HEADS)
    outs_x, outs_c = [], []
    for d in range(2):
        sl = slice(d * GLA_RANK, (d + 1) * GLA_RANK)
        gate_x = heads(jax.nn.log_sigmoid(lr[..., sl] @ w_gate[d] + b_gate[d]) / GLA_NORMALIZER, GLA_HEADS)
        gate_c = heads(jax.nn.log_sigmoid(lr_c[..., sl] @ w_gate[d] + b_gate[d]) / GLA_NORMALIZER, GLA_HEADS)
        flip = (lambda a: jnp.flip(a, axis=1)) if d == 1 else (lambda a: a)
        state0 = jnp.zeros((B, GLA_HEADS, GLA_DK, GLA_DV), jnp.float32)
        o_c, s_c = gla_chunk_scan(flip(q_c), flip(k_c), flip(v_c), flip(gate_c), state0, ctx_out)
        o_x, _ = gla_chunk_scan(flip(q), flip(k), flip(v), flip(gate_x), s_c, True)
        outs_x.append(flip(o_x))
        if ctx_out:
            outs_c.append(flip(o_c))
    y_x = gla_output(outs_x[0] + outs_x[1], g, norm_g)
    y_c = gla_output(outs_c[0] + outs_c[1], g_c, norm_g) if ctx_out else None
    return y_x, y_c

def swiglu_2(h, w_up, w_down):
    a, b = jnp.split(h @ w_up, 2, axis=-1)
    return (jax.nn.silu(a) * b) @ w_down

def layer(x, ctx, mod_x, mod_c, cos, sin, g1, g2, w_in, conv_w, sink, gate_w, gate_b, norm_g,
          w_out, w_up, w_down, ctx_out):
    sh1, sc1, gt1, sh2, sc2, gt2 = jnp.split(mod_x[:, None, :], N_MOD_2, axis=-1)
    csh1, csc1, cgt1, csh2, csc2, cgt2 = jnp.split(mod_c, N_MOD_2, axis=-1)
    hx = rmsnorm(x, g1) * (1 + sc1) + sh1
    hc = rmsnorm(ctx, g1) * (1 + csc1) + csh1
    (xc_in, xc_b, xc_c, xq, xk, xv, xgq, xgk, xgv, xgg, xlr) = jnp.split(hx @ w_in, COL_SPLITS, axis=-1)
    (cc_in, cc_b, cc_c, cq, ck, cv, cgq, cgk, cgv, cgg, clr) = jnp.split(hc @ w_in, COL_SPLITS, axis=-1)
    k_ctx = heads(ck, ATT_KV_HEADS)
    v_ctx = heads(cv, ATT_KV_HEADS)
    conv_x = short_conv_2(xc_in, xc_b, xc_c, conv_w)
    attn_x = window_attention(apply_rope(heads(xq, ATT_HEADS), cos, sin),
                              apply_rope(heads(xk, ATT_KV_HEADS), cos, sin),
                              heads(xv, ATT_KV_HEADS), k_ctx, v_ctx, sink)
    gla_x, gla_c = gla_bidir(xgq, xgk, xgv, xlr, xgg, cgq, cgk, cgv, clr, cgg,
                             gate_w, gate_b, norm_g, ctx_out)
    x = x + gt1 * (jnp.concatenate([conv_x, attn_x, gla_x], axis=-1) @ w_out)
    x = x + gt2 * swiglu_2(rmsnorm(x, g2) * (1 + sc2) + sh2, w_up, w_down)
    if ctx_out:
        conv_c = short_conv_2(cc_in, cc_b, cc_c, conv_w)
        attn_c = context_attention(heads(cq, ATT_HEADS), k_ctx, v_ctx, sink)
        ctx = ctx + cgt1 * (jnp.concatenate([conv_c, attn_c, gla_c], axis=-1) @ w_out)
        ctx = ctx + cgt2 * swiglu_2(rmsnorm(ctx, g2) * (1 + csc2) + csh2, w_up, w_down)
    return x, ctx

def second_inputs(seed: int = 0) -> dict:
    key = jax.random.key(seed)
    ks = jax.random.split(key, 18)

    def nrm(k, shape, s):
        return jax.random.normal(k, shape, jnp.float32) * s

    return {
        "x": nrm(ks[0], (BATCH, SEQ, D_MODEL), 1.0),
        "c": nrm(ks[1], (BATCH, D_MODEL), 1.0),
        "ctx": nrm(ks[2], (BATCH, CTX_LEN, D_MODEL), 1.0),
        "c_ctx": nrm(ks[3], (D_MODEL,), 1.0),
        "w_mod": nrm(ks[4], (DEPTH_2, D_MODEL, N_MOD_2 * D_MODEL), 0.02),
        "b_mod": nrm(ks[5], (DEPTH_2, N_MOD_2 * D_MODEL), 0.01),
        "norm1_g": 1.0 + nrm(ks[6], (DEPTH_2, D_MODEL), 0.02),
        "norm2_g": 1.0 + nrm(ks[7], (DEPTH_2, D_MODEL), 0.02),
        "w_in": nrm(ks[8], (DEPTH_2, D_MODEL, N_IN), D_MODEL ** -0.5),
        "conv_w": nrm(ks[9], (DEPTH_2, CONV_K, CONV_CH), CONV_K ** -0.5),
        "attn_sink": nrm(ks[10], (DEPTH_2, ATT_HEADS), 1.0),
        "gla_gate_w": nrm(ks[11], (DEPTH_2, 2, GLA_RANK, GLA_HEADS * GLA_DK), GLA_RANK ** -0.5),
        "gla_gate_b": nrm(ks[12], (DEPTH_2, 2, GLA_HEADS * GLA_DK), 0.1),
        "gla_norm_g": 1.0 + nrm(ks[13], (DEPTH_2, GLA_DV), 0.02),
        "w_out": nrm(ks[14], (DEPTH_2, D_MIX, D_MODEL), D_MIX ** -0.5),
        "w_up": nrm(ks[15], (DEPTH_2, D_MODEL, 2 * D_FF_2), D_MODEL ** -0.5),
        "w_down": nrm(ks[16], (DEPTH_2, D_FF_2, D_MODEL), D_FF_2 ** -0.5),
        "final_norm_g": 1.0 + nrm(ks[17], (D_MODEL,), 0.02),
    }

def second_block(x, c, ctx, c_ctx, w_mod, b_mod, norm1_g, norm2_g, w_in, conv_w, attn_sink,
              gla_gate_w, gla_gate_b, gla_norm_g, w_out, w_up, w_down, final_norm_g):
    ROWS = x.shape[1] // GRID_W
    cos, sin = axial_rope_tables(ROWS)
    for l in range(DEPTH_2):
        mod_x = jax.nn.silu(c) @ w_mod[l] + b_mod[l]
        mod_c = jax.nn.silu(c_ctx) @ w_mod[l] + b_mod[l]
        x, ctx = layer(x, ctx, mod_x, mod_c, cos, sin, norm1_g[l], norm2_g[l], w_in[l], conv_w[l],
                       attn_sink[l], gla_gate_w[l], gla_gate_b[l], gla_norm_g[l], w_out[l],
                       w_up[l], w_down[l], l < DEPTH_2 - 1)
    return rmsnorm(x, final_norm_g)


def setup_inputs(seed=0):
    out = dict(first_inputs(seed))
    for name, value in second_inputs(seed + 1).items():
        if name != "x":
            out[name + "_2"] = value
    return out


def reference(
    x, c, ctx, c_ctx, mod_w, mod_b, ffn_w_gate, ffn_w_up, ffn_w_down, w_in, hgrn_lb_logits,
    hgrn_norm_w, hyena_conv_w, hyena_conv_b, hyena_w1, hyena_b1, hyena_freq1, hyena_w2,
    hyena_b2, hyena_freq2, hyena_w3, hyena_bias, w_proj_a, w_proj_b, w_out, final_norm_w, c_2,
    ctx_2, c_ctx_2, w_mod_2, b_mod_2, norm1_g_2, norm2_g_2, w_in_2, conv_w_2, attn_sink_2,
    gla_gate_w_2, gla_gate_b_2, gla_norm_g_2, w_out_2, w_up_2, w_down_2, final_norm_g_2,
):
    x = first_block(
        x, c, ctx, c_ctx, mod_w, mod_b, ffn_w_gate, ffn_w_up, ffn_w_down, w_in, hgrn_lb_logits,
        hgrn_norm_w, hyena_conv_w, hyena_conv_b, hyena_w1, hyena_b1, hyena_freq1, hyena_w2,
        hyena_b2, hyena_freq2, hyena_w3, hyena_bias, w_proj_a, w_proj_b, w_out, final_norm_w,
    )
    return second_block(
        x, c_2, ctx_2, c_ctx_2, w_mod_2, b_mod_2, norm1_g_2, norm2_g_2, w_in_2, conv_w_2,
        attn_sink_2, gla_gate_w_2, gla_gate_b_2, gla_norm_g_2, w_out_2, w_up_2, w_down_2,
        final_norm_g_2,
    )


_drawn_inputs = setup_inputs


def setup_inputs(seed=0):
    import zlib

    import numpy as np

    out = dict(_drawn_inputs(seed))
    spreads = {}
    factors = {'ctx': 8.0,
     'c_ctx': 8.0,
     'mod_b': 2.809,
     'hgrn_lb_logits': 8.0,
     'hyena_conv_b': 6.863,
     'hyena_freq1': 5.181,
     'hyena_freq2': 7.065,
     'b_mod_2': 2.707,
     'norm1_g_2': 3.669,
     'norm2_g_2': 18.112,
     'attn_sink_2': 64.0,
     'gla_gate_b_2': 5.022,
     'gla_norm_g_2': 37.866,
     'final_norm_g_2': 21.373}
    for name, (base, spread) in spreads.items():
        noise = np.random.default_rng([zlib.crc32(name.encode()), seed]).standard_normal(out[name].shape)
        drawn = base * np.exp(spread * noise) if base else spread * noise
        out[name] = __import__('jax').numpy.asarray(drawn.astype(out[name].dtype))
    for name, factor in factors.items():
        out[name] = (out[name] * factor).astype(out[name].dtype)
    return out
```

```python
from contextlib import ExitStack
from contextlib import contextmanager

import numpy as np

import concourse.bass as bass
from concourse import mybir

ALU = mybir.AluOpType
ACT = mybir.ActivationFunctionType
AX = mybir.AxisListType
F32 = mybir.dt.float32
F32R = mybir.dt.float32r
U8 = mybir.dt.uint8
I32 = mybir.dt.int32

P = 128
D = 1024
KC = D // P
NX = 512
NCTX = 256
NT = NX + NCTX
CH = P
XCH = NX // CH
ALLCH = NT // CH
F_THIRDS = (8, 8, 6)
DFF = sum(F_THIRDS) * P
EPS = 1e-6
LEVELS = (64, 32, 16, 8, 4, 2, 1)
RING = 4
NFREQ = 8
ATT_HEADS = 8
HD = 64

MOD1_COLS = 9 * D
MOD2_COLS = 6 * D
VEC_FIELDS = (
    ("mod_b", 72), ("b_mod0", 48), ("b_mod1", 48), ("cvec", 16), ("cvec2", 16), ("lbl", 16),
    ("hgrn_w", 1), ("conv_w", 36), ("conv_b", 12), ("hy_bias", 8), ("final_w", 8),
    ("n1g", 16), ("n2g", 16), ("conv2_w", 12), ("gate_b", 8), ("gla_w", 2), ("final2", 8),
    ("sink", 16), ("hyv", 4), ("s4", 2),
)
VEC_AT = {}
_at = 0
for _name, _n in VEC_FIELDS:
    VEC_AT[_name] = (_at, _n)
    _at += _n
NVEC = _at + _at % 2


class Tally:

    def __init__(self):
        self.n = {}
        self.i, self.per = None, {}

    def now(self, name, more=0, share=1):
        base = self.n.get(name, 0) // share + more
        per = self.per.get(name, 0) // share
        return self.i * per + base if self.i is not None and per else base

    def passed(self, name, count=1):
        self.n[name] = self.n.get(name, 0) + count

    def next(self, name, count=1):
        self.passed(name, count)
        return self.now(name)

    @contextmanager
    def turns(self, i, turns, **per):
        before = dict(self.n)
        self.i, self.per = i, per
        yield
        for name in set(self.n) | set(per):
            grew = self.n.get(name, 0) - before.get(name, 0)
            per_turn = per.get(name, 0)
            assert grew == per_turn, (name, grew, per_turn)
            self.n[name] = self.n.get(name, 0) + grew * (turns - 1)
        self.i, self.per = None, {}

    def take(self, kind):
        self.passed(kind)
        return (self.n[kind] - 1) % 2

    def place(self, kind, back=0):
        return (self.n.get(kind, 0) - back) % 2

    def free(self, kind, back=0):
        return self.read(kind, back, 1)

    def read(self, kind, back=1, more=2):
        base = (self.n.get(kind, 0) - back) // 2 + more
        per = self.per.get(kind, 0) // 2
        return self.i * per + base if self.i is not None and per else base


def memory_map():
    at = {}
    top = 0

    def put(name, words):
        nonlocal top
        at[name] = top
        top += (words + 7) // 8 * 8

    for name, words in (
        ("ident", P), ("ones", P), ("blk", P), ("rot", P), ("reset", NT), ("masks", 2 * 8 * P // 4),
        ("amask", 3 * P), ("vecs", NVEC), ("mods", 144), ("cs", 16), ("c4", 32), 
        ("scv", 16), ("hgv", 16), ("lb", 32), ("small", 64), ("mx", 48), ("dec", 8), ("lrs", 512),
        ("raw", RING * D), ("wr_hi", RING * D), ("wr_lo", RING * D),
        ("H", KC * NT), ("xx_hi", KC * NX), ("xx_lo", KC * NX), ("xc_hi", KC * NCTX), ("xc_lo", KC * NCTX),
    ):
        put(name, words)
    at["arena"] = top
    return at


def build(nc, ins, out, stop=None):
    A = memory_map()
    base = (nc.sbuf_base + 31) // 32 * 32
    arena_words = (nc.sbuf_usable_end - base) // 4 - A["arena"]

    with ExitStack() as ctx:
        def at(name, shape, words, dt=F32, parts=P):
            t = nc.alloc_sbuf_tensor_at(name, [parts, *shape], dt, offset=base + 4 * words)
            return t

        def fixed(name, shape, dt=F32, parts=P):
            return at(name, shape, A[name], dt, parts)

        def arena(name, shape, words, dt=F32, parts=P):
            n = int(np.prod(shape)) if dt != U8 else int(np.prod(shape)) // 4
            assert words + n <= arena_words, (name, words, n, arena_words)
            return at(name, shape, A["arena"] + words, dt, parts)

        ident, ones, blk, rot = (fixed(n, [P]) for n in ("ident", "ones", "blk", "rot"))
        reset = fixed("reset", [NT])
        masks = fixed("masks", [2, 8, P], U8)
        amask = fixed("amask", [3 * P])
        vecs = fixed("vecs", [NVEC])
        mods = fixed("mods", [72, 2])
        cs = fixed("cs", [KC, 2])
        c4 = fixed("c4", [KC, 4], F32R)
        scv = fixed("scv", [KC, 2])
        hgv = fixed("hgv", [KC, 2])
        lb = fixed("lb", [4, 8])
        small = fixed("small", [64])
        mx = fixed("mx", [ATT_HEADS, 6])
        dec = fixed("dec", [8])
        lrs = (at("lrs_hi", [KC, 32], A["lrs"], F32R), at("lrs_lo", [KC, 32], A["lrs"] + 256, F32R))
        raw = fixed("raw", [RING, D])
        wr_hi = fixed("wr_hi", [RING, D], F32R)
        wr_lo = fixed("wr_lo", [RING, D], F32R)
        H = fixed("H", [KC, NT])
        xx = (fixed("xx_hi", [KC, NX], F32R), fixed("xx_lo", [KC, NX], F32R))
        xc = (fixed("xc_hi", [KC, NCTX], F32R), fixed("xc_lo", [KC, NCTX], F32R))

        hid = (arena("hid_hi", [8, NT], 0, F32R), arena("hid_lo", [8, NT], 8 * NT, F32R))
        ff_gate = arena("ff_gate", [2, NT], 16 * NT)
        ff_raw = arena("ff_raw", [2, NT], 18 * NT)
        rows = arena("rows", [2, 512], 5248)
        sq = arena("sq", [2, NT], 16 * NT)
        ssq = arena("ssq", [NT], 18 * NT)
        rstd = arena("rstd", [NT], 19 * NT)
        xt = arena("xt", [2, NT], 20 * NT)
        pos = at("pos", [KC, NX], A["xc_hi"])
        fz = arena("fz", [2 * NX], 0, parts=33)
        fw1 = arena("fw1", [64], 1024, parts=33)
        fw2 = arena("fw2", [64], 1088, parts=64)
        fw3 = arena("fw3", [4, 512], 1152, parts=64)
        fh = arena("fh", [2, 2 * NX], 3200, parts=64)
        fk = arena("fk", [2 * NX], 5248, parts=64)
        fwin = arena("fwin", [2, 4, 512], 6272)
        fe = arena("fe", [4, 512], 10368)
        fd = arena("fd", [4, 512], 12416)
        fabs = arena("fabs", [2, 2, 512], 14464)
        fst = arena("fst", [4, 512], 16512)
        dft0 = at("dft0", [4, 1024], A["xx_hi"])
        fa = at("fa", [2, 2, 512], A["xx_lo"])
        fzero = at("fzero", [512], A["xx_lo"] + 2048)
        fnorm = at("fnorm", [512], A["xx_lo"] + 2560)
        oab = (arena("oab_hi", [8, NX], 0, F32R), arena("oab_lo", [8, NX], 4096, F32R))
        dft = at("dft", [4, 1024], A["xc_hi"])
        idft = arena("idft", [8, 512], 8192)
        hp = arena("hp", [3, 514], 12288)
        hu = arena("hu", [4, P], 12288)
        hv = arena("hv", [3, NX], 13832)
        hK = arena("hK", [9, 2, P], 15368)
        hY = arena("hY", [8, P], 17672)

        def unit_space(tag, w, toks, nsub):
            r = {}
            for name, shape in (("lf", [NT]), ("cum", [NT]), ("eq", [NT]), ("ek", [NT]), ("ktok", [NT]),
                                ("S", [6, P])):
                r[name] = arena(f"{tag}_{name}", shape, w)
                w += NT
            for name, n in (("Z", 2), ("ex", 2), ("P", nsub)):
                r[name] = arena(f"{tag}_{name}", [n, toks], w)
                w += n * toks
            return r, w

        u1, end1 = unit_space("u1", 0, NX, 1)
        k1 = arena("k1", [NT], end1)
        assert end1 + NT <= 8192
        vt1 = arena("vt1", [2, NT], 0)
        vtok1 = arena("vtok1", [ALLCH, 512], 8192)
        q1 = arena("q1", [4, NX], 11264)
        oacc1 = arena("oacc1", [4, NX], 13312)
        g1s = arena("g1s", [4, NX], 15360)
        hn = arena("hn", [3, NX], 17408)
        masks32 = arena("masks32", [2, 8, P], 15360, I32)
        yy = (arena("y_hi", [8, NX], 8192, F32R), arena("y_lo", [8, NX], 12288, F32R))
        mg = arena("mg", [4, NX], 16384)
        mo = (arena("mo_hi", [8, NT], 0, F32R), arena("mo_lo", [8, NT], 8 * NT, F32R))
        u2, end2 = unit_space("u2", 0, NT, 2)
        assert end2 <= 9216, end2
        vt2 = arena("vt2", [2, NT], 0)
        gq = arena("gq", [2, NT], 9216)
        gk = arena("gk", [2, NT], 10752)
        vtok2 = arena("vtok2", [ALLCH, 256], 12288)
        oacc2 = arena("oacc2", [2, NT], 13824)
        gg = arena("gg", [2, NT], 15360)
        lr = arena("lr", [NT], 16896, parts=32)
        gatew = arena("gatew", [4, P], 17664, parts=32)
        lrw = arena("lrw", [KC, 32], 18176)
        hn2 = arena("hn2", [3, NT], 0)
        cv = arena("cv", [3, 2, NT], 12288)
        cu = arena("cu", [772], 12288 + 6 * NT)
        cy = arena("cy", [NT], 12288 + 6 * NT + 776)
        aq = arena("aq", [4, NT], 12288)
        akx = arena("akx", [NT], 12288 + 4 * NT)
        avt = arena("avt", [ALLCH, P], 12288 + 5 * NT)
        araw = arena("araw", [2, NT], 2 * NT)
        rope = arena("rope", [2, NX], 4 * NT)
        arot = arena("arot", [NX], 10 * NT)
        sl = at("sl", [2, 640], A["xx_hi"])
        pr = at("pr", [2, 640], A["xx_hi"] + 1280)
        pT = at("pT", [2, 640], A["xx_hi"] + 2560)

        ps = ctx.enter_context(nc.psum_tensor("ps", [P, 4, 1024], F32))

        def gslot(s):
            return ps[:, s, :]

        def mslot(s):
            return ps[:, 2 + s, :]

        kdram = nc.dram_tensor("hyena_k", [18, P, 512], F32, kind="Internal").ap()

        n_tiles = ins["stream"].shape[0] if stop in (None, 9) else max(4, 4 + sum((0, 140, 64, 68, 76, 68, 76, 68, 0)[:stop]))

        def vec(name, i=0, n=1):
            a, _ = VEC_AT[name]
            return vecs[:, a + i:a + i + n]

        def semaphore(name):
            return ctx.enter_context(nc.semaphore(name))

        tile_hi = semaphore("tile_hi")
        tile_lo = semaphore("tile_lo")
        tile_used = semaphore("tile_used")
        misc_done = semaphore("misc_done")
        dve_step = semaphore("dve_step")
        act_step = semaphore("act_step")
        const_landed = semaphore("const_landed")
        masks_landed = semaphore("masks_landed")
        c_hi = semaphore("c_hi")
        c_ready = semaphore("c_ready")
        sq_ready = semaphore("sq_ready")
        ssq_step = semaphore("ssq_step")
        root_ready = semaphore("root_ready")
        xt_ready = semaphore("xt_ready")
        xhi_ready = semaphore("xhi_ready")
        x_ready = semaphore("x_ready")
        hhi_ready = semaphore("hhi_ready")
        hid_ready = semaphore("hid_ready")
        arg_ready = semaphore("arg_ready")
        sin_ready = semaphore("sin_ready")
        abs_ready = semaphore("abs_ready")
        abs_summed = semaphore("abs_summed")
        e_ready = semaphore("e_ready")
        lb_in = semaphore("lb_in")
        lb_exp = semaphore("lb_exp")
        f_ready = semaphore("f_ready")
        lf_ready = semaphore("lf_ready")
        decay_in = semaphore("decay_in")
        decay_ready = semaphore("decay_ready")
        ke_ready = semaphore("ke_ready")
        ex_in = semaphore("ex_in")
        ex_out = semaphore("ex_out")
        z_ready = semaphore("z_ready")
        nsq_ready = semaphore("nsq_ready")
        nroot_ready = semaphore("nroot_ready")
        oraw_ready = semaphore("oraw_ready")
        ohi_ready = semaphore("ohi_ready")
        mix_ready = semaphore("mix_ready")
        dft_landed = semaphore("dft_landed")
        k_landed = semaphore("k_landed")
        hv_ready = semaphore("hv_ready")
        z_done = semaphore("z_done")
        freq_ready = semaphore("freq_ready")
        yraw_ready = semaphore("yraw_ready")
        yhi_ready = semaphore("yhi_ready")
        y_ready = semaphore("y_ready")
        ctx2_landed = semaphore("ctx2_landed")
        arena_free = semaphore("arena_free")
        gate_landed = semaphore("gate_landed")
        lrw_landed = semaphore("lrw_landed")
        lrw_hi = semaphore("lrw_hi")
        lrw_ready = semaphore("lrw_ready")
        lr_ready = semaphore("lr_ready")
        gx_ready = semaphore("gx_ready")
        ge_ready = semaphore("ge_ready")
        conv_ready = semaphore("conv_ready")
        rope_landed = semaphore("rope_landed")
        rope_done = semaphore("rope_done")
        m_ready = semaphore("m_ready")
        exp_ready = semaphore("exp_ready")
        pn_ready = semaphore("pn_ready")
        pt_done = semaphore("pt_done")
        pt_ready = semaphore("pt_ready")
        ao_done = semaphore("ao_done")
        final_ready = semaphore("final_ready")
        out_landed = semaphore("out_landed")
        h_ready = semaphore("h_ready")
        landed = [semaphore(f"landed{s}") for s in range(RING)]
        slot_free = [semaphore(f"slot_free{s}") for s in range(2)]
        misc_free = [semaphore(f"misc_free{s}") for s in range(2)]
        k_stored = [semaphore(f"k_stored{s}") for s in range(4)]


        def tile_slot(tally):
            return tally.n.get("tile_used", 0) % RING

        def pe_tile(pe, tally, groups, order=None):
            s = tile_slot(tally)
            pe.wait_ge(tile_lo, tally.now("tile_used", 1))
            last = None
            for gi, blocks in enumerate(groups):
                slot = tally.take("group")
                pe.wait_ge(slot_free[slot], tally.free("group", 1))
                for bi, (j, spans) in enumerate(blocks):
                    if order is not None and gi == 0:
                        pe.wait_ge(order[0], order[1] + bi + 1)
                    w_hi, w_lo = wr_hi[:, s, j * P:(j + 1) * P], wr_lo[:, s, j * P:(j + 1) * P]
                    for pi, (w, part) in enumerate(((w_hi, 0), (w_hi, 1), (w_lo, 0))):
                        for rhs, col, n in spans:
                            last = pe.matmul(gslot(slot)[:, col:col + n], w, rhs[part],
                                                start=(bi == 0 and pi == 0),
                                                stop=(bi == len(blocks) - 1 and pi == 2))
            last.then_inc(tile_used, 1)
            tally.passed("tile_used")

        def wide_spans(pair, k, with_ctx):
            s = [((pair[0][:, k, 0:NX], pair[1][:, k, 0:NX]), 0, NX)]
            if with_ctx:
                s.append(((pair[0][:, k, NX:NT], pair[1][:, k, NX:NT]), NX, NCTX))
            return s

        def x_spans(k, with_ctx):
            s = [((xx[0][:, k, :], xx[1][:, k, :]), 0, NX)]
            if with_ctx:
                s.append(((xc[0][:, k, :], xc[1][:, k, :]), NX, NCTX))
            return s

        def pe_x_tiles(pe, tally, count, with_ctx):
            for _ in range(count):
                pe_tile(pe, tally, [[(k, x_spans(k, with_ctx)) for k in range(KC)]])

        def split_tile(act, tally):
            ahead = tally.n["tile_used"] - 1 + RING
            if tally.i is None and ahead >= n_tiles:
                return
            s = ahead % RING
            want = 16 * (ahead // RING + 1)
            if tally.i is not None:
                want = tally.i * (16 * tally.per["tile_used"] // RING) + want
            act.wait_ge(tile_used, tally.now("tile_used"))
            act.wait_ge(landed[s], want)
            act.activation(wr_hi[:, s, :], raw[:, s, :], ACT.Copy).then_inc(tile_hi, 1)
            act.wait_ge(tile_hi, tally.next("tile_hi"))

        def act_proj(act, tally, dst, n, func=ACT.Copy, done=None):
            tally.passed("tile_used")
            slot = tally.take("group")
            act.wait_ge(tile_used, tally.now("tile_used"))
            pieces = dst if isinstance(dst, list) else [(dst, 0, n)]
            for pi, (o, a, b) in enumerate(pieces):
                ins = act.activation(o, gslot(slot)[:, a:b], func)
                if pi < len(pieces) - 1:
                    ins.then_inc(act_step, 1)
                    act.wait_ge(act_step, tally.next("act_step"))
                else:
                    ins.then_inc(slot_free[slot], 1)
                    act.wait_ge(slot_free[slot], tally.read("group"))
            split_tile(act, tally)

        def skip_tiles(tally, tiles, groups=None):
            tally.passed("tile_used", tiles)
            tally.passed("group", tiles if groups is None else groups)


        def pe_mod(pe, tally, cols):
            pe.wait_ge(c_ready, tally.next("c_ready"))
            with pe.Fori(0, cols // 1024) as i, tally.turns(i, cols // 1024, tile_used=8, group=2, misc_done=2):
                for par in range(2):
                    slot = tally.take("group")
                    pe.wait_ge(slot_free[slot], tally.free("group", 1))
                    for kk in range(4):
                        s = tile_slot(tally)
                        pe.wait_ge(tile_lo, tally.now("tile_used", 1))
                        for h in range(2):
                            for wi, w in enumerate((wr_hi, wr_lo)):
                                last = pe.matmul(gslot(slot)[0:4, 0:512], c4[:, 2 * kk + h, :],
                                                    w[:, s, h * 512:(h + 1) * 512],
                                                    start=(kk == 0 and h == 0 and wi == 0),
                                                    stop=(kk == 3 and h == 1 and wi == 1))
                        last.then_inc(tile_used, 1)
                        tally.passed("tile_used")
                    pe.wait_ge(slot_free[tally.place("group", 1)], tally.read("group"))
                    place = tally.place("misc_done")
                    pe.wait_ge(misc_free[place], tally.free("misc_done"))
                    m = mslot(place)
                    for j in range(4):
                        last = pe.matmul(m[:, 2 * j:2 * j + 2], rows[0:4, par, j * P:(j + 1) * P],
                                            vecs[0:4, VEC_AT["s4"][0]:VEC_AT["s4"][0] + 2], start=True, stop=True)
                    last.then_inc(misc_done, 1)
                    tally.passed("misc_done")

        def act_mod(act, tally, cols, cname):
            a = VEC_AT[cname][0]
            act.activation(cs[:, :, :], vecs[:, a:a + 16].rearrange("p (k v) -> p k v", v=2), ACT.Silu
                ).then_inc(act_step, 1)
            act.wait_ge(act_step, tally.next("act_step"))
            act.activation(c4[:, :, 0:4:2], cs[:, :, :], ACT.Copy).then_inc(c_hi, 1)
            act.wait_ge(c_hi, tally.next("c_hi"))
            with act.Fori(0, cols // 1024) as i, tally.turns(i, cols // 1024, tile_used=8, group=2, misc_done=2, tile_hi=8):
                for par in range(2):
                    tally.take("group")
                    tally.take("misc_done")
                    for kk in range(4):
                        tally.passed("tile_used")
                        split_tile(act, tally)

        def dve_mod(dve, tally, cols, bname):
            dve.wait_ge(c_hi, tally.next("c_hi"))
            dve.tensor_tensor(c4[:, :, 1:4:2], cs[:, :, :], c4[:, :, 0:4:2], ALU.subtract).then_inc(c_ready, 1)
            dve.wait_ge(c_ready, tally.next("c_ready"))
            b0 = VEC_AT[bname][0]
            with dve.Fori(0, cols // 1024) as i, tally.turns(i, cols // 1024, tile_used=8, group=2, misc_done=2):
                for par in range(2):
                    slot = tally.take("group")
                    tally.passed("tile_used", 4)
                    dve.wait_ge(tile_used, tally.now("tile_used"))
                    dve.tensor_copy(rows[0:4, par, :], gslot(slot)[0:4, 0:512]).then_inc(slot_free[slot], 1)
                    dve.wait_ge(slot_free[slot], tally.read("group"))
                    ms = tally.take("misc_done")
                    dve.wait_ge(misc_done, tally.now("misc_done"))
                    dve.tensor_tensor(
                        mods[:, bass.ds(i * 8 + 4 * par, 4), :], mslot(ms)[:, 0:8].rearrange("p (j v) -> p j v", v=2),
                        vecs[:, bass.ds(i * 8 + (4 * par + b0), 4)].unsqueeze(2).broadcast_to([P, 4, 2]), ALU.add
                            ).then_inc(misc_free[ms], 1)
                    dve.wait_ge(misc_free[ms], tally.read("misc_done"))
            dve.wait_ge(misc_free[tally.place("misc_done", 1)], tally.read("misc_done"))


        def act_norm(act, tally, with_ctx, final=False):
            n = NT if with_ctx else NX
            act.wait_ge(slot_free[tally.place("group", 1)], tally.read("group", 1))
            act.wait_ge(slot_free[tally.place("group", 2)], tally.read("group", 2))
            for m in range(KC):
                if m >= 2:
                    act.wait_ge(ssq_step, tally.next("ssq_step"))
                act.activation(sq[:, m % 2, 0:n], H[:, m, 0:n], ACT.Square).then_inc(sq_ready, 1)
                act.wait_ge(sq_ready, tally.next("sq_ready"))
            act.wait_ge(ssq_step, tally.next("ssq_step", KC - 1 - (KC - 2)))
            tally.take("misc_done")
            act.wait_ge(misc_free[tally.place("misc_done", 1)], tally.read("misc_done"))
            act.activation(rstd[:, 0:n], rstd[:, 0:n], ACT.Sqrt).then_inc(root_ready, 1)
            act.wait_ge(root_ready, tally.next("root_ready"))
            if final:
                return
            for m in range(KC):
                act.wait_ge(xt_ready, tally.next("xt_ready"))
                ins = act.activation(xx[0][:, m, :], xt[:, m % 2, 0:NX], ACT.Copy)
                if with_ctx:
                    ins.then_inc(act_step, 1)
                    act.wait_ge(act_step, tally.next("act_step"))
                    ins = act.activation(xc[0][:, m, :], xt[:, m % 2, NX:NT], ACT.Copy)
                ins.then_inc(xhi_ready, 1)
                act.wait_ge(xhi_ready, tally.next("xhi_ready"))

        def pe_norm(pe, tally, with_ctx):
            pe.wait_ge(ssq_step, tally.next("ssq_step", KC - 1))
            place = tally.place("misc_done")
            pe.wait_ge(misc_free[place], tally.free("misc_done"))
            m = mslot(place)
            last = pe.matmul(m[:, 0:NX], ones[:, :], ssq[:, 0:NX], start=True, stop=True)
            if with_ctx:
                last = pe.matmul(m[:, NX:NT], ones[:, :], ssq[:, NX:NT], start=True, stop=True)
            last.then_inc(misc_done, 1)
            tally.passed("misc_done")

        def dve_norm(dve, tally, with_ctx, shift=0, scale=0, gain=None, final=None):
            n = NT if with_ctx else NX
            if final is None:
                dve.tensor_scalar(scv[:, :, :], mods[:, 8 * scale:8 * scale + 8, :], 1.0, None, ALU.add
                    ).then_inc(dve_step, 1)
                dve.wait_ge(dve_step, tally.next("dve_step"))
                if gain is not None:
                    dve.tensor_tensor(scv[:, :, :], scv[:, :, :],
                                              gain.unsqueeze(2).broadcast_to([P, KC, 2]), ALU.mult
                                                  ).then_inc(dve_step, 1)
                    dve.wait_ge(dve_step, tally.next("dve_step"))
            for m in range(1, KC):
                dve.wait_ge(sq_ready, tally.next("sq_ready", 2 if m == 1 else 1))
                a = sq[:, 0, 0:n] if m == 1 else ssq[:, 0:n]
                dve.tensor_tensor(ssq[:, 0:n], a, sq[:, m % 2, 0:n], ALU.add).then_inc(ssq_step, 1)
                dve.wait_ge(ssq_step, tally.next("ssq_step"))
                dve.wait_ge(ssq_step, tally.now("ssq_step"))
            ms = tally.take("misc_done")
            dve.wait_ge(misc_done, tally.now("misc_done"))
            dve.tensor_scalar(rstd[:, 0:n], mslot(ms)[:, 0:n], 1.0 / D, EPS, ALU.mult, ALU.add
                ).then_inc(misc_free[ms], 1)
            dve.wait_ge(misc_free[ms], tally.read("misc_done"))
            dve.wait_ge(root_ready, tally.next("root_ready"))
            dve.reciprocal(rstd[:, 0:n], rstd[:, 0:n]).then_inc(dve_step, 1)
            dve.wait_ge(dve_step, tally.next("dve_step"))

            def low(m):
                dve.wait_ge(xhi_ready, tally.next("xhi_ready"))
                ins = dve.tensor_tensor(xx[1][:, m, :], xt[:, m % 2, 0:NX], xx[0][:, m, :], ALU.subtract)
                if with_ctx:
                    ins = dve.tensor_tensor(xc[1][:, m, :], xt[:, m % 2, NX:NT], xc[0][:, m, :], ALU.subtract)
                ins.then_inc(x_ready, 1)
                dve.wait_ge(x_ready, tally.next("x_ready"))

            for m in range(KC):
                if final is not None:
                    dve.tensor_tensor(H[:, m, 0:n], H[:, m, 0:n], rstd[:, 0:n], ALU.mult).then_inc(dve_step, 1)
                    dve.wait_ge(dve_step, tally.next("dve_step"))
                    dve.tensor_scalar(H[:, m, 0:n], H[:, m, 0:n], final[:, m:m + 1], None, ALU.mult
                        ).then_inc(final_ready, 1)
                    dve.wait_ge(final_ready, tally.next("final_ready"))
                    continue
                dve.tensor_tensor(xt[:, m % 2, 0:n], H[:, m, 0:n], rstd[:, 0:n], ALU.mult).then_inc(dve_step, 1)
                dve.wait_ge(dve_step, tally.next("dve_step"))
                ins = dve.tensor_scalar(xt[:, m % 2, 0:NX], xt[:, m % 2, 0:NX], scv[:, m, 0:1],
                                          mods[:, 8 * shift + m, 0:1], ALU.mult, ALU.add)
                if with_ctx:
                    ins = dve.tensor_scalar(xt[:, m % 2, NX:NT], xt[:, m % 2, NX:NT], scv[:, m, 1:2],
                                              mods[:, 8 * shift + m, 1:2], ALU.mult, ALU.add)
                ins.then_inc(xt_ready, 1)
                dve.wait_ge(xt_ready, tally.next("xt_ready"))
                if m:
                    low(m - 1)
            if final is None:
                low(KC - 1)


        def pe_ffn(pe, tally, with_ctx):
            pe.wait_ge(x_ready, tally.next("x_ready", KC))
            for F in F_THIRDS:
                with pe.Fori(0, F // 2) as i, tally.turns(i, F // 2, tile_used=4, group=4):
                    pe_x_tiles(pe, tally, 4, with_ctx)
                before = tally.n.get("hid_ready", 0)
                tally.passed("hid_ready", F)
                with pe.Fori(0, 2) as i, tally.turns(i, 2, tile_used=4, group=4):
                    for q in range(4):
                        pe_tile(pe, tally, [[(k, wide_spans(hid, k, with_ctx)) for k in range(F)]],
                                (hid_ready, before) if q == 0 else None)

        def act_ffn(act, tally, with_ctx, last=False):
            n = NT if with_ctx else NX
            for third, F in enumerate(F_THIRDS):
                with act.Fori(0, F // 2) as i, tally.turns(i, F // 2, tile_used=4, group=4, tile_hi=4, hhi_ready=2):
                    for q in range(2):
                        tally.passed("tile_used")
                        slot = tally.take("group")
                        act.wait_ge(slot_free[tally.place("group", 4)], tally.read("group", 4))
                        act.wait_ge(tile_used, tally.now("tile_used"))
                        act.activation(ff_gate[:, q, 0:n], gslot(slot)[:, 0:n], ACT.Silu).then_inc(slot_free[slot], 1)
                        act.wait_ge(slot_free[slot], tally.read("group"))
                        split_tile(act, tally)
                        tally.passed("tile_used")
                        tally.take("group")
                        act.wait_ge(slot_free[tally.place("group", 1)], tally.read("group", 1))
                        act.activation(hid[0][:, bass.ds(i * 2 + q, 1), 0:n], ff_raw[:, q:q + 1, 0:n],
                                                  ACT.Copy).then_inc(hhi_ready, 1)
                        act.wait_ge(hhi_ready, tally.next("hhi_ready"))
                        split_tile(act, tally)
                if last and third == len(F_THIRDS) - 1:
                    for _ in range(8):
                        skip_tiles(tally, 1)
                        split_tile(act, tally)
                else:
                    with act.Fori(0, 2) as i, tally.turns(i, 2, tile_used=4, group=4, tile_hi=4):
                        for _ in range(4):
                            skip_tiles(tally, 1)
                            split_tile(act, tally)

        def dve_ffn(dve, tally, with_ctx, gate, factor):
            n = NT if with_ctx else NX
            dve.tensor_scalar(hgv[:, :, :], mods[:, 8 * gate:8 * gate + 8, :], factor, None, ALU.mult
                ).then_inc(dve_step, 1)
            dve.wait_ge(dve_step, tally.next("dve_step"))
            for F in F_THIRDS:
                with dve.Fori(0, F // 2) as i, tally.turns(i, F // 2, tile_used=4, group=4, hhi_ready=2, hid_ready=2):
                    for q in range(2):
                        skip_tiles(tally, 1)
                        tally.passed("tile_used")
                        slot = tally.take("group")
                        dve.wait_ge(slot_free[tally.place("group", 2)], tally.read("group", 2))
                        dve.wait_ge(tile_used, tally.now("tile_used"))
                        dve.tensor_tensor(ff_raw[:, q, 0:n], gslot(slot)[:, 0:n], ff_gate[:, q, 0:n],
                                                    ALU.mult).then_inc(slot_free[slot], 1)
                        dve.wait_ge(slot_free[slot], tally.read("group"))
                        dve.wait_ge(hhi_ready, tally.next("hhi_ready"))
                        dve.tensor_tensor(hid[1][:, bass.ds(i * 2 + q, 1), 0:n], ff_raw[:, q:q + 1, 0:n],
                                                     hid[0][:, bass.ds(i * 2 + q, 1), 0:n], ALU.subtract
                                                         ).then_inc(hid_ready, 1)
                        dve.wait_ge(hid_ready, tally.next("hid_ready"))
                with dve.Fori(0, 2) as i, tally.turns(i, 2, tile_used=4, group=4):
                    for q in range(4):
                        tally.passed("tile_used")
                        slot = tally.take("group")
                        dve.wait_ge(tile_used, tally.now("tile_used"))
                        dve_residual(dve, tally, slot, i * 4 + q, with_ctx)

        def dve_residual(dve, tally, slot, m, with_ctx):
            for v, (a, b) in enumerate(((0, NX), (NX, NT))[:2 if with_ctx else 1]):
                ins = dve.scalar_tensor_tensor(out=H[:, bass.ds(m, 1), a:b], in0=gslot(slot)[:, a:b].unsqueeze(1),
                                                 scalar=hgv[:, bass.ds(m, 1), v], in1=H[:, bass.ds(m, 1), a:b],
                                                 op0=ALU.mult, op1=ALU.add)
            ins.then_inc(slot_free[slot], 1)
            dve.wait_ge(slot_free[slot], tally.read("group"))


        def halves(ap, b):
            return ap.rearrange("p (n h b) -> p n h b", h=2, b=b)

        def chunks(ap):
            return ap.rearrange("p (c t) -> p c t", t=CH)

        def chunk_order(bw):
            return (5, 4, 3, 2, 1, 0) if bw else (4, 5, 0, 1, 2, 3)

        def pe_unit(pe, tally, U, q, k, vt, nsub, toks):
            nch = toks // CH
            bw = U["bw"]
            order = chunk_order(bw)
            pe.wait_ge(ke_ready, tally.next("ke_ready"))
            place = tally.place("misc_done")
            pe.wait_ge(misc_free[place], tally.free("misc_done"))
            m = mslot(place)
            for c in range(ALLCH):
                last = pe.transpose(m[:, c * P:(c + 1) * P], U["ek"][:, c * CH:(c + 1) * CH], ident[:, :])
            last.then_inc(misc_done, 1)
            tally.passed("misc_done")
            items = [(0, j) for j in range(nsub)]
            for j in range(nsub):
                r = slice(j * HD, (j + 1) * HD) if nsub == 2 else slice(0, P)
                place = tally.place("misc_done")
                pe.wait_ge(misc_free[place], tally.free("misc_done"))
                m = mslot(place)
                for c in range(nch):
                    cc = slice(c * CH, (c + 1) * CH)
                    last = pe.matmul(m[:, cc], k[r, cc], q[r, cc], start=True, stop=True)
                last.then_inc(misc_done, 1)
                tally.passed("misc_done")
            pe.wait_ge(misc_free[tally.place("misc_done", nsub + 1)], tally.read("misc_done", nsub + 1))
            place = tally.place("misc_done")
            pe.wait_ge(misc_free[place], tally.free("misc_done"))
            m = mslot(place)
            for c in order[:5]:
                last = pe.matmul(m[:, c * P:(c + 1) * P], U["ktok"][:, c * P:(c + 1) * P], vt(c),
                                    start=True, stop=True)
            last.then_inc(misc_done, 1)
            tally.passed("misc_done")
            for li in range(len(LEVELS)):
                pe.wait_ge(z_ready, tally.next("z_ready"))
                Z = U["Z"][:, li % 2, :]
                for j in range(nsub):
                    r = slice(j * HD, (j + 1) * HD) if nsub == 2 else slice(0, P)
                    place = tally.place("misc_done")
                    pe.wait_ge(misc_free[place], tally.free("misc_done"))
                    m = mslot(place)
                    for c in range(nch):
                        cc = slice(c * CH, (c + 1) * CH)
                        last = pe.matmul(m[:, cc], Z[r, cc], Z[r, cc], start=True, stop=True)
                    last.then_inc(misc_done, 1)
                    tally.passed("misc_done")
            pe.wait_ge(misc_free[tally.place("misc_done", 1)], tally.read("misc_done"))
            place = tally.place("misc_done")
            pe.wait_ge(misc_free[place], tally.free("misc_done"))
            m = mslot(place)
            for c in range(nch):
                cc = slice(c * CH, (c + 1) * CH)
                at_order = order.index(c)
                for j in range(nsub):
                    f = slice(j * HD, (j + 1) * HD) if nsub == 2 else slice(0, P)
                    last = pe.matmul(m[f, cc], vt(c)[:, f], U["P"][:, j, cc], start=True, stop=False,
                                        skip_group_check=True)
                    if at_order > 0:
                        last = pe.matmul(m[f, cc], U["S"][:, at_order, f], U["eq"][:, cc], start=False, stop=True,
                                            skip_group_check=True)
            last.then_inc(misc_done, 1)
            tally.passed("misc_done")

        def act_unit(act, tally, U, nsub, toks):
            bw = U["bw"]
            end = 0 if bw else CH - 1
            act.wait_ge(decay_in, tally.next("decay_in"))
            act.activation(U["eq"][:, :], U["cum"][:, :], ACT.Exp).then_inc(act_step, 1)
            act.wait_ge(act_step, tally.next("act_step"))
            act.activation(U["ek"][:, :], U["ek"][:, :], ACT.Exp).then_inc(act_step, 1)
            act.wait_ge(act_step, tally.next("act_step"))
            act.activation(dec[:, 0:ALLCH], chunks(U["cum"][:, :])[:, :, end], ACT.Exp).then_inc(decay_ready, 1)
            act.wait_ge(decay_ready, tally.next("decay_ready"))
            ms = tally.take("misc_done")
            act.wait_ge(misc_done, tally.now("misc_done"))
            act.activation(U["ktok"][:, :], mslot(ms)[:, 0:NT], ACT.Copy).then_inc(misc_free[ms], 1)
            act.wait_ge(misc_free[ms], tally.read("misc_done"))
            tally.passed("misc_done", nsub + 1)
            for li in range(len(LEVELS)):
                act.wait_ge(ex_in, tally.next("ex_in"))
                x = U["ex"][:, li % 2, 0:toks]
                act.activation(x, x, ACT.Exp).then_inc(ex_out, 1)
                act.wait_ge(ex_out, tally.next("ex_out"))
                tally.passed("misc_done", nsub)
            tally.passed("misc_done")

        def dve_unit(dve, tally, U, q, k, nsub, toks, oacc):
            bw = U["bw"]
            d = 1 if bw else 0
            nch = toks // CH
            order = chunk_order(bw)
            cum, lf = U["cum"][:, :], U["lf"][:, :]
            if not bw:
                dve.tensor_tensor_scan(cum, reset[:, :], lf, 0.0, ALU.mult, ALU.add).then_inc(dve_step, 1)
                dve.wait_ge(dve_step, tally.next("dve_step"))
                end = CH - 1
            else:
                fwd = U["ek"][:, :]
                dve.tensor_tensor_scan(fwd, reset[:, :], lf, 0.0, ALU.mult, ALU.add).then_inc(dve_step, 1)
                dve.wait_ge(dve_step, tally.next("dve_step"))
                total = chunks(fwd)[:, :, CH - 1:CH].broadcast_to([P, ALLCH, CH])
                dve.tensor_tensor(chunks(cum), total, chunks(fwd), ALU.subtract).then_inc(dve_step, 1)
                dve.wait_ge(dve_step, tally.next("dve_step"))
                dve.tensor_tensor(cum, cum, lf, ALU.add).then_inc(dve_step, 1)
                dve.wait_ge(dve_step, tally.next("dve_step"))
                end = 0
            last = chunks(cum)[:, :, end:end + 1].broadcast_to([P, ALLCH, CH])
            dve.tensor_tensor(chunks(U["ek"][:, :]), last, chunks(cum), ALU.subtract).then_inc(decay_in, 1)
            dve.wait_ge(decay_in, tally.next("decay_in"))
            ce = cum[:, 0:toks]

            def seam(li):
                b = LEVELS[li]
                x = halves(U["ex"][:, li % 2, 0:toks], b)
                c4_ = halves(ce, b)
                n = toks // (2 * b)
                a = c4_[:, :, 1, 0:1] if bw else c4_[:, :, 0, b - 1:b]
                a = a.broadcast_to([P, n, b])
                first, second = c4_[:, :, 0, :], c4_[:, :, 1, :]
                if bw:
                    ins = (x[:, :, 0, :], first, a), (x[:, :, 1, :], a, second)
                else:
                    ins = (x[:, :, 0, :], a, first), (x[:, :, 1, :], second, a)
                dve.tensor_tensor(*ins[0], ALU.subtract).then_inc(dve_step, 1)
                dve.wait_ge(dve_step, tally.next("dve_step"))
                dve.tensor_tensor(*ins[1], ALU.subtract).then_inc(ex_in, 1)
                dve.wait_ge(ex_in, tally.next("ex_in"))

            def make_z(li):
                b = LEVELS[li]
                dve.wait_ge(ex_out, tally.next("ex_out"))
                x, z = halves(U["ex"][:, li % 2, 0:toks], b), halves(U["Z"][:, li % 2, 0:toks], b)
                qh, kh = halves(q[:, 0:toks], b), halves(k[:, 0:toks], b)
                left, right = (qh, kh) if bw else (kh, qh)
                dve.tensor_tensor(z[:, :, 0, :], x[:, :, 0, :], left[:, :, 0, :], ALU.mult).then_inc(dve_step, 1)
                dve.wait_ge(dve_step, tally.next("dve_step"))
                dve.tensor_tensor(z[:, :, 1, :], x[:, :, 1, :], right[:, :, 1, :], ALU.mult).then_inc(z_ready, 1)
                dve.wait_ge(z_ready, tally.next("z_ready"))

            def put(li):
                for j in range(nsub):
                    ms = tally.take("misc_done")
                    dve.wait_ge(misc_done, tally.now("misc_done"))
                    mk = masks[:, d, li, :].unsqueeze(1).broadcast_to([P, nch, CH])
                    dve.copy_predicated(chunks(U["P"][:, j, 0:toks]), mk, chunks(mslot(ms)[:, 0:toks])
                        ).then_inc(misc_free[ms], 1)
                    dve.wait_ge(misc_free[ms], tally.read("misc_done"))

            seam(0)
            dve.wait_ge(decay_ready, tally.next("decay_ready"))
            dve.tensor_tensor(U["eq"][:, 0:toks], U["eq"][:, 0:toks], q[:, 0:toks], ALU.mult).then_inc(dve_step, 1)
            dve.wait_ge(dve_step, tally.next("dve_step"))
            dve.tensor_tensor(U["ek"][:, :], U["ek"][:, :], k[:, :], ALU.mult).then_inc(ke_ready, 1)
            dve.wait_ge(ke_ready, tally.next("ke_ready"))
            tally.take("misc_done")
            for j in range(nsub):
                ms = tally.take("misc_done")
                dve.wait_ge(misc_done, tally.now("misc_done"))
                dve.tensor_tensor(chunks(U["P"][:, j, 0:toks]), chunks(mslot(ms)[:, 0:toks]),
                                            ident[:, :].unsqueeze(1).broadcast_to([P, nch, CH]), ALU.mult
                                                ).then_inc(misc_free[ms], 1)
                dve.wait_ge(misc_free[ms], tally.read("misc_done"))
            make_z(0)
            seam(1)
            ms = tally.take("misc_done")
            dve.wait_ge(misc_done, tally.now("misc_done"))
            add = mslot(ms)
            for n_, c in enumerate(order[:5]):
                src = add[:, c * P:(c + 1) * P]
                if nsub == 2:
                    src = U["Z"][:, 1, c * P:(c + 1) * P]
                    dve.tensor_tensor(src, add[:, c * P:(c + 1) * P], blk[:, :], ALU.mult).then_inc(dve_step, 1)
                    dve.wait_ge(dve_step, tally.next("dve_step"))
                dst = U["S"][:, n_ + 1, :]
                if n_ == 0:
                    ins = dve.tensor_copy(dst, src)
                else:
                    ins = dve.scalar_tensor_tensor(out=dst, in0=U["S"][:, n_, :], scalar=dec[:, c:c + 1], in1=src,
                                                     op0=ALU.mult, op1=ALU.add)
                if n_ < 4:
                    ins.then_inc(dve_step, 1)
                    dve.wait_ge(dve_step, tally.next("dve_step"))
                else:
                    ins.then_inc(misc_free[ms], 1)
                    dve.wait_ge(misc_free[ms], tally.read("misc_done"))
            nl = len(LEVELS)
            for li in range(1, nl):
                make_z(li)
                if li + 1 < nl:
                    seam(li + 1)
                put(li - 1)
            put(nl - 1)
            ms = tally.take("misc_done")
            dve.wait_ge(misc_done, tally.now("misc_done"))
            if not bw:
                ins = dve.tensor_copy(oacc, mslot(ms)[:, 0:toks])
            else:
                ins = dve.tensor_tensor(oacc, mslot(ms)[:, 0:toks], oacc, ALU.add)
            ins.then_inc(misc_free[ms], 1)
            dve.wait_ge(misc_free[ms], tally.read("misc_done"))


        def pe_head_norm(pe, tally, count, n, mat, sqt):
            for h in range(count):
                pe.wait_ge(nsq_ready, tally.next("nsq_ready"))
                place = tally.place("misc_done")
                pe.wait_ge(misc_free[place], tally.free("misc_done"))
                m = mslot(place)
                last = pe.matmul(m[:, 0:NX], mat, sqt[:, 0, 0:NX], start=True, stop=True)
                if n > NX:
                    last = pe.matmul(m[:, NX:n], mat, sqt[:, 0, NX:n], start=True, stop=True)
                last.then_inc(misc_done, 1)
                tally.passed("misc_done")

        def act_head_norm(act, tally, count, n, sqt, oacc, out_pair, first):
            for h in range(count):
                act.wait_ge(misc_free[tally.place("misc_done", 1)], tally.read("misc_done"))
                act.activation(sqt[:, 0, 0:n], oacc[:, h, 0:n], ACT.Square).then_inc(nsq_ready, 1)
                act.wait_ge(nsq_ready, tally.next("nsq_ready"))
                tally.take("misc_done")
                act.wait_ge(misc_free[tally.place("misc_done", 1)], tally.read("misc_done"))
                act.activation(sqt[:, 1, 0:n], sqt[:, 1, 0:n], ACT.Sqrt).then_inc(nroot_ready, 1)
                act.wait_ge(nroot_ready, tally.next("nroot_ready"))
                act.wait_ge(oraw_ready, tally.next("oraw_ready"))
                act.activation(out_pair[0][:, first + h, 0:n], sqt[:, 2, 0:n], ACT.Copy).then_inc(ohi_ready, 1)
                act.wait_ge(ohi_ready, tally.next("ohi_ready"))

        def dve_head_norm(dve, tally, count, n, width, sqt, oacc, gates, w, out_pair, first):
            for h in range(count):
                ms = tally.take("misc_done")
                dve.wait_ge(misc_done, tally.now("misc_done"))
                dve.tensor_scalar(sqt[:, 1, 0:n], mslot(ms)[:, 0:n], 1.0 / width, EPS, ALU.mult, ALU.add
                    ).then_inc(misc_free[ms], 1)
                dve.wait_ge(misc_free[ms], tally.read("misc_done"))
                dve.wait_ge(nroot_ready, tally.next("nroot_ready"))
                dve.reciprocal(sqt[:, 1, 0:n], sqt[:, 1, 0:n]).then_inc(dve_step, 1)
                dve.wait_ge(dve_step, tally.next("dve_step"))
                dve.tensor_tensor(sqt[:, 2, 0:n], oacc[:, h, 0:n], sqt[:, 1, 0:n], ALU.mult).then_inc(dve_step, 1)
                dve.wait_ge(dve_step, tally.next("dve_step"))
                dve.scalar_tensor_tensor(out=sqt[:, 2, 0:n], in0=sqt[:, 2, 0:n], scalar=w,
                                                    in1=gates[:, h, 0:n], op0=ALU.mult, op1=ALU.mult
                                                        ).then_inc(oraw_ready, 1)
                dve.wait_ge(oraw_ready, tally.next("oraw_ready"))
                dve.wait_ge(ohi_ready, tally.next("ohi_ready"))
                dve.tensor_tensor(out_pair[1][:, first + h, 0:n], sqt[:, 2, 0:n],
                                             out_pair[0][:, first + h, 0:n], ALU.subtract).then_inc(mix_ready, 1)
                dve.wait_ge(mix_ready, tally.next("mix_ready"))


        def pe_filters(pe, tally):
            place = tally.place("misc_done")
            pe.wait_ge(misc_free[place], tally.free("misc_done"))
            m = mslot(place)
            for h in range(2):
                last = pe.matmul(m[0:64, h * NX:(h + 1) * NX], fw1[:, :], fz[:, h * NX:(h + 1) * NX],
                                    start=True, stop=True)
            last.then_inc(misc_done, 1)
            tally.passed("misc_done")
            pe.wait_ge(sin_ready, tally.next("sin_ready"))
            place = tally.place("misc_done")
            pe.wait_ge(misc_free[place], tally.free("misc_done"))
            m = mslot(place)
            for h in range(2):
                last = pe.matmul(m[0:64, h * NX:(h + 1) * NX], fw2[:, :], fh[:, 0, h * NX:(h + 1) * NX],
                                    start=True, stop=True)
            last.then_inc(misc_done, 1)
            tally.passed("misc_done")
            pe.wait_ge(sin_ready, tally.next("sin_ready"))
            for o in range(2):
                norm = tally.take("group")
                pe.wait_ge(slot_free[norm], tally.free("group", 1))
                for t in range(5):
                    if t < 4:
                        place = tally.place("misc_done")
                        pe.wait_ge(misc_free[place], tally.free("misc_done"))
                        m = mslot(place)
                        for h in range(2):
                            last = pe.matmul(m[:, h * NX:(h + 1) * NX], fh[:, 1, h * NX + t * P:h * NX + (t + 1) * P],
                                                fw3[:, 2 * o + h, :], start=True, stop=True)
                        last.then_inc(misc_done, 1)
                        tally.passed("misc_done")
                    if t:
                        pe.wait_ge(abs_ready, tally.next("abs_ready"))
                        for h in range(2):
                            last = pe.matmul(gslot(norm)[:, 0:NX], ones[:, :], fabs[:, (t - 1) % 2, h, :],
                                                start=(t == 1 and h == 0), stop=(t == 4 and h == 1))
                        last.then_inc(abs_summed, 1)
                        tally.passed("abs_summed")
                pe.wait_ge(e_ready, tally.next("e_ready", 4))
                for c in range(NFREQ):
                    src = fe if c % 4 < 2 else fd
                    place = tally.place("misc_done")
                    pe.wait_ge(misc_free[place], tally.free("misc_done"))
                    m = mslot(place)
                    for t in range(4):
                        last = pe.matmul(m[:, 0:NX], dft0[:, t, c * P:(c + 1) * P], src[:, t, :],
                                            start=(t == 0), stop=(t == 3))
                    last.then_inc(misc_done, 1)
                    tally.passed("misc_done")

        def act_filters(act, tally):
            for layer in range(2):
                tally.take("misc_done")
                act.wait_ge(arg_ready, tally.next("arg_ready"))
                act.activation(fh[:, layer, :], fh[:, layer, :], ACT.Sin).then_inc(sin_ready, 1)
                act.wait_ge(sin_ready, tally.next("sin_ready"))
            for o in range(2):
                tally.take("group")
                for t in range(4):
                    tally.take("misc_done")
                    if t >= 2 or o:
                        act.wait_ge(abs_summed, tally.next("abs_summed"))
                    act.wait_ge(misc_free[tally.place("misc_done", 1)], tally.read("misc_done"))
                    act.activation(fabs[:, t % 2, :, :], fa[:, t % 2, :, :], ACT.Abs).then_inc(abs_ready, 1)
                    act.wait_ge(abs_ready, tally.next("abs_ready"))
                for c in range(NFREQ):
                    tally.take("misc_done")
                    act.wait_ge(misc_free[tally.place("misc_done", 1)], tally.read("misc_done"))
                    st = fst[:, c % 4, :]
                    n = tally.n.setdefault(f"k_stored{c % 4}", 0)

                    def store(dst, src):
                        act.dma_start(dst, src).then_inc(k_stored[c % 4], 16)
                        tally.n[f"k_stored{c % 4}"] += 16

                    if c == 0:
                        store(kdram[2 * 0 + o, :, :], st)
                        store(kdram[2 * 8 + o, 1:P, :], st[1:P, :])
                    elif c == 4:
                        store(kdram[2 * 4 + o, 1:P, :], st[1:P, :])
                        store(kdram[2 * 4 + o, 0:1, :], fzero[0:1, :])
                        store(kdram[2 * 8 + o, 0:1, :], st[0:1, :])
                    else:
                        store(kdram[2 * c + o, :, :], st)

        def dve_filters(dve, tally):
            dve.memset(fzero[0:1, :], 0.0).then_inc(dve_step, 1)
            dve.wait_ge(dve_step, tally.next("dve_step"))
            hy0 = VEC_AT["hyv"][0]
            for layer in range(2):
                x = fh[:, layer, :]
                ms = tally.take("misc_done")
                dve.wait_ge(misc_done, tally.now("misc_done"))
                ins = dve.tensor_scalar(x, mslot(ms)[0:64, 0:2 * NX], vecs[0:64, hy0 + 2 * layer:hy0 + 2 * layer + 1],
                                          vecs[0:64, hy0 + 2 * layer + 1:hy0 + 2 * layer + 2], ALU.add, ALU.mult)
                ins.then_inc(misc_free[ms], 1)
                dve.wait_ge(misc_free[ms], tally.read("misc_done"))
                dve.wait_ge(misc_free[tally.place("misc_done", 1)], tally.read("misc_done"))
                dve.tensor_scalar(fk[:, :], x, 1.0 / (2 * np.pi), MAGIC, ALU.mult, ALU.add).then_inc(dve_step, 1)
                dve.wait_ge(dve_step, tally.next("dve_step"))
                dve.tensor_scalar(fk[:, :], fk[:, :], MAGIC, None, ALU.subtract).then_inc(dve_step, 1)
                dve.wait_ge(dve_step, tally.next("dve_step"))
                for part in (TWO_PI_HI, 2 * np.pi - TWO_PI_HI):
                    dve.scalar_tensor_tensor(out=x, in0=fk[:, :], scalar=-float(part), in1=x,
                                                     op0=ALU.mult, op1=ALU.add).then_inc(dve_step, 1)
                    dve.wait_ge(dve_step, tally.next("dve_step"))
                dve.tensor_scalar(x, x, PI_F, -PI_F, ALU.min, ALU.max).then_inc(arg_ready, 1)
                dve.wait_ge(arg_ready, tally.next("arg_ready"))
            for o in range(2):
                norm = tally.take("group")
                for t in range(5):
                    if t < 4:
                        ms = tally.take("misc_done")
                        dve.wait_ge(misc_done, tally.now("misc_done"))
                        dve.tensor_tensor(fa[:, t % 2, 0, :], mslot(ms)[:, 0:NX], fwin[:, 0, t, :],
                                                     ALU.mult).then_inc(dve_step, 1)
                        dve.wait_ge(dve_step, tally.next("dve_step"))
                        dve.tensor_tensor(fa[:, t % 2, 1, :], mslot(ms)[:, NX:2 * NX], fwin[:, 1, t, :],
                                                    ALU.mult).then_inc(misc_free[ms], 1)
                        dve.wait_ge(misc_free[ms], tally.read("misc_done"))
                    if t:
                        dve.wait_ge(abs_ready, tally.next("abs_ready"))
                        dve.tensor_tensor(fe[:, t - 1, :], fa[:, (t - 1) % 2, 0, :],
                                                     fa[:, (t - 1) % 2, 1, :], ALU.add).then_inc(dve_step, 1)
                        dve.wait_ge(dve_step, tally.next("dve_step"))
                        dve.tensor_tensor(fd[:, t - 1, :], fa[:, (t - 1) % 2, 0, :],
                                                     fa[:, (t - 1) % 2, 1, :], ALU.subtract).then_inc(e_ready, 1)
                        dve.wait_ge(e_ready, tally.next("e_ready"))
                dve.wait_ge(abs_summed, tally.next("abs_summed", 4))
                dve.tensor_scalar(fnorm[:, :], gslot(norm)[:, 0:NX], 1e-6, None, ALU.add).then_inc(slot_free[norm], 1)
                dve.wait_ge(slot_free[norm], tally.read("group"))
                dve.wait_ge(slot_free[tally.place("group", 1)], tally.read("group", 1))
                dve.reciprocal(fnorm[:, :], fnorm[:, :]).then_inc(dve_step, 1)
                dve.wait_ge(dve_step, tally.next("dve_step"))
                for c in range(NFREQ):
                    ms = tally.take("misc_done")
                    dve.wait_ge(misc_done, tally.now("misc_done"))
                    stored = K_STORES[c % 4]
                    times = o * 2 + (c >= 4)
                    want = 16 * (sum(stored) * (times // 2) + (stored[0] if times % 2 else 0))
                    if want:
                        dve.wait_ge(k_stored[c % 4], want)
                    dve.tensor_tensor(fst[:, c % 4, :], mslot(ms)[:, 0:NX], fnorm[:, :], ALU.mult
                        ).then_inc(misc_free[ms], 1)
                    dve.wait_ge(misc_free[ms], tally.read("misc_done"))


        def pe_values(pe, tally, count, vt, with_ctx=True):
            for h in range(count + 1):
                if h < count:
                    pe_x_tiles(pe, tally, 1, with_ctx)
                if h:
                    pe.wait_ge(slot_free[tally.place("group", 2 if h < count else 1)], tally.read("group", 2 if h < count else 1))
                    place = tally.place("misc_done")
                    pe.wait_ge(misc_free[place], tally.free("misc_done"))
                    m = mslot(place)
                    for c in range(ALLCH):
                        last = pe.transpose(m[:, c * P:(c + 1) * P], vt[:, (h - 1) % 2, c * P:(c + 1) * P],
                                               ident[:, :])
                    last.then_inc(misc_done, 1)
                    tally.passed("misc_done")

        def act_values(act, tally, count, vt):
            m0 = tally.n.get("misc_done", 0)
            for h in range(count):
                if h >= 2:
                    act.wait_ge(misc_free[(m0 + h - 2) % 2], (m0 + h - 2) // 2 + 2)
                act_proj(act, tally, vt[:, h % 2, :], NT)
            tally.passed("misc_done", count)

        def dve_values(dve, tally, count, vtok):
            skip_tiles(tally, count)
            for h in range(count):
                ms = tally.take("misc_done")
                dve.wait_ge(misc_done, tally.now("misc_done"))
                dve.tensor_copy(vtok[:, :, h * P:(h + 1) * P],
                                          mslot(ms)[:, 0:NT].rearrange("p (c f) -> p c f", f=P)
                                              ).then_inc(misc_free[ms], 1)
                dve.wait_ge(misc_free[ms], tally.read("misc_done"))

        def unit1(d):
            U = dict(u1)
            U["bw"] = d == 1
            return U

        def pe_hgrn(pe, tally):
            pe_values(pe, tally, 4, vt1)
            pe_x_tiles(pe, tally, 4, False)
            for d in range(2):
                for h in range(4):
                    pe_x_tiles(pe, tally, 1, True)
                    pe_unit(pe, tally, unit1(d), q1[:, h, :], k1[:, :], lambda c, h=h: vtok1[:, c, h * P:(h + 1) * P],
                            1, NX)
            pe_x_tiles(pe, tally, 4, False)
            pe_head_norm(pe, tally, 4, NX, ones[:, :], hn)

        def act_hgrn(act, tally):
            act.wait_ge(lb_in, tally.next("lb_in"))
            act.dma_start(masks32[:, :, :, :], ins["masks"]).then_inc(masks_landed, 16)
            act_values(act, tally, 4, vt1)
            for h in range(4):
                act_proj(act, tally, q1[:, h, :], NX, ACT.Silu)
            act.activation(lb[:, 0:2, :], lb[:, 0:2, :], ACT.Exp).then_inc(lb_exp, 1)
            act.wait_ge(lb_exp, tally.next("lb_exp"))
            for d in range(2):
                for h in range(4):
                    tally.passed("tile_used")
                    slot = tally.take("group")
                    act.wait_ge(tile_used, tally.now("tile_used"))
                    act.activation(u1["lf"][:, :], gslot(slot)[:, 0:NT], ACT.Exp, scale=-1.0
                        ).then_inc(slot_free[slot], 1)
                    act.wait_ge(slot_free[slot], tally.read("group"))
                    split_tile(act, tally)
                    act.wait_ge(f_ready, tally.next("f_ready"))
                    act.activation(u1["lf"][:, :], u1["lf"][:, :], ACT.Ln).then_inc(lf_ready, 1)
                    act.wait_ge(lf_ready, tally.next("lf_ready"))
                    act_unit(act, tally, unit1(d), 1, NX)
            act.wait_ge(misc_free[tally.place("misc_done", 1)], tally.read("misc_done"))
            act.dma_start(dft[:, :, :], ins["dft"]).then_inc(dft_landed, 16)
            act.dma_start(idft[:, :, :], ins["idft"]).then_inc(dft_landed, 16)
            for h in range(4):
                act_proj(act, tally, g1s[:, h, :], NX, ACT.Silu)
            act_head_norm(act, tally, 4, NX, hn, oacc1, oab, 0)

        def dve_hgrn(dve, tally):
            a = vec("lbl", 0, 8)
            b = vec("lbl", 8, 8)
            dve.tensor_tensor(lb[:, 2, :], a, b, ALU.max).then_inc(dve_step, 1)
            dve.wait_ge(dve_step, tally.next("dve_step"))
            dve.tensor_tensor(lb[:, 0, :], a, lb[:, 2, :], ALU.subtract).then_inc(dve_step, 1)
            dve.wait_ge(dve_step, tally.next("dve_step"))
            dve.tensor_tensor(lb[:, 1, :], b, lb[:, 2, :], ALU.subtract).then_inc(lb_in, 1)
            dve.wait_ge(lb_in, tally.next("lb_in"))
            dve.wait_ge(masks_landed, 16)
            dve.tensor_copy(masks[:, :, :, :], masks32[:, :, :, :]).then_inc(dve_step, 1)
            dve.wait_ge(dve_step, tally.next("dve_step"))
            dve_values(dve, tally, 4, vtok1)
            skip_tiles(tally, 4)
            dve.wait_ge(lb_exp, tally.next("lb_exp"))
            dve.tensor_tensor(lb[:, 1, :], lb[:, 0, :], lb[:, 1, :], ALU.add).then_inc(dve_step, 1)
            dve.wait_ge(dve_step, tally.next("dve_step"))
            dve.reciprocal(lb[:, 1, :], lb[:, 1, :]).then_inc(dve_step, 1)
            dve.wait_ge(dve_step, tally.next("dve_step"))
            dve.tensor_tensor(lb[:, 2, :], lb[:, 0, :], lb[:, 1, :], ALU.mult).then_inc(dve_step, 1)
            dve.wait_ge(dve_step, tally.next("dve_step"))
            dve.tensor_scalar(lb[:, 3, :], lb[:, 2, :], -1.0, 1.0, ALU.mult, ALU.add).then_inc(dve_step, 1)
            dve.wait_ge(dve_step, tally.next("dve_step"))
            for d in range(2):
                for h in range(4):
                    skip_tiles(tally, 1)
                    i = d * 4 + h
                    f = u1["lf"][:, :]
                    dve.wait_ge(slot_free[tally.place("group", 1)], tally.read("group"))
                    dve.tensor_scalar(f, f, 1.0, None, ALU.add).then_inc(dve_step, 1)
                    dve.wait_ge(dve_step, tally.next("dve_step"))
                    dve.reciprocal(f, f).then_inc(dve_step, 1)
                    dve.wait_ge(dve_step, tally.next("dve_step"))
                    dve.tensor_scalar(f, f, lb[:, 3, i:i + 1], lb[:, 2, i:i + 1], ALU.mult, ALU.add
                        ).then_inc(dve_step, 1)
                    dve.wait_ge(dve_step, tally.next("dve_step"))
                    dve.tensor_scalar(k1[:, :], f, -1.0, 1.0, ALU.mult, ALU.add).then_inc(f_ready, 1)
                    dve.wait_ge(f_ready, tally.next("f_ready"))
                    dve.wait_ge(lf_ready, tally.next("lf_ready"))
                    dve_unit(dve, tally, unit1(d), q1[:, h, :], k1[:, :], 1, NX, oacc1[:, h, :])
            skip_tiles(tally, 4)
            dve.wait_ge(slot_free[tally.place("group", 1)], tally.read("group"))
            dve_head_norm(dve, tally, 4, NX, P, hn, oacc1, g1s, vec("hgrn_w"), oab, 0)


        def pe_hyena(pe, tally):
            pe.wait_ge(dft_landed, 32)
            for g in range(4):
                pe_x_tiles(pe, tally, 3, False)
                for o in range(2):
                    pe.wait_ge(hv_ready, tally.next("hv_ready"))
                    place = tally.place("misc_done")
                    pe.wait_ge(misc_free[place], tally.free("misc_done"))
                    m = mslot(place)
                    for t in range(4):
                        last = pe.transpose(m[:, t * P:(t + 1) * P], hv[:, 0, t * P:(t + 1) * P], ident[:, :])
                    last.then_inc(misc_done, 1)
                    tally.passed("misc_done")
                    pe.wait_ge(misc_free[tally.place("misc_done", 1)], tally.read("misc_done"))
                    place = tally.place("misc_done")
                    pe.wait_ge(misc_free[place], tally.free("misc_done"))
                    m = mslot(place)
                    for c in range(NFREQ):
                        for t in range(4):
                            last = pe.matmul(m[:, c * P:(c + 1) * P], dft[:, t, c * P:(c + 1) * P], hu[:, t, :],
                                                start=(t == 0), stop=(t == 3))
                    last.then_inc(misc_done, 1)
                    tally.passed("misc_done")
                    pe.wait_ge(freq_ready, tally.next("freq_ready"))
                    place = tally.place("misc_done")
                    pe.wait_ge(misc_free[place], tally.free("misc_done"))
                    m = mslot(place)
                    for c in range(NFREQ):
                        last = pe.matmul(m[:, 0:NX], hY[:, c, :], idft[:, c, :], start=(c == 0),
                                            stop=(c == NFREQ - 1))
                    last.then_inc(misc_done, 1)
                    tally.passed("misc_done")

        def act_hyena(act, tally):
            for s in range(4):
                act.wait_ge(k_stored[s], 2 * 16 * sum(K_STORES[s]))
            for g in range(4):
                act.dma_start(hK[:, :, :, :].rearrange("p c o f -> p (c o) f"), kdram[:, :, g * P:(g + 1) * P].rearrange(
                    "q p f -> p q f")).then_inc(k_landed, 16)
                for j in range(3):
                    act_proj(act, tally, hp[:, j, 1:513], NX)
                tally.passed("misc_done", 6)
                act.wait_ge(z_done, tally.next("z_done"))
                act.activation(oab[0][:, 4 + g, :], hv[:, 0, :], ACT.Copy).then_inc(ohi_ready, 1)
                act.wait_ge(ohi_ready, tally.next("ohi_ready"))

        def dve_hyena(dve, tally):
            for g in range(4):
                dve.memset(hp[:, :, 0:514:513], 0.0).then_inc(dve_step, 1)
                dve.wait_ge(dve_step, tally.next("dve_step"))
                skip_tiles(tally, 3)
                dve.wait_ge(slot_free[tally.place("group", 1)], tally.read("group"))
                for j in range(3):
                    c = 4 * j + g
                    dve.tensor_scalar(hv[:, j, :], hp[:, j, 0:NX], vec("conv_w", c), vec("conv_b", c),
                                              ALU.mult, ALU.add).then_inc(dve_step, 1)
                    dve.wait_ge(dve_step, tally.next("dve_step"))
                    for tap in (1, 2):
                        ins = dve.scalar_tensor_tensor(out=hv[:, j, :], in0=hp[:, j, tap:tap + NX],
                                                         scalar=vec("conv_w", 12 * tap + c), in1=hv[:, j, :],
                                                         op0=ALU.mult, op1=ALU.add)
                        if tap == 1 or j < 2:
                            ins.then_inc(dve_step, 1)
                            dve.wait_ge(dve_step, tally.next("dve_step"))
                        else:
                            ins.then_inc(hv_ready, 1)
                            dve.wait_ge(hv_ready, tally.next("hv_ready"))
                dve.wait_ge(hv_ready, tally.now("hv_ready"))
                dve.wait_ge(k_landed, 16 * (g + 1))
                for o in range(2):
                    ms = tally.take("misc_done")
                    dve.wait_ge(misc_done, tally.now("misc_done"))
                    dve.tensor_copy(hu[:, :, :], mslot(ms)[:, 0:NX].rearrange("p (t f) -> p t f", f=P)
                        ).then_inc(misc_free[ms], 1)
                    dve.wait_ge(misc_free[ms], tally.read("misc_done"))
                    ms = tally.take("misc_done")
                    dve.wait_ge(misc_done, tally.now("misc_done"))
                    Uf = mslot(ms).rearrange("p (c f) -> p c f", f=P)
                    K = hK[:, :, o, :]
                    dve.tensor_tensor(hY[:, 0:4, :], Uf[:, 0:4, :], K[:, 0:4, :], ALU.mult).then_inc(dve_step, 1)
                    dve.wait_ge(dve_step, tally.next("dve_step"))
                    dve.tensor_tensor(hY[:, 4:8, :], Uf[:, 0:4, :], K[:, 4:8, :], ALU.mult).then_inc(dve_step, 1)
                    dve.wait_ge(dve_step, tally.next("dve_step"))
                    dve.tensor_tensor(K[:, 4:8, :], Uf[:, 4:8, :], K[:, 4:8, :], ALU.mult).then_inc(dve_step, 1)
                    dve.wait_ge(dve_step, tally.next("dve_step"))
                    dve.tensor_tensor(K[:, 1:4, :], Uf[:, 5:8, :], K[:, 1:4, :], ALU.mult).then_inc(dve_step, 1)
                    dve.wait_ge(dve_step, tally.next("dve_step"))
                    dve.tensor_tensor(K[:, 8, :], Uf[:, 4, :], K[:, 8, :], ALU.mult).then_inc(misc_free[ms], 1)
                    dve.wait_ge(misc_free[ms], tally.read("misc_done"))
                    dve.wait_ge(misc_free[tally.place("misc_done", 1)], tally.read("misc_done"))
                    dve.tensor_tensor(hY[:, 0:4, :], hY[:, 0:4, :], K[:, 4:8, :], ALU.subtract).then_inc(dve_step, 1)
                    dve.wait_ge(dve_step, tally.next("dve_step"))
                    dve.tensor_tensor(hY[:, 5:8, :], hY[:, 5:8, :], K[:, 1:4, :], ALU.add).then_inc(dve_step, 1)
                    dve.wait_ge(dve_step, tally.next("dve_step"))
                    dve.tensor_tensor(hY[:, 4, :], hY[:, 4, :], K[:, 8, :], ALU.add).then_inc(freq_ready, 1)
                    dve.wait_ge(freq_ready, tally.next("freq_ready"))
                    ms = tally.take("misc_done")
                    dve.wait_ge(misc_done, tally.now("misc_done"))
                    dve.scalar_tensor_tensor(out=hv[:, 0, :], in0=hv[:, 0, :],
                                                       scalar=vec("hy_bias", 4 * o + g), in1=mslot(ms)[:, 0:NX],
                                                       op0=ALU.mult, op1=ALU.add).then_inc(misc_free[ms], 1)
                    dve.wait_ge(misc_free[ms], tally.read("misc_done"))
                    dve.wait_ge(misc_free[tally.place("misc_done", 1)], tally.read("misc_done"))
                    dve.tensor_tensor(hv[:, 0, :], hv[:, 0, :], hv[:, 1 + o, :], ALU.mult
                        ).then_inc(z_done if o else hv_ready, 1)
                    dve.wait_ge(z_done if o else hv_ready, tally.next("z_done" if o else "hv_ready"))
                    if not o:
                        dve.wait_ge(hv_ready, tally.now("hv_ready"))
                dve.wait_ge(ohi_ready, tally.next("ohi_ready"))
                dve.tensor_tensor(oab[1][:, 4 + g, :], hv[:, 0, :], oab[0][:, 4 + g, :], ALU.subtract
                    ).then_inc(mix_ready, 1)
                dve.wait_ge(mix_ready, tally.next("mix_ready"))


        def pe_merge(pe, tally):
            pe.wait_ge(mix_ready, tally.next("mix_ready", 8))

            def spans(pair, k):
                return [((pair[0][:, k, :], pair[1][:, k, :]), 0, NX)]

            with pe.Fori(0, 2) as i, tally.turns(i, 2, tile_used=12, group=16):
                for m in range(4):
                    pe_x_tiles(pe, tally, 2, False)
                    pe_tile(pe, tally, [[(k, spans(oab, k)) for k in range(4)], [(k, spans(oab, k)) for k in range(4, 8)]])
            before = tally.n.get("y_ready", 0)
            tally.passed("y_ready", KC)
            with pe.Fori(0, 2) as i, tally.turns(i, 2, tile_used=4, group=4):
                for q in range(4):
                    pe_tile(pe, tally, [[(k, spans(yy, k)) for k in range(KC)]], (y_ready, before) if q == 0 else None)

        def act_merge(act, tally):
            with act.Fori(0, 2) as i, tally.turns(i, 2, tile_used=12, group=16, tile_hi=12, yraw_ready=4, yhi_ready=4):
                for m in range(4):
                    for half in range(2):
                        tally.passed("tile_used")
                        slot = tally.take("group")
                        act.wait_ge(slot_free[tally.place("group", 3 + half)], tally.read("group", 3 + half))
                        act.wait_ge(tile_used, tally.now("tile_used"))
                        act.activation(mg[:, 2 * (m % 2) + half, :], gslot(slot)[:, 0:NX], ACT.Sigmoid
                            ).then_inc(slot_free[slot], 1)
                        act.wait_ge(slot_free[slot], tally.read("group"))
                        split_tile(act, tally)
                    skip_tiles(tally, 1, 2)
                    split_tile(act, tally)
                    act.wait_ge(yraw_ready, tally.next("yraw_ready"))
                    act.activation(yy[0][:, bass.ds(i * 4 + m, 1), :], mg[:, 2 * (m % 2):2 * (m % 2) + 1, :],
                                              ACT.Copy).then_inc(yhi_ready, 1)
                    act.wait_ge(yhi_ready, tally.next("yhi_ready"))
            with act.Fori(0, 2) as i, tally.turns(i, 2, tile_used=4, group=4, tile_hi=4):
                for _ in range(4):
                    skip_tiles(tally, 1)
                    split_tile(act, tally)

        def dve_merge(dve, tally):
            dve.tensor_copy(hgv[:, :, :], mods[:, 40:48, :]).then_inc(dve_step, 1)
            dve.wait_ge(dve_step, tally.next("dve_step"))
            with dve.Fori(0, 2) as i, tally.turns(i, 2, tile_used=12, group=16, yraw_ready=4, yhi_ready=4, y_ready=4):
                for m in range(4):
                    a, b = mg[:, 2 * (m % 2), :], mg[:, 2 * (m % 2) + 1, :]
                    skip_tiles(tally, 2)
                    dve.wait_ge(slot_free[tally.place("group", 2)], tally.read("group", 2))
                    dve.wait_ge(slot_free[tally.place("group", 1)], tally.read("group", 1))
                    tally.passed("tile_used")
                    for half, t in enumerate((a, b)):
                        slot = tally.take("group")
                        if not half:
                            dve.wait_ge(tile_used, tally.now("tile_used"))
                        dve.tensor_tensor(t, gslot(slot)[:, 0:NX], t, ALU.mult).then_inc(slot_free[slot], 1)
                        dve.wait_ge(slot_free[slot], tally.read("group"))
                    dve.wait_ge(slot_free[tally.place("group", 1)], tally.read("group"))
                    dve.tensor_tensor(a, a, b, ALU.add).then_inc(yraw_ready, 1)
                    dve.wait_ge(yraw_ready, tally.next("yraw_ready"))
                    dve.wait_ge(yhi_ready, tally.next("yhi_ready"))
                    dve.tensor_tensor(yy[1][:, bass.ds(i * 4 + m, 1), :],
                                                 mg[:, 2 * (m % 2):2 * (m % 2) + 1, :],
                                                 yy[0][:, bass.ds(i * 4 + m, 1), :], ALU.subtract).then_inc(y_ready, 1)
                    dve.wait_ge(y_ready, tally.next("y_ready"))
            with dve.Fori(0, 2) as i, tally.turns(i, 2, tile_used=4, group=4):
                for q in range(4):
                    tally.passed("tile_used")
                    slot = tally.take("group")
                    dve.wait_ge(tile_used, tally.now("tile_used"))
                    dve_residual(dve, tally, slot, i * 4 + q, False)


        def unit2(d):
            U = dict(u2)
            U["bw"] = d == 1
            return U

        def pe_gla(pe, tally, toks):
            with_ctx = toks == NT
            pe.wait_ge(lrw_ready, tally.next("lrw_ready"))
            pe.wait_ge(x_ready, tally.next("x_ready", KC))
            place = tally.place("misc_done")
            pe.wait_ge(misc_free[place], tally.free("misc_done"))
            m = mslot(place)
            for k in range(KC):
                for pi, (w, part) in enumerate(((0, 0), (0, 1), (1, 0))):
                    for rhs, col, n in x_spans(k, True):
                        last = pe.matmul(m[0:32, col:col + n], lrs[w][:, k, :], rhs[part],
                                            start=(k == 0 and pi == 0), stop=(k == KC - 1 and pi == 2))
            last.then_inc(misc_done, 1)
            tally.passed("misc_done")
            pe_values(pe, tally, 2, vt2)
            pe_x_tiles(pe, tally, 4, True)
            pe_x_tiles(pe, tally, 2, with_ctx)
            for d in range(2):
                for t in range(2):
                    if d == t == 0:
                        pe.wait_ge(lr_ready, tally.next("lr_ready"))
                    place = tally.place("misc_done")
                    pe.wait_ge(misc_free[place], tally.free("misc_done"))
                    m = mslot(place)
                    for a, b in ((0, NX), (NX, NT)):
                        last = pe.matmul(m[:, a:b], gatew[:, 2 * d + t, :], lr[:, a:b], start=True, stop=True)
                    last.then_inc(misc_done, 1)
                    tally.passed("misc_done")
                    pe_unit(pe, tally, unit2(d), gq[:, t, :], gk[:, t, :], lambda c, t=t: vtok2[:, c, t * P:(t + 1) * P],
                            2, toks)
            pe_head_norm(pe, tally, 2, toks, blk[:, :], hn2)

        def act_gla(act, tally, layer, toks):
            with_ctx = toks == NT
            act.wait_ge(arena_free, tally.next("arena_free"))
            act.dma_start(gatew[:, :, :], ins["gatew"][layer]).then_inc(gate_landed, 16)
            act.dma_start(lrw[:, :, :], ins["lrw"][layer]).then_inc(lrw_landed, 16)
            act.wait_ge(lrw_landed, 16 * (layer + 1))
            act.activation(lrs[0][:, :, :], lrw[:, :, :], ACT.Copy).then_inc(lrw_hi, 1)
            act.wait_ge(lrw_hi, tally.next("lrw_hi"))
            tally.take("misc_done")
            act_values(act, tally, 2, vt2)
            for t in range(2):
                tally.passed("tile_used")
                slot = tally.take("group")
                act.wait_ge(tile_used, tally.now("tile_used"))
                act.activation(gq[:, t, :], gslot(slot)[:, 0:NT], ACT.Copy, scale=HD ** -0.5
                    ).then_inc(slot_free[slot], 1)
                act.wait_ge(slot_free[slot], tally.read("group"))
                split_tile(act, tally)
            for t in range(2):
                act_proj(act, tally, gk[:, t, :], NT)
            for t in range(2):
                act_proj(act, tally, gg[:, t, 0:toks], toks, ACT.Silu)
            for d in range(2):
                for t in range(2):
                    tally.take("misc_done")
                    act.wait_ge(misc_free[tally.place("misc_done", 1)], tally.read("misc_done"))
                    x = u2["ek"][:, :]
                    act.activation(x, u2["lf"][:, :], ACT.Abs).then_inc(act_step, 1)
                    act.wait_ge(act_step, tally.next("act_step"))
                    act.activation(x, x, ACT.Exp, scale=-1.0).then_inc(act_step, 1)
                    act.wait_ge(act_step, tally.next("act_step"))
                    act.activation(x, x, ACT.Ln, bias=1.0).then_inc(ge_ready, 1)
                    act.wait_ge(ge_ready, tally.next("ge_ready"))
                    act_unit(act, tally, unit2(d), 2, toks)
            act_head_norm(act, tally, 2, toks, hn2, oacc2, mo, 6)

        def dve_gla(dve, tally, layer, toks):
            dve.tensor_copy(small[:, 0:1], vec("final_w")).then_inc(arena_free, 1)
            dve.wait_ge(arena_free, tally.next("arena_free"))
            dve.wait_ge(lrw_hi, tally.next("lrw_hi"))
            dve.tensor_tensor(lrs[1][:, :, :], lrw[:, :, :], lrs[0][:, :, :], ALU.subtract).then_inc(lrw_ready, 1)
            dve.wait_ge(lrw_ready, tally.next("lrw_ready"))
            ms = tally.take("misc_done")
            dve.wait_ge(misc_done, tally.now("misc_done"))
            dve.tensor_copy(lr[:, :], mslot(ms)[0:32, 0:NT]).then_inc(misc_free[ms], 1)
            dve.wait_ge(misc_free[ms], tally.read("misc_done"))
            dve.wait_ge(gate_landed, 16 * (layer + 1))
            dve.tensor_copy(small[:, 0:1], vec("final_w")).then_inc(lr_ready, 1)
            dve.wait_ge(lr_ready, tally.next("lr_ready"))
            dve_values(dve, tally, 2, vtok2)
            skip_tiles(tally, 6)
            for back in (1, 2):
                dve.wait_ge(slot_free[tally.place("group", back)], tally.read("group", back))
            for d in range(2):
                for t in range(2):
                    ms = tally.take("misc_done")
                    dve.wait_ge(misc_done, tally.now("misc_done"))
                    f, x = u2["lf"][:, :], u2["ek"][:, :]
                    dve.tensor_scalar(f, mslot(ms)[:, 0:NT], vec("gate_b", 4 * layer + 2 * d + t), None,
                                                ALU.add).then_inc(misc_free[ms], 1)
                    dve.wait_ge(misc_free[ms], tally.read("misc_done"))
                    dve.wait_ge(ge_ready, tally.next("ge_ready"))
                    dve.scalar_tensor_tensor(out=f, in0=f, scalar=0.0, in1=x, op0=ALU.min, op1=ALU.subtract
                        ).then_inc(dve_step, 1)
                    dve.wait_ge(dve_step, tally.next("dve_step"))
                    dve.tensor_scalar(f, f, 1.0 / 16.0, None, ALU.mult).then_inc(dve_step, 1)
                    dve.wait_ge(dve_step, tally.next("dve_step"))
                    dve_unit(dve, tally, unit2(d), gq[:, t, :], gk[:, t, :], 2, toks, oacc2[:, t, 0:toks])
            dve_head_norm(dve, tally, 2, toks, HD, hn2, oacc2, gg, vec("gla_w", layer), mo, 6)


        def act_conv2(act, tally, toks):
            for j in range(3):
                for t in range(2):
                    act_proj(act, tally, cv[:, j, t, 0:toks], toks)
            for t in range(2):
                act.wait_ge(conv_ready, tally.next("conv_ready"))
                act.activation(mo[0][:, t, 0:toks], cy[:, 0:toks], ACT.Copy).then_inc(ohi_ready, 1)
                act.wait_ge(ohi_ready, tally.next("ohi_ready"))

        def dve_conv2(dve, tally, layer, toks):
            parts = ((0, NX, 1), (NX, NT, 3))[:2 if toks == NT else 1]
            dve.memset(cu[:, :], 0.0).then_inc(dve_step, 1)
            dve.wait_ge(dve_step, tally.next("dve_step"))
            skip_tiles(tally, 6)
            for back in (1, 2):
                dve.wait_ge(slot_free[tally.place("group", back)], tally.read("group", back))
            for t in range(2):
                for a, b, sh in parts:
                    ins = dve.tensor_tensor(cu[:, a + sh:b + sh], cv[:, 0, t, a:b], cv[:, 1, t, a:b], ALU.mult)
                    ins.then_inc(dve_step, 1)
                    dve.wait_ge(dve_step, tally.next("dve_step"))
                for a, b, sh in parts:
                    w = 6 * layer
                    dve.tensor_scalar(cy[:, a:b], cu[:, a + sh - 1:b + sh - 1], vec("conv2_w", w + t), None,
                                              ALU.mult).then_inc(dve_step, 1)
                    dve.wait_ge(dve_step, tally.next("dve_step"))
                    for tap in (1, 2):
                        dve.scalar_tensor_tensor(out=cy[:, a:b], in0=cu[:, a + sh - 1 + tap:b + sh - 1 + tap],
                                                         scalar=vec("conv2_w", w + 2 * tap + t), in1=cy[:, a:b],
                                                         op0=ALU.mult, op1=ALU.add).then_inc(dve_step, 1)
                        dve.wait_ge(dve_step, tally.next("dve_step"))
                dve.tensor_tensor(cy[:, 0:toks], cy[:, 0:toks], cv[:, 2, t, 0:toks], ALU.mult).then_inc(conv_ready, 1)
                dve.wait_ge(conv_ready, tally.next("conv_ready"))
                dve.wait_ge(conv_ready, tally.now("conv_ready"))
                dve.wait_ge(ohi_ready, tally.next("ohi_ready"))
                dve.tensor_tensor(mo[1][:, t, 0:toks], cy[:, 0:toks], mo[0][:, t, 0:toks], ALU.subtract
                    ).then_inc(mix_ready, 1)
                dve.wait_ge(mix_ready, tally.next("mix_ready"))


        def att_items(toks):
            return [(c, s, qb) for c in range(4) for s in range(2) for qb in range(toks // P)]

        def local_keys(qb):
            return [] if qb >= XCH else [b for b in (qb - 1, qb, qb + 1) if 0 <= b < XCH]

        def pe_rope(pe, tally, src_slot, back):
            pe.wait_ge(slot_free[tally.place("group", back)], tally.read("group", back))
            place = tally.place("misc_done")
            pe.wait_ge(misc_free[place], tally.free("misc_done"))
            m = mslot(place)
            pe.matmul(m[:, 0:NX], rot[:, :], araw[:, src_slot, 0:NX], start=True, stop=True).then_inc(misc_done, 1)
            tally.passed("misc_done")

        def pe_attention(pe, tally, toks):
            with_ctx = toks == NT
            pe_x_tiles(pe, tally, 6, with_ctx)
            pe_x_tiles(pe, tally, 1, True)
            pe_rope(pe, tally, 0, 1)
            pe_x_tiles(pe, tally, 1, True)
            pe.wait_ge(slot_free[tally.place("group", 1)], tally.read("group"))
            place = tally.place("misc_done")
            pe.wait_ge(misc_free[place], tally.free("misc_done"))
            m = mslot(place)
            for c in range(ALLCH):
                last = pe.transpose(m[:, c * P:(c + 1) * P], araw[:, 1, c * P:(c + 1) * P], ident[:, :])
            last.then_inc(misc_done, 1)
            tally.passed("misc_done")
            for c in range(4):
                pe_x_tiles(pe, tally, 1, with_ctx)
                pe_rope(pe, tally, c % 2, 1)
            pe.wait_ge(slot_free[tally.place("group", 1)], tally.read("group", 1))
            pe.wait_ge(slot_free[tally.place("group", 2)], tally.read("group", 2))
            pe.wait_ge(rope_done, tally.next("rope_done", 5))
            items = att_items(toks)

            def scores(i):
                c, s, qb = items[i]
                place = tally.place("misc_done")
                pe.wait_ge(misc_free[place], tally.free("misc_done"))
                m = mslot(place)
                r = slice(s * HD, (s + 1) * HD)
                qq = aq[r, c, qb * P:(qb + 1) * P]
                last = pe.matmul(m[:, 0:NCTX], qq, akx[r, NX:NT], start=True, stop=True)
                lk = local_keys(qb)
                if lk:
                    last = pe.matmul(m[:, 512:512 + len(lk) * P], qq, akx[r, lk[0] * P:(lk[-1] + 1) * P],
                                        start=True, stop=True)
                last.then_inc(misc_done, 1)
                tally.passed("misc_done")

            def turn(i):
                n = 2 + len(local_keys(items[i][2]))
                pe.wait_ge(pn_ready, tally.next("pn_ready"))
                if i >= 1:
                    pe.wait_ge(pt_ready, tally.next("pt_ready"))
                for b in range(n):
                    last = pe.transpose(gslot(1)[:, b * P:(b + 1) * P], pr[:, i % 2, b * P:(b + 1) * P],
                                           ident[:, :])
                last.then_inc(pt_done, 1)
                tally.passed("pt_done")

            def values(i):
                c, s, qb = items[i]
                if i == len(items) - 1:
                    pe.wait_ge(pt_ready, tally.next("pt_ready"))
                if (s, qb) == (0, 0) and c:
                    pe.wait_ge(mix_ready, tally.next("mix_ready"))
                keys = [4, 5] + local_keys(qb)
                f = slice(s * HD, (s + 1) * HD)
                for n, kc in enumerate(keys):
                    last = pe.matmul(gslot(0)[f, qb * P:(qb + 1) * P], avt[:, kc, f],
                                        pT[:, i % 2, n * P:(n + 1) * P], start=(n == 0), stop=(n == len(keys) - 1),
                                        skip_group_check=True)
                if i == len(items) - 1 or items[i + 1][0] != c:
                    last.then_inc(ao_done, 1)
                    tally.passed("ao_done")

            pe.wait_ge(mix_ready, tally.next("mix_ready", 4))
            scores(0)
            for i in range(len(items)):
                if i + 1 < len(items):
                    scores(i + 1)
                turn(i)
                if i:
                    values(i - 1)
            values(len(items) - 1)
            pe.wait_ge(mix_ready, tally.next("mix_ready"))

        def act_attention(act, tally, layer, toks):
            act.dma_start(rope[:, :, :], ins["rope"]).then_inc(rope_landed, 16)
            act_proj(act, tally, araw[:, 0, :], NT)
            tally.take("misc_done")
            act_proj(act, tally, araw[:, 1, :], NT)
            tally.take("misc_done")
            for c in range(4):
                if c == 0:
                    act.wait_ge(rope_done, tally.next("rope_done"))
                elif c == 1:
                    act.wait_ge(misc_free[tally.place("misc_done", 2)], tally.read("misc_done", 2))
                else:
                    act.wait_ge(rope_done, tally.next("rope_done"))
                act_proj(act, tally, araw[:, c % 2, 0:toks], toks)
                tally.take("misc_done")
            items = att_items(toks)
            act.wait_ge(rope_done, tally.next("rope_done", 2))

            def expo(i):
                c, s, qb = items[i]
                h = c + 4 * s
                w = 6 + 8 * (i % 2)
                act.wait_ge(m_ready, tally.next("m_ready"))
                lk = len(local_keys(qb))
                neg = small[:, w + 1:w + 2]
                sums = small[:, w + 2:w + 5]
                ms = tally.take("misc_done")
                act.activation(pr[:, i % 2, 0:NCTX], mslot(ms)[:, 0:NCTX], ACT.Exp, bias=neg, scale=ATT_SCALE,
                                         accum_out=sums[:, 1:2]).then_inc(misc_free[ms], 1)
                act.wait_ge(misc_free[ms], tally.read("misc_done"))
                if lk:
                    act.activation(pr[:, i % 2, NCTX:NCTX + lk * P], sl[:, i % 2, 0:lk * P], ACT.Exp,
                                              bias=neg, scale=ATT_SCALE, accum_out=sums[:, 0:1]).then_inc(act_step, 1)
                    act.wait_ge(act_step, tally.next("act_step"))
                act.activation(sums[:, 2:3], mx[:, h, 2:3], ACT.Exp, bias=neg, scale=ATT_SCALE).then_inc(exp_ready, 1)
                act.wait_ge(exp_ready, tally.next("exp_ready"))

            def copy(i):
                n = 2 + len(local_keys(items[i][2]))
                act.wait_ge(pt_done, tally.next("pt_done"))
                act.activation(pT[:, i % 2, 0:n * P], gslot(1)[:, 0:n * P], ACT.Copy).then_inc(pt_ready, 1)
                act.wait_ge(pt_ready, tally.next("pt_ready"))

            def leave(c):
                act.wait_ge(ao_done, tally.next("ao_done"))
                act.activation(mo[0][:, 2 + c, 0:toks], gslot(0)[:, 0:toks], ACT.Copy).then_inc(ohi_ready, 1)
                act.wait_ge(ohi_ready, tally.next("ohi_ready"))

            per = len(items) // 4
            for i in range(len(items)):
                expo(i)
                if i:
                    copy(i - 1)
                if i > 1 and (i - 1) % per == 0:
                    leave((i - 1) // per - 1)
            copy(len(items) - 1)
            leave(3)

        def dve_attention(dve, tally, layer, toks):
            skip_tiles(tally, 1)
            dve.wait_ge(rope_landed, 16 * (layer + 1))

            def rotate(dst, src, n):
                dve.wait_ge(slot_free[tally.place("group", 1)], tally.read("group"))
                ms = tally.take("misc_done")
                dve.wait_ge(misc_done, tally.now("misc_done"))
                dve.tensor_tensor(arot[:, 0:NX], mslot(ms)[:, 0:NX], rope[:, 1, :], ALU.mult
                    ).then_inc(misc_free[ms], 1)
                dve.wait_ge(misc_free[ms], tally.read("misc_done"))
                dve.tensor_tensor(dst[:, 0:NX], src[:, 0:NX], rope[:, 0, :], ALU.mult).then_inc(dve_step, 1)
                dve.wait_ge(dve_step, tally.next("dve_step"))
                ins = dve.tensor_tensor(dst[:, 0:NX], dst[:, 0:NX], arot[:, 0:NX], ALU.add)
                if n > NX:
                    ins.then_inc(dve_step, 1)
                    dve.wait_ge(dve_step, tally.next("dve_step"))
                    ins = dve.tensor_copy(dst[:, NX:n], src[:, NX:n])
                ins.then_inc(rope_done, 1)
                dve.wait_ge(rope_done, tally.next("rope_done"))

            rotate(akx[:, :], araw[:, 0, :], NT)
            skip_tiles(tally, 1)
            ms = tally.take("misc_done")
            dve.wait_ge(misc_done, tally.now("misc_done"))
            dve.tensor_copy(avt[:, :, :], mslot(ms)[:, 0:NT].rearrange("p (c f) -> p c f", f=P)
                ).then_inc(misc_free[ms], 1)
            dve.wait_ge(misc_free[ms], tally.read("misc_done"))
            for c in range(4):
                skip_tiles(tally, 1)
                rotate(aq[:, c, :], araw[:, c % 2, :], toks)
            dve.tensor_scalar(mx[:, :, 2], vec("sink", 8 * layer, 8), 1.0 / ATT_SCALE, None, ALU.mult
                ).then_inc(dve_step, 1)
            dve.wait_ge(dve_step, tally.next("dve_step"))
            items = att_items(toks)
            per = len(items) // 4

            def top(i):
                c, s, qb = items[i]
                h = c + 4 * s
                w = 6 + 8 * (i % 2)
                ms = tally.take("misc_done")
                dve.wait_ge(misc_done, tally.now("misc_done"))
                lk = local_keys(qb)
                if lk:
                    a0 = P if qb == 0 else 0
                    dve.tensor_tensor(sl[:, i % 2, 0:len(lk) * P], mslot(ms)[:, 512:512 + len(lk) * P],
                                                 amask[:, a0:a0 + len(lk) * P], ALU.add).then_inc(dve_step, 1)
                    dve.wait_ge(dve_step, tally.next("dve_step"))
                    dve.wait_ge(dve_step, tally.now("dve_step"))
                    dve.tensor_reduce(mx[:, h, 0:1], sl[:, i % 2, 0:len(lk) * P], AX.X, ALU.max).then_inc(dve_step, 1)
                    dve.wait_ge(dve_step, tally.next("dve_step"))
                dve.tensor_reduce(mx[:, h, 1:2], mslot(ms)[:, 0:NCTX], AX.X, ALU.max).then_inc(dve_step, 1)
                dve.wait_ge(dve_step, tally.next("dve_step"))
                dve.tensor_reduce(small[:, w:w + 1], mx[:, h, (0 if lk else 1):3], AX.X, ALU.max).then_inc(dve_step, 1)
                dve.wait_ge(dve_step, tally.next("dve_step"))
                dve.tensor_scalar(small[:, w + 1:w + 2], small[:, w:w + 1], -ATT_SCALE, None, ALU.mult
                    ).then_inc(m_ready, 1)
                dve.wait_ge(m_ready, tally.next("m_ready"))

            def norm(i):
                lk = len(local_keys(items[i][2]))
                w = 6 + 8 * (i % 2)
                dve.wait_ge(exp_ready, tally.next("exp_ready"))
                dve.tensor_reduce(small[:, w + 5:w + 6], small[:, w + (2 if lk else 3):w + 5], AX.X, ALU.add
                    ).then_inc(dve_step, 1)
                dve.wait_ge(dve_step, tally.next("dve_step"))
                dve.reciprocal(small[:, w + 5:w + 6], small[:, w + 5:w + 6]).then_inc(dve_step, 1)
                dve.wait_ge(dve_step, tally.next("dve_step"))
                n = NCTX + lk * P
                dve.tensor_scalar(pr[:, i % 2, 0:n], pr[:, i % 2, 0:n], small[:, w + 5:w + 6], None,
                                             ALU.mult).then_inc(pn_ready, 1)
                dve.wait_ge(pn_ready, tally.next("pn_ready"))

            def leave(c):
                dve.wait_ge(ohi_ready, tally.next("ohi_ready"))
                dve.tensor_tensor(mo[1][:, 2 + c, 0:toks], gslot(0)[:, 0:toks], mo[0][:, 2 + c, 0:toks],
                                             ALU.subtract).then_inc(mix_ready, 1)
                dve.wait_ge(mix_ready, tally.next("mix_ready"))

            top(0)
            for i in range(len(items)):
                if i + 1 < len(items):
                    top(i + 1)
                norm(i)
                if i > 1 and (i - 1) % per == 0:
                    leave((i - 1) // per - 1)
            leave(3)

        def pe_out2(pe, tally, with_ctx):
            with pe.Fori(0, 2) as i, tally.turns(i, 2, tile_used=4, group=4):
                for _ in range(4):
                    pe_tile(pe, tally, [[(k, wide_spans(mo, k, with_ctx)) for k in range(KC)]])

        def act_out2(act, tally):
            with act.Fori(0, 2) as i, tally.turns(i, 2, tile_used=4, group=4, tile_hi=4):
                for _ in range(4):
                    skip_tiles(tally, 1)
                    split_tile(act, tally)

        def dve_out2(dve, tally, with_ctx):
            dve.tensor_copy(hgv[:, :, :], mods[:, 16:24, :]).then_inc(dve_step, 1)
            dve.wait_ge(dve_step, tally.next("dve_step"))
            with dve.Fori(0, 2) as i, tally.turns(i, 2, tile_used=4, group=4):
                for q in range(4):
                    tally.passed("tile_used")
                    slot = tally.take("group")
                    dve.wait_ge(tile_used, tally.now("tile_used"))
                    dve_residual(dve, tally, slot, i * 4 + q, with_ctx)


        stages = STAGES if stop is None else STAGES[:stop]
        last_stage = stages[-1]
        block = ctx.enter_context(nc.Block())
        consts = [(ident[:, :], ins["ident"]), (ones[:, :], ins["ones"]), (blk[:, :], ins["blk"]),
                  (rot[:, :], ins["rot"]), (reset[:, :], ins["reset"]),
                  (amask[:, :], ins["amask"]), (vecs[:, :], ins["vecs"]), (H[:, :, :], ins["h"]),
                  (pos[:, :, :], ins["pos"]), (fz[:, :], ins["fz"]), (fw1[:, :], ins["fw1"]), (fw2[:, :], ins["fw2"]),
                  (fw3[:, :, :], ins["fw3"]), (fwin[:, :, :, :], ins["fwin"]), (dft0[:, :, :], ins["dft"])]

        @block.sync
        def _(sp):
            for dst, src in consts:
                sp.dma_start(dst, src).then_inc(const_landed, 16)
            for s in range(RING):
                sp.dma_start(raw[:, s, :], ins["stream"][s]).then_inc(landed[s], 16)
            n = n_tiles // RING
            with sp.Fori(1, max(n, 2)) as i:
                for s in range(RING if n > 1 else 0):
                    sp.wait_ge(tile_lo, i * RING + (s + 1 - RING))
                    sp.dma_start(raw[:, s, :], ins["stream"][bass.ds(i * RING + s, 1)].rearrange("a p n -> (a p) n")
                                 ).then_inc(landed[s], 16)
            sp.wait_ge(h_ready, 1)
            for m in range(KC):
                sp.dma_start(out[m], H[:, m, 0:NX]).then_inc(out_landed, 16)
            sp.wait_ge(out_landed, 16 * KC)
            for s in range(4):
                sp.wait_ge(k_stored[s], 2 * 16 * sum(K_STORES[s]))
            if stop == 4:
                sp.wait_ge(ctx2_landed, 16)

        @block.gpsimd
        def _(pool):
            with pool.Fori(0, n_tiles // RING) as i:
                for s in range(RING):
                    pool.wait_ge(tile_hi, i * RING + s + 1)
                    nc.gpsimd.tensor_tensor(wr_lo[:, s, :], raw[:, s, :], wr_hi[:, s, :],
                                            ALU.subtract).then_inc(tile_lo, 1)

        @block.tensor
        def _(pe):
            tally = Tally()
            pe.wait_ge(const_landed, 16 * len(consts))
            for stage in stages:
                if stage == "filters":
                    pe_filters(pe, tally)
                elif stage == "block1_ffn1":
                    pe_mod(pe, tally, MOD1_COLS)
                    pe_norm(pe, tally, True)
                    pe_ffn(pe, tally, True)
                elif stage == "block1_mix":
                    pe_norm(pe, tally, True)
                    pe.wait_ge(x_ready, tally.next("x_ready", KC))
                    pe_hgrn(pe, tally)
                    pe_hyena(pe, tally)
                    pe_merge(pe, tally)
                elif stage == "block1_ffn2":
                    pe_norm(pe, tally, False)
                    pe_ffn(pe, tally, False)
                    pe_norm(pe, tally, False)
                elif stage[:-1] == "block2_mix":
                    toks = NT if stage[-1] == "0" else NX
                    pe_mod(pe, tally, MOD2_COLS)
                    pe_norm(pe, tally, True)
                    pe_gla(pe, tally, toks)
                    pe_attention(pe, tally, toks)
                    pe_out2(pe, tally, toks == NT)
                elif stage[:-1] == "block2_ffn":
                    with_ctx = stage[-1] == "0"
                    pe_norm(pe, tally, with_ctx)
                    pe_ffn(pe, tally, with_ctx)
                elif stage == "final":
                    pe_norm(pe, tally, False)

        @block.scalar
        def _(act):
            tally = Tally()
            act.wait_ge(const_landed, 16 * len(consts))
            for s in range(RING):
                act.wait_ge(landed[s], 16)
                act.activation(wr_hi[:, s, :], raw[:, s, :], ACT.Copy).then_inc(tile_hi, 1)
                act.wait_ge(tile_hi, tally.next("tile_hi"))
            for stage in stages:
                if stage == "filters":
                    act_filters(act, tally)
                elif stage == "block1_ffn1":
                    act_mod(act, tally, MOD1_COLS, "cvec")
                    act_norm(act, tally, True)
                    act_ffn(act, tally, True)
                elif stage == "block1_mix":
                    act_norm(act, tally, True)
                    act_hgrn(act, tally)
                    act_hyena(act, tally)
                    act_merge(act, tally)
                elif stage == "block1_ffn2":
                    act_norm(act, tally, False)
                    act_ffn(act, tally, False)
                    act.dma_start(H[:, :, NX:NT], ins["ctx2"]).then_inc(ctx2_landed, 16)
                    act_norm(act, tally, False, final=True)
                elif stage[:-1] == "block2_mix":
                    toks = NT if stage[-1] == "0" else NX
                    layer = int(stage[-1])
                    act_mod(act, tally, MOD2_COLS, "cvec2")
                    if layer == 0:
                        act.wait_ge(ctx2_landed, 16)
                        act.wait_ge(final_ready, tally.next("final_ready", KC))
                    act_norm(act, tally, True)
                    act_gla(act, tally, layer, toks)
                    act_conv2(act, tally, toks)
                    act_attention(act, tally, layer, toks)
                    act_out2(act, tally)
                elif stage[:-1] == "block2_ffn":
                    with_ctx = stage[-1] == "0"
                    act_norm(act, tally, with_ctx)
                    act_ffn(act, tally, with_ctx, last=not with_ctx)
                elif stage == "final":
                    act_norm(act, tally, False, final=True)

        @block.vector
        def _(dve):
            tally = Tally()
            for j, place in enumerate((*slot_free, *misc_free)):
                dve.memset(small[:, 56 + j:57 + j], 0.0).then_inc(place, 1)
            dve.wait_ge(const_landed, 16 * len(consts))
            for m in range(KC):
                dve.tensor_tensor(H[:, m, 0:NX], H[:, m, 0:NX], pos[:, m, :], ALU.add).then_inc(dve_step, 1)
                dve.wait_ge(dve_step, tally.next("dve_step"))
            for stage in stages:
                if stage == "filters":
                    dve_filters(dve, tally)
                elif stage == "block1_ffn1":
                    dve_mod(dve, tally, MOD1_COLS, "mod_b")
                    for s in range(4):
                        dve.wait_ge(k_stored[s], 2 * 16 * sum(K_STORES[s]))
                    dve_norm(dve, tally, True, 0, 1)
                    dve_ffn(dve, tally, True, 2, 0.5)
                elif stage == "block1_mix":
                    dve_norm(dve, tally, True, 3, 4)
                    dve_hgrn(dve, tally)
                    dve_hyena(dve, tally)
                    dve_merge(dve, tally)
                elif stage == "block1_ffn2":
                    dve_norm(dve, tally, False, 6, 7)
                    dve_ffn(dve, tally, False, 8, 0.5)
                    dve_norm(dve, tally, False, final=vec("final_w", 0, 8))
                elif stage[:-1] == "block2_mix":
                    layer = int(stage[-1])
                    toks = NX if layer else NT
                    dve_mod(dve, tally, MOD2_COLS, f"b_mod{layer}")
                    if layer == 0:
                        dve.wait_ge(ctx2_landed, 16)
                    dve_norm(dve, tally, True, 0, 1, gain=vec("n1g", 8 * layer, 8))
                    dve_gla(dve, tally, layer, toks)
                    dve_conv2(dve, tally, layer, toks)
                    dve_attention(dve, tally, layer, toks)
                    dve_out2(dve, tally, toks == NT)
                elif stage[:-1] == "block2_ffn":
                    layer = int(stage[-1])
                    dve_norm(dve, tally, layer == 0, 3, 4, gain=vec("n2g", 8 * layer, 8))
                    dve_ffn(dve, tally, layer == 0, 5, 1.0)
                elif stage == "final":
                    dve_norm(dve, tally, False, final=vec("final2", 0, 8))
            dve.memset(small[:, 62:63], 0.0).then_inc(h_ready, 1)


STAGES = ("filters", "block1_ffn1", "block1_mix", "block1_ffn2", "block2_mix0", "block2_ffn0", "block2_mix1",
          "block2_ffn1", "final")
MAGIC = 1.5 * 2.0 ** 23
TWO_PI_HI = 6.28125
PI_F = 3.14159250
K_STORES = ((2, 3), (1, 1), (1, 1), (1, 1))
ATT_SCALE = HD ** -0.5



def _tiles(w):
    n = w.shape[1] // P
    return w.reshape(KC, P, n, P).transpose(2, 1, 0, 3).reshape(n, P, D)


def _mod_tiles(w):
    n = w.shape[1] // 512
    return w.reshape(4, 2, P, n, 512).transpose(3, 0, 2, 1, 4).reshape(4 * n, P, D)


def _ffn_tiles(gate, up, down):
    out = []
    at = 0
    g, u = _tiles(gate), _tiles(up)
    for F in F_THIRDS:
        out.append(np.stack([g[at:at + F], u[at:at + F]], 1).reshape(2 * F, P, D))
        d = down[at * P:(at + F) * P].reshape(F, P, KC, P).transpose(2, 1, 0, 3).reshape(KC, P, F * P)
        out.append(np.pad(d, ((0, 0), (0, 0), (0, D - F * P))))
        at += F
    return out


def _cols(v):
    v = np.asarray(v)
    return v.reshape(-1, P).T


def _tables():
    t = {}
    eye = np.eye(P, dtype=np.float32)
    t["ident"], t["ones"] = eye, np.ones((P, P), np.float32)
    idx = np.arange(P)
    t["blk"] = (idx[:, None] // HD == idx[None, :] // HD).astype(np.float32)
    r = np.zeros((P, P), np.float32)
    for m in range(P):
        if m % 32 < 16:
            r[m + 16, m] = -1.0
        else:
            r[m - 16, m] = 1.0
    t["rot"] = r
    t["reset"] = np.broadcast_to((np.arange(NT) % CH != 0).astype(np.float32), (P, NT)).copy()
    mk = np.zeros((P, 2, 8, P), np.int32)
    s, q = idx[:, None], idx[None, :]
    for li, b in enumerate(LEVELS):
        same = s // (2 * b) == q // (2 * b)
        first_s, first_q = (s // b) % 2 == 0, (q // b) % 2 == 0
        mk[:, 0, li] = same & first_s & ~first_q
        mk[:, 1, li] = same & ~first_s & first_q
    t["masks"] = mk
    am = np.zeros((P, 3, P), np.float32)
    am[:, 0] = np.where(q >= s, 0.0, -1e30)
    am[:, 2] = np.where(q <= s, 0.0, -1e30)
    t["amask"] = am.reshape(P, 3 * P)
    grid = 64
    rows_ = NX // grid
    quarter = D // 4
    omega = (1.0 / (10000.0 ** (np.arange(quarter, dtype=np.float32) / quarter))).astype(np.float32)
    ar = np.arange(rows_, dtype=np.float32)[:, None] * omega
    ac = np.arange(grid, dtype=np.float32)[:, None] * omega
    er = np.concatenate([np.sin(ar), np.cos(ar)], -1)
    ec = np.concatenate([np.sin(ac), np.cos(ac)], -1)
    emb = np.concatenate([np.broadcast_to(er[:, None], (rows_, grid, D // 2)),
                          np.broadcast_to(ec[None], (rows_, grid, D // 2))], -1).reshape(NX, D)
    t["pos"] = emb.T.reshape(KC, P, NX).transpose(1, 0, 2).astype(np.float32).copy()
    p = np.arange(NX, dtype=np.float32)
    tt = p / (NX - 1)
    w = (2.0 * np.pi * p / NX).astype(np.float32)
    f = np.linspace(1e-4, 15, 16, dtype=np.float32)
    ang = w[:, None] * f[None]
    z = np.concatenate([tt[:, None], np.cos(ang), -np.sin(ang)], -1).astype(np.float32)
    t["fz"] = np.concatenate([z, z[::-1]], 0).T.copy()
    lo, hi = np.log(1e-2) / 1.5, np.log(1e-2) / 0.3
    deltas = np.abs(np.linspace(lo, hi, 512, dtype=np.float32))
    win = (np.exp(-tt[:, None] * deltas[None]) + 0.05).astype(np.float32)
    t["fwin"] = np.stack([win, win[::-1]]).reshape(2, 4, P, 512).transpose(2, 0, 1, 3).astype(np.float32).copy()
    fr = np.concatenate([np.arange(0, 512, 2), np.arange(1, 512, 2)])
    n = np.arange(NX)
    a = 2 * np.pi * ((n[:, None] * fr[None]) % 1024) / 1024.0
    C = np.cos(a)
    S = -np.sin(a)
    S[:, 0] = np.where(n % 2 == 0, 1.0, -1.0)
    t["dft"] = np.concatenate([C, S], 1).reshape(4, P, 1024).transpose(1, 0, 2).astype(np.float32).copy()
    inv = np.concatenate([2 * C, 2 * S], 1)
    inv[:, 0] = 1.0
    inv[:, 512] = S[:, 0]
    t["idft"] = (inv.T / 1024.0).reshape(8, P, NX).transpose(1, 0, 2).astype(np.float32).copy()
    tok = np.arange(NX)
    row, col = (tok // grid).astype(np.float32), (tok % grid).astype(np.float32)
    inv_freq = (10000.0 ** (-np.arange(16, dtype=np.float32) / 16)).astype(np.float32)
    h = idx % HD
    pos = np.where((h // 32 == 0)[:, None], row[None], col[None])
    an = pos * inv_freq[h % 16][:, None]
    t["rope"] = np.stack([np.cos(an), np.sin(an)], 1).astype(np.float32)
    return t


def _fm(a, n):
    return np.asarray(a).T.reshape(KC, P, n).transpose(1, 0, 2)


def kernel(**inputs):
    import concourse.bacc as _bacc
    from concourse.bass_utils import run_bass_kernel_spmd as _run

    x = {k: np.asarray(v) for k, v in inputs.items()}
    w = x["w_in"][0]
    v_, ffw, fbw, q_, g_ = (w[:, i * 512:(i + 1) * 512] for i in range(5))
    hy, mer = w[:, 2560:4096], w[:, 4096:6144]
    hyt = _tiles(hy)
    mt = _tiles(mer)
    pab = np.concatenate([x["w_proj_a"][0].reshape(4, P, KC, P), x["w_proj_b"][0].reshape(4, P, KC, P)], 0
                         ).transpose(2, 1, 0, 3).reshape(KC, P, D)
    s = [_mod_tiles(x["mod_w"][0])]
    s += _ffn_tiles(x["ffn_w_gate"][0, 0], x["ffn_w_up"][0, 0], x["ffn_w_down"][0, 0])
    s += [_tiles(v_), _tiles(q_), _tiles(ffw), _tiles(fbw), _tiles(g_)]
    s += [hyt.reshape(3, 4, P, D).transpose(1, 0, 2, 3).reshape(12, P, D)]
    s += [np.stack([mt[:KC], mt[KC:], pab], 1).reshape(3 * KC, P, D)]
    s += [_tiles(x["w_out"][0])]
    s += _ffn_tiles(x["ffn_w_gate"][0, 1], x["ffn_w_up"][0, 1], x["ffn_w_down"][0, 1])
    heads = np.concatenate([np.concatenate([np.arange(c * HD, (c + 1) * HD), np.arange((c + 4) * HD, (c + 5) * HD)])
                            for c in range(4)])
    for layer in range(2):
        wi = x["w_in_2"][layer]
        ci, cb, cc = wi[:, 0:256], wi[:, 256:512], wi[:, 512:768]
        aq_, ak_, av_ = wi[:, 768:1280][:, heads], wi[:, 1280:1408], wi[:, 1408:1536]
        gq_, gk_, gv_, gg_ = (wi[:, 1536 + 256 * i:1792 + 256 * i] for i in range(4))
        s += [_mod_tiles(x["w_mod_2"][layer])]
        s += [_tiles(a) for a in (gv_, gq_, gk_, gg_, ci, cc, cb, ak_, av_, aq_)]
        wo = x["w_out_2"][layer]
        s += [_tiles(np.concatenate([wo[:256], wo[256:768][heads], wo[768:]], 0))]
        up = x["w_up_2"][layer]
        s += _ffn_tiles(up[:, :DFF], up[:, DFF:], x["w_down_2"][layer])
    lrw_ = np.stack([x["w_in_2"][l][:, 2560:2592].reshape(KC, P, 32).transpose(1, 0, 2) for l in range(2)])
    gw = np.zeros((2, 32, 4, P), np.float32)
    for d in range(2):
        gw[:, 16 * d:16 * d + 16, 2 * d:2 * d + 2] = x["gla_gate_w_2"][:, d].reshape(2, 16, 2, P)

    vecs = np.zeros((P, NVEC), np.float32)

    def put(name, v):
        a, n = VEC_AT[name]
        assert v.shape[1] == n, (name, v.shape)
        vecs[:v.shape[0], a:a + n] = v

    put("mod_b", _cols(x["mod_b"][0]))
    put("b_mod0", _cols(x["b_mod_2"][0]))
    put("b_mod1", _cols(x["b_mod_2"][1]))
    put("cvec", np.stack([_cols(x["c"]), _cols(x["c_ctx"])], -1).reshape(P, 16))
    put("cvec2", np.stack([_cols(x["c_2"]), _cols(x["c_ctx_2"])], -1).reshape(P, 16))
    put("lbl", _cols(x["hgrn_lb_logits"]))
    put("hgrn_w", _cols(x["hgrn_norm_w"]))
    put("conv_w", _cols(x["hyena_conv_w"]))
    put("conv_b", _cols(x["hyena_conv_b"]))
    put("hy_bias", _cols(x["hyena_bias"]))
    put("final_w", _cols(x["final_norm_w"]))
    put("n1g", _cols(x["norm1_g_2"]))
    put("n2g", _cols(x["norm2_g_2"]))
    put("conv2_w", _cols(x["conv_w_2"]))
    put("gate_b", _cols(x["gla_gate_b_2"]))
    put("gla_w", np.concatenate([x["gla_norm_g_2"].T] * 2, 0))
    put("final2", _cols(x["final_norm_g_2"]))
    put("sink", np.broadcast_to(x["attn_sink_2"].reshape(1, 16), (P, 16)))
    put("hyv", np.stack([x["hyena_b1"][0], x["hyena_freq1"][0], x["hyena_b2"][0], x["hyena_freq2"][0]], 1))
    put("s4", np.repeat(np.eye(2, dtype=np.float32), 2, 0))

    arrays = _tables()
    arrays["stream"] = np.concatenate(s, 0)
    arrays["vecs"] = vecs
    arrays["h"] = np.concatenate([_fm(x["x"][0], NX), _fm(x["ctx"][0], NCTX)], 2)
    arrays["ctx2"] = _fm(x["ctx_2"][0], NCTX)
    arrays["fw1"], arrays["fw2"] = x["hyena_w1"][0], x["hyena_w2"][0]
    arrays["fw3"] = x["hyena_w3"][0].reshape(64, 4, 512)
    arrays["lrw"], arrays["gatew"] = lrw_, gw
    arrays = {k: np.ascontiguousarray(v) for k, v in arrays.items()}

    nc = _bacc.Bacc("TRN2", target_bir_lowering=False, num_devices=1)
    aps = {}
    for name, a in arrays.items():
        aps[name] = nc.dram_tensor(f"in_{name}", a.shape, mybir.dt.from_np(a.dtype), kind="ExternalInput").ap()
    out = nc.dram_tensor("out_t", (KC, P, NX), F32, kind="ExternalOutput").ap()
    build(nc, aps, out)
    r = _run(nc, [{f"in_{k}": v for k, v in arrays.items()}], core_ids=[0])
    y = r.results[0]["out_t"]
    return y.reshape(1, D, NX).transpose(0, 2, 1)
```

```python
from contextlib import ExitStack
from contextlib import contextmanager

import numpy as np

import concourse.bass as bass
from concourse import mybir

ALU = mybir.AluOpType
ACT = mybir.ActivationFunctionType
AX = mybir.AxisListType
F32 = mybir.dt.float32
F32R = mybir.dt.float32r
U8 = mybir.dt.uint8
I32 = mybir.dt.int32

P = 128
D = 1024
KC = D // P
NX = 512
NCTX = 256
NT = NX + NCTX
CH = P
XCH = NX // CH
ALLCH = NT // CH
F_THIRDS = (8, 8, 6)
DFF = sum(F_THIRDS) * P
EPS = 1e-6
LEVELS = (64, 32, 16, 8, 4, 2, 1)
RING = 4
NFREQ = 8
ATT_HEADS = 8
HD = 64

VEC_FIELDS = (
    ("mod_b", 72), ("b_mod0", 48), ("b_mod1", 48), ("cvec", 16), ("cvec2", 16), ("lbl", 16),
    ("hgrn_w", 1), ("conv_w", 36), ("conv_b", 12), ("hy_bias", 8), ("final_w", 8),
    ("n1g", 16), ("n2g", 16), ("conv2_w", 12), ("gate_b", 8), ("gla_w", 2), ("final2", 8),
    ("sink", 16), ("hyv", 4), ("s4", 2),
)
VEC_AT = {}
_at = 0
for _name, _n in VEC_FIELDS:
    VEC_AT[_name] = (_at, _n)
    _at += _n
NVEC = _at + _at % 2


class Tally:

    def __init__(self):
        self.n = {}
        self.i, self.per = None, {}

    def now(self, name, more=0, share=1):
        base = self.n.get(name, 0) // share + more
        per = self.per.get(name, 0) // share
        return self.i * per + base if self.i is not None and per else base

    def passed(self, name, count=1):
        self.n[name] = self.n.get(name, 0) + count

    def next(self, name, count=1):
        self.passed(name, count)
        return self.now(name)

    @contextmanager
    def turns(self, i, turns, **per):
        before = dict(self.n)
        self.i, self.per = i, per
        yield
        for name in set(self.n) | set(per):
            grew = self.n.get(name, 0) - before.get(name, 0)
            per_turn = per.get(name, 0)
            assert grew == per_turn, (name, grew, per_turn)
            self.n[name] = self.n.get(name, 0) + grew * (turns - 1)
        self.i, self.per = None, {}

    def take(self, kind):
        self.passed(kind)
        return (self.n[kind] - 1) % 2

    def place(self, kind, back=0):
        return (self.n.get(kind, 0) - back) % 2

    def free(self, kind, back=0):
        return self.read(kind, back, 1)

    def read(self, kind, back=1, more=2):
        base = (self.n.get(kind, 0) - back) // 2 + more
        per = self.per.get(kind, 0) // 2
        return self.i * per + base if self.i is not None and per else base


def memory_map():
    at = {}
    top = 0

    def put(name, words):
        nonlocal top
        at[name] = top
        top += (words + 7) // 8 * 8

    for name, words in (
        ("ident", P), ("ones", P), ("blk", P), ("rot", P), ("reset", NT), ("masks", 2 * 8 * P // 4),
        ("amask", 3 * P), ("vecs", NVEC), ("mods", 144), ("cs", 16), ("c4", 32), 
        ("scv", 16), ("hgv", 16), ("lb", 32), ("small", 64), ("mx", 48), ("dec", 16), ("inv", 32), ("lrs", 512),
        ("raw", RING * D), ("wr_hi", RING * D), ("wr_lo", RING * D),
        ("H", KC * NT), ("xx_hi", KC * NX), ("xx_lo", KC * NX), ("xc_hi", KC * NCTX), ("xc_lo", KC * NCTX),
    ):
        put(name, words)
    at["arena"] = top
    return at


def build(nc, ins, out):
    A = memory_map()
    base = (nc.sbuf_base + 31) // 32 * 32
    arena_words = (nc.sbuf_usable_end - base) // 4 - A["arena"]

    with ExitStack() as ctx:
        def at(name, shape, words, dt=F32, parts=P):
            t = nc.alloc_sbuf_tensor_at(name, [parts, *shape], dt, offset=base + 4 * words)
            return t

        def fixed(name, shape, dt=F32, parts=P):
            return at(name, shape, A[name], dt, parts)

        def arena(name, shape, words, dt=F32, parts=P):
            n = int(np.prod(shape)) if dt != U8 else int(np.prod(shape)) // 4
            assert words + n <= arena_words, (name, words, n, arena_words)
            return at(name, shape, A["arena"] + words, dt, parts)

        ident, ones, blk, rot = (fixed(n, [P]) for n in ("ident", "ones", "blk", "rot"))
        reset = fixed("reset", [NT])
        masks = fixed("masks", [2, 8, P], U8)
        amask = fixed("amask", [3 * P])
        vecs = fixed("vecs", [NVEC])
        mods = fixed("mods", [72, 2])
        cs = fixed("cs", [KC, 2])
        c4 = fixed("c4", [KC, 4], F32R)
        scv = fixed("scv", [KC, 2])
        hgv = fixed("hgv", [KC, 2])
        lb = fixed("lb", [4, 8])
        small = fixed("small", [64])
        mx = fixed("mx", [ATT_HEADS, 6])
        dec = fixed("dec", [2, 8])
        inv = fixed("inv", [32])
        lrs = (at("lrs_hi", [KC, 32], A["lrs"], F32R), at("lrs_lo", [KC, 32], A["lrs"] + 256, F32R))
        raw = fixed("raw", [RING, D])
        wr_hi = fixed("wr_hi", [RING, D], F32R)
        wr_lo = fixed("wr_lo", [RING, D], F32R)
        H = fixed("H", [KC, NT])
        xx = (fixed("xx_hi", [KC, NX], F32R), fixed("xx_lo", [KC, NX], F32R))
        xc = (fixed("xc_hi", [KC, NCTX], F32R), fixed("xc_lo", [KC, NCTX], F32R))

        hid = (arena("hid_hi", [8, NT], 0, F32R), arena("hid_lo", [8, NT], 8 * NT, F32R))
        ff_gate = arena("ff_gate", [2, NT], 16 * NT)
        ff_raw = arena("ff_raw", [2, NT], 18 * NT)
        rows = (at("rows_filters", [512], A["xx_lo"] + 3072), arena("rows_ffn", [512], 15360))
        xt = arena("xt", [2, NT], 16 * NT)
        rstd = arena("rstd", [NT], 18 * NT)
        sq = arena("sq", [2, NT], 16384)
        ssq = arena("ssq", [NT], 16384 + 2 * NT)
        pos = at("pos", [KC, NX], A["xc_hi"])
        fz = arena("fz", [2 * NX], 0, parts=33)
        fw1 = arena("fw1", [64], 1024, parts=33)
        fw2 = arena("fw2", [64], 1088, parts=64)
        fw3 = arena("fw3", [4, 512], 1152, parts=64)
        fh = arena("fh", [2, 2 * NX], 3200, parts=64)
        fk = arena("fk", [2 * NX], 5248, parts=64)
        fwin = arena("fwin", [2, 4, 512], 6272)
        fe = arena("fe", [4, 512], 10368)
        fd = arena("fd", [4, 512], 12416)
        fabs = arena("fabs", [2, 2, 512], 14464)
        fst = arena("fst", [4, 512], 16512)
        dft0 = at("dft0", [4, 1024], A["xx_hi"])
        fa = at("fa", [2, 2, 512], A["xx_lo"])
        fzero = at("fzero", [512], A["xx_lo"] + 2048)
        fnorm = at("fnorm", [512], A["xx_lo"] + 2560)
        oab = (arena("oab_hi", [8, NX], 0, F32R), arena("oab_lo", [8, NX], 4096, F32R))
        dft = at("dft", [4, 1024], A["xc_hi"])
        idft = arena("idft", [8, 512], 8192)
        hp = arena("hp", [3, 514], 12288)
        hu = at("hu", [4, P], A["lrs"])
        hv = arena("hv", [3, NX], 13832)
        hK = arena("hK", [9, 2, P], 15368)
        hY = arena("hY", [8, P], 17672)

        def unit_space(tag, w, toks, nsub):
            r = {}
            for name, shape in (("lf", [NT]), ("cum", [NT]), ("eq", [NT]), ("ek", [NT]), ("ktok", [NT]),
                                ("S", [6, P])):
                r[name] = arena(f"{tag}_{name}", shape, w)
                w += NT
            for name, n in (("Z", 2), ("ex", 2), ("P", nsub)):
                r[name] = arena(f"{tag}_{name}", [n, toks], w)
                w += n * toks
            return r, w

        u1, end1 = unit_space("u1", 0, NX, 1)
        k1 = (arena("k1a", [NT], end1), arena("k1b", [NT], 15360))
        assert end1 + NT <= 8192
        vt1 = arena("vt1", [2, NT], 0)
        vtok1 = arena("vtok1", [ALLCH, 512], 8192)
        q1 = arena("q1", [4, NX], 11264)
        oacc1 = arena("oacc1", [4, NX], 13312)
        g1s = arena("g1s", [4, NX], 15360)
        hsq1 = arena("hsq1", [4, NX], 2048)
        masks32 = arena("masks32", [2, 8, P], 15360, I32)
        yy = (arena("y_hi", [8, NX], 8192, F32R), arena("y_lo", [8, NX], 12288, F32R))
        mg = arena("mg", [4, NX], 16384)
        mo = (arena("mo_hi", [8, NT], 0, F32R), arena("mo_lo", [8, NT], 8 * NT, F32R))
        u2, end2 = unit_space("u2", 0, NT, 2)
        assert end2 <= 9216, end2
        vt2 = arena("vt2", [2, NT], 0)
        gq = arena("gq", [2, NT], 9216)
        gk = arena("gk", [2, NT], 10752)
        vtok2 = arena("vtok2", [ALLCH, 256], 12288)
        oacc2 = arena("oacc2", [2, NT], 13824)
        gg = arena("gg", [2, NT], 15360)
        lr = arena("lr", [NT], 16896, parts=32)
        gatew = arena("gatew", [4, P], 17664, parts=32)
        lrw = arena("lrw", [KC, 32], 18176)
        hsq2 = arena("hsq2", [2, NT], 0)
        cv = arena("cv", [3, 2, NT], 12288)
        cu = arena("cu", [772], 12288 + 6 * NT)
        cy = arena("cy", [NT], 12288 + 6 * NT + 776)
        aq = arena("aq", [4, NT], 12288)
        akx = arena("akx", [NT], 12288 + 4 * NT)
        avt = arena("avt", [ALLCH, P], 12288 + 5 * NT)
        araw = arena("araw", [2, NT], 2 * NT)
        rope = arena("rope", [2, NX], 4 * NT)
        arot = arena("arot", [NX], 10 * NT)
        sl = at("sl", [2, 640], A["xx_hi"])
        pr = at("pr", [2, 640], A["xx_hi"] + 1280)
        pT = at("pT", [2, 640], A["xx_hi"] + 2560)

        ps = ctx.enter_context(nc.psum_tensor("ps", [P, 4, 1024], F32))

        def gslot(s):
            return ps[:, s, :]

        def mslot(s):
            return ps[:, 2 + s, :]

        kdram = nc.dram_tensor("hyena_k", [18, P, 512], F32, kind="Internal").ap()

        n_tiles = ins["stream"].shape[0]

        def vec(name, i=0, n=1):
            a, _ = VEC_AT[name]
            return vecs[:, a + i:a + i + n]

        def semaphore(name):
            return ctx.enter_context(nc.semaphore(name))

        tile_hi = semaphore("tile_hi")
        tile_lo = semaphore("tile_lo")
        tile_used = semaphore("tile_used")
        misc_done = semaphore("misc_done")
        dve_step = semaphore("dve_step")
        act_step = semaphore("act_step")
        first_landed = semaphore("first_landed")
        second_landed = semaphore("second_landed")
        third_landed = semaphore("third_landed")
        masks_landed = semaphore("masks_landed")
        c_hi = semaphore("c_hi")
        c_ready = semaphore("c_ready")
        sq_ready = semaphore("sq_ready")
        ssq_step = semaphore("ssq_step")
        root_ready = semaphore("root_ready")
        xt_ready = semaphore("xt_ready")
        xhi_ready = semaphore("xhi_ready")
        x_ready = semaphore("x_ready")
        hhi_ready = semaphore("hhi_ready")
        hid_ready = semaphore("hid_ready")
        arg_ready = semaphore("arg_ready")
        sin_ready = semaphore("sin_ready")
        abs_ready = semaphore("abs_ready")
        abs_summed = semaphore("abs_summed")
        e_ready = semaphore("e_ready")
        lb_in = semaphore("lb_in")
        lb_exp = semaphore("lb_exp")
        f_ready = semaphore("f_ready")
        lf_ready = semaphore("lf_ready")
        decay_in = semaphore("decay_in")
        decay_ready = semaphore("decay_ready")
        ke_ready = semaphore("ke_ready")
        ex_in = semaphore("ex_in")
        ex_out = semaphore("ex_out")
        z_ready = semaphore("z_ready")
        nsq_ready = semaphore("nsq_ready")
        inv_ready = semaphore("inv_ready")
        ohi_ready = semaphore("ohi_ready")
        mix_ready = semaphore("mix_ready")
        dft_landed = semaphore("dft_landed")
        k_landed = semaphore("k_landed")
        hv_ready = semaphore("hv_ready")
        z_done = semaphore("z_done")
        freq_ready = semaphore("freq_ready")
        yraw_ready = semaphore("yraw_ready")
        yhi_ready = semaphore("yhi_ready")
        y_ready = semaphore("y_ready")
        ctx2_landed = semaphore("ctx2_landed")
        arena_free = semaphore("arena_free")
        gate_landed = semaphore("gate_landed")
        lrw_landed = semaphore("lrw_landed")
        lrw_hi = semaphore("lrw_hi")
        lrw_ready = semaphore("lrw_ready")
        lr_ready = semaphore("lr_ready")
        gx_ready = semaphore("gx_ready")
        ge_ready = semaphore("ge_ready")
        conv_ready = semaphore("conv_ready")
        conv_done = semaphore("conv_done")
        edge_ready = semaphore("edge_ready")
        rope_landed = semaphore("rope_landed")
        rope_done = semaphore("rope_done")
        m_ready = semaphore("m_ready")
        exp_ready = semaphore("exp_ready")
        pn_ready = semaphore("pn_ready")
        pt_done = semaphore("pt_done")
        pt_ready = semaphore("pt_ready")
        ao_done = semaphore("ao_done")
        final_ready = semaphore("final_ready")
        out_landed = semaphore("out_landed")
        landed = [semaphore(f"landed{s}") for s in range(RING)]
        slot_free = [semaphore(f"slot_free{s}") for s in range(2)]
        misc_free = [semaphore(f"misc_free{s}") for s in range(2)]
        k_stored = [semaphore(f"k_stored{s}") for s in range(4)]


        def tile_slot(tally):
            return tally.n.get("tile_used", 0) % RING

        def pe_tile(pe, tally, groups, order=None):
            s = tile_slot(tally)
            pe.wait_ge(tile_lo, tally.now("tile_used", 1))
            last = None
            for gi, blocks in enumerate(groups):
                slot = tally.take("group")
                pe.wait_ge(slot_free[slot], tally.free("group", 1))
                for bi, (j, spans) in enumerate(blocks):
                    if order is not None and gi == 0:
                        pe.wait_ge(order[0], order[1] + bi + 1)
                    w_hi, w_lo = wr_hi[:, s, j * P:(j + 1) * P], wr_lo[:, s, j * P:(j + 1) * P]
                    for pi, (w, part) in enumerate(((w_hi, 0), (w_hi, 1), (w_lo, 0))):
                        for rhs, col, n in spans:
                            last = pe.matmul(gslot(slot)[:, col:col + n], w, rhs[part],
                                             start=(bi == 0 and pi == 0),
                                             stop=(bi == len(blocks) - 1 and pi == 2))
            last.then_inc(tile_used, 1)
            tally.passed("tile_used")

        def pe_x_part(pe, tally, first, end):
            s = tile_slot(tally)
            if first == 0:
                pe.wait_ge(tile_lo, tally.now("tile_used", 1))
                pe.wait_ge(slot_free[tally.place("group")], tally.free("group"))
            slot = tally.place("group")
            for k in range(first, end):
                w_hi, w_lo = wr_hi[:, s, k * P:(k + 1) * P], wr_lo[:, s, k * P:(k + 1) * P]
                for pi, (w, part) in enumerate(((w_hi, 0), (w_hi, 1), (w_lo, 0))):
                    for rhs, col, n in x_spans(k, True):
                        last = pe.matmul(gslot(slot)[:, col:col + n], w, rhs[part],
                                         start=(k == 0 and pi == 0), stop=(k == KC - 1 and pi == 2))
            if end == KC:
                last.then_inc(tile_used, 1)
                tally.passed("tile_used")
                tally.passed("group")

        def wide_spans(pair, k, with_ctx):
            s = [((pair[0][:, k, 0:NX], pair[1][:, k, 0:NX]), 0, NX)]
            if with_ctx:
                s.append(((pair[0][:, k, NX:NT], pair[1][:, k, NX:NT]), NX, NCTX))
            return s

        def x_spans(k, with_ctx):
            s = [((xx[0][:, k, :], xx[1][:, k, :]), 0, NX)]
            if with_ctx:
                s.append(((xc[0][:, k, :], xc[1][:, k, :]), NX, NCTX))
            return s

        def pe_x_tiles(pe, tally, count, with_ctx, order=None):
            for n in range(count):
                pe_tile(pe, tally, [[(k, x_spans(k, with_ctx)) for k in range(KC)]], order if n == 0 else None)

        def split_tile(act, tally):
            ahead = tally.n["tile_used"] - 1 + RING
            if tally.i is None and ahead >= n_tiles:
                return
            s = ahead % RING
            want = 16 * (ahead // RING + 1)
            if tally.i is not None:
                want = tally.i * (16 * tally.per["tile_used"] // RING) + want
            act.wait_ge(tile_used, tally.now("tile_used"))
            act.wait_ge(landed[s], want)
            act.activation(wr_hi[:, s, :], raw[:, s, :], ACT.Copy).then_inc(tile_hi, 1)
            act.wait_ge(tile_hi, tally.next("tile_hi"))

        def act_proj(act, tally, dst, n, func=ACT.Copy, done=None):
            tally.passed("tile_used")
            slot = tally.take("group")
            act.wait_ge(tile_used, tally.now("tile_used"))
            pieces = dst if isinstance(dst, list) else [(dst, 0, n)]
            for pi, (o, a, b) in enumerate(pieces):
                ins = act.activation(o, gslot(slot)[:, a:b], func)
                if pi < len(pieces) - 1:
                    ins.then_inc(act_step, 1)
                    act.wait_ge(act_step, tally.next("act_step"))
                else:
                    ins.then_inc(slot_free[slot], 1)
                    act.wait_ge(slot_free[slot], tally.read("group"))
            split_tile(act, tally)

        def skip_tiles(tally, tiles, groups=None):
            tally.passed("tile_used", tiles)
            tally.passed("group", tiles if groups is None else groups)



        def pe_mod_place(pe, tally):
            place = tally.place("misc_done")
            pe.wait_ge(misc_free[place], tally.free("misc_done"))
            return place

        def pe_mod_tile(pe, tally, place, kk):
            s = tile_slot(tally)
            pe.wait_ge(tile_lo, tally.now("tile_used", 1))
            for h in range(2):
                for wi, w in enumerate((wr_hi, wr_lo)):
                    last = pe.matmul(mslot(place)[0:4, 0:512], c4[:, 2 * kk + h, :], w[:, s, h * 512:(h + 1) * 512],
                                     start=(kk == 0 and h == 0 and wi == 0), stop=(kk == 3 and h == 1 and wi == 1))
                if kk == 3 and h == 0:
                    last.then_inc(misc_done, 1)
            last.then_inc(tile_used, 1)
            tally.passed("tile_used")

        def pe_mod_columns(pe, tally, row, back=1):
            pe.wait_ge(misc_free[tally.place("misc_done", back)], tally.read("misc_done", back))
            place = tally.place("misc_done")
            pe.wait_ge(misc_free[place], tally.free("misc_done"))
            m = mslot(place)
            for j in range(4):
                last = pe.matmul(m[:, 2 * j:2 * j + 2], row[0:4, j * P:(j + 1) * P],
                                 vecs[0:4, VEC_AT["s4"][0]:VEC_AT["s4"][0] + 2], start=True, stop=True)
            last.then_inc(misc_done, 1)
            tally.passed("misc_done")

        def act_mod_input(act, tally, cname):
            a = VEC_AT[cname][0]
            act.activation(cs[:, :, :], vecs[:, a:a + 16].rearrange("p (k v) -> p k v", v=2), ACT.Silu
                ).then_inc(act_step, 1)
            act.wait_ge(act_step, tally.next("act_step"))
            act.activation(c4[:, :, 0:4:2], cs[:, :, :], ACT.Copy).then_inc(c_hi, 1)
            act.wait_ge(c_hi, tally.next("c_hi"))

        def act_mod_tiles(act, tally, count):
            for _ in range(count):
                tally.passed("tile_used")
                split_tile(act, tally)

        def dve_mod_input(dve, tally):
            dve.wait_ge(c_hi, tally.next("c_hi"))
            dve.tensor_tensor(c4[:, :, 1:4:2], cs[:, :, :], c4[:, :, 0:4:2], ALU.subtract).then_inc(c_ready, 1)
            dve.wait_ge(c_ready, tally.next("c_ready"))

        def dve_mod_rows(dve, tally, row):
            ms = tally.take("misc_done")
            dve.wait_ge(tile_used, tally.now("tile_used"))
            dve.tensor_copy(row[0:4, :], mslot(ms)[0:4, 0:512]).then_inc(misc_free[ms], 1)
            dve.wait_ge(misc_free[ms], tally.read("misc_done"))

        def dve_mod_columns(dve, tally, bias, m):
            ms = tally.take("misc_done")
            dve.wait_ge(misc_done, tally.now("misc_done"))
            dve.tensor_tensor(mods[:, bass.ds(m, 4), :], mslot(ms)[:, 0:8].rearrange("p (j v) -> p j v", v=2),
                              vecs[:, bass.ds(m + bias, 4)].unsqueeze(2).broadcast_to([P, 4, 2]), ALU.add
                ).then_inc(misc_free[ms], 1)
            dve.wait_ge(misc_free[ms], tally.read("misc_done"))



        def pe_token_sums(pe, tally, squares, columns):
            place = tally.place("misc_done")
            pe.wait_ge(misc_free[place], tally.free("misc_done"))
            m = mslot(place)
            at_chunk = 0
            for sq_part, n in squares:
                for c in range(n // P):
                    last = pe.matmul(m[:, 2 * at_chunk:2 * at_chunk + 2], sq_part[:, c * P:(c + 1) * P], columns,
                                     start=True, stop=True)
                    at_chunk += 1
            last.then_inc(misc_done, 1)
            tally.passed("misc_done")

        def pe_spread(pe, tally, first, n, groups=1):
            place = tally.place("misc_done")
            pe.wait_ge(misc_free[place], tally.free("misc_done"))
            m = mslot(place)
            for c in range(n // P):
                for half in range(groups):
                    k = 2 * (first + c) + half
                    f = slice(half * HD, (half + 1) * HD) if groups == 2 else slice(0, P)
                    last = pe.matmul(m[f, c * P:(c + 1) * P], inv[:, k:k + 1].broadcast_to([P, P // groups]),
                                     ident[:, :], start=True, stop=True)
            last.then_inc(misc_done, 1)
            tally.passed("misc_done")

        def act_root(act, tally, columns):
            tally.take("misc_done")
            act.wait_ge(misc_free[tally.place("misc_done", 1)], tally.read("misc_done"))
            act.activation(inv[:, 0:columns], inv[:, 0:columns], ACT.Sqrt).then_inc(root_ready, 1)
            act.wait_ge(root_ready, tally.next("root_ready"))

        def dve_inverse(dve, tally, columns, width):
            ms = tally.take("misc_done")
            dve.wait_ge(misc_done, tally.now("misc_done"))
            dve.tensor_scalar(inv[:, 0:columns], mslot(ms)[:, 0:columns], 1.0 / width, EPS, ALU.mult, ALU.add
                ).then_inc(misc_free[ms], 1)
            dve.wait_ge(misc_free[ms], tally.read("misc_done"))
            dve.wait_ge(root_ready, tally.next("root_ready"))
            dve.reciprocal(inv[:, 0:columns], inv[:, 0:columns]).then_inc(inv_ready, 1)
            dve.wait_ge(inv_ready, tally.next("inv_ready"))


        def act_square(act, tally, m, place, n):
            act.wait_ge(slot_free[tally.place("group", 1)], tally.read("group", 1))
            act.wait_ge(ssq_step, tally.next("ssq_step"))
            act.activation(sq[:, place:place + 1, 0:n], H[:, bass.ds(m, 1), 0:n], ACT.Square).then_inc(sq_ready, 1)
            act.wait_ge(sq_ready, tally.next("sq_ready"))

        def dve_sum_start(dve, tally):
            for half in range(2):
                dve.memset(ssq[:, half * NT // 2:(half + 1) * NT // 2], 0.0).then_inc(ssq_step, 1)
                dve.wait_ge(ssq_step, tally.next("ssq_step"))

        def dve_sum(dve, tally, place, n):
            dve.wait_ge(sq_ready, tally.next("sq_ready"))
            dve.tensor_tensor(ssq[:, 0:n], ssq[:, 0:n], sq[:, place, 0:n], ALU.add).then_inc(ssq_step, 1)
            dve.wait_ge(ssq_step, tally.next("ssq_step"))

        def act_norm(act, tally, with_ctx, shift=0, final=False, summed=False):
            n = NT if with_ctx else NX
            if not summed:
                act.wait_ge(slot_free[tally.place("group", 1)], tally.read("group", 1))
                act.wait_ge(slot_free[tally.place("group", 2)], tally.read("group", 2))
                for m in range(KC):
                    act.wait_ge(ssq_step, tally.next("ssq_step"))
                    act.activation(sq[:, m % 2, 0:n], H[:, m, 0:n], ACT.Square).then_inc(sq_ready, 1)
                    act.wait_ge(sq_ready, tally.next("sq_ready"))
                tally.passed("ssq_step", 2)
            act_root(act, tally, 2 * n // P)
            ms = tally.take("misc_done")
            act.wait_ge(misc_done, tally.now("misc_done"))
            act.activation(rstd[:, 0:n], mslot(ms)[:, 0:n], ACT.Copy).then_inc(misc_free[ms], 1)
            act.wait_ge(misc_free[ms], tally.read("misc_done"))
            if final:
                return
            for m in range(KC):
                act.wait_ge(xt_ready, tally.next("xt_ready"))
                ins = act.activation(xx[0][:, m, :], xt[:, m % 2, 0:NX], ACT.Identity,
                                     bias=mods[:, 8 * shift + m, 0:1])
                if with_ctx:
                    ins.then_inc(act_step, 1)
                    act.wait_ge(act_step, tally.next("act_step"))
                    ins = act.activation(xc[0][:, m, :], xt[:, m % 2, NX:NT], ACT.Identity,
                                         bias=mods[:, 8 * shift + m, 1:2])
                ins.then_inc(xhi_ready, 1)
                act.wait_ge(xhi_ready, tally.next("xhi_ready"))

        def pe_norm(pe, tally, with_ctx):
            n = NT if with_ctx else NX
            pe.wait_ge(ssq_step, tally.next("ssq_step", KC + 2))
            pe_token_sums(pe, tally, [(ssq, n)], ones[:, 0:2])
            pe.wait_ge(inv_ready, tally.next("inv_ready"))
            pe_spread(pe, tally, 0, n)

        def dve_norm(dve, tally, with_ctx, shift=0, scale=0, gain=None, final=None, summed=False):
            n = NT if with_ctx else NX
            if final is None:
                dve.tensor_scalar(scv[:, :, :], mods[:, 8 * scale:8 * scale + 8, :], 1.0, None, ALU.add
                    ).then_inc(dve_step, 1)
                dve.wait_ge(dve_step, tally.next("dve_step"))
                if gain is not None:
                    dve.tensor_tensor(scv[:, :, :], scv[:, :, :],
                                      gain.unsqueeze(2).broadcast_to([P, KC, 2]), ALU.mult).then_inc(dve_step, 1)
                    dve.wait_ge(dve_step, tally.next("dve_step"))
            if not summed:
                dve_sum_start(dve, tally)
                for m in range(KC):
                    dve_sum(dve, tally, m % 2, n)
            dve_inverse(dve, tally, 2 * n // P, D)
            tally.take("misc_done")
            dve.wait_ge(misc_free[tally.place("misc_done", 1)], tally.read("misc_done"))

            def low(m):
                dve.wait_ge(xhi_ready, tally.next("xhi_ready"))
                ins = dve.scalar_tensor_tensor(out=xx[1][:, m, :], in0=xt[:, m % 2, 0:NX],
                                               scalar=mods[:, 8 * shift + m, 0:1], in1=xx[0][:, m, :],
                                               op0=ALU.add, op1=ALU.subtract)
                if with_ctx:
                    ins = dve.scalar_tensor_tensor(out=xc[1][:, m, :], in0=xt[:, m % 2, NX:NT],
                                                   scalar=mods[:, 8 * shift + m, 1:2], in1=xc[0][:, m, :],
                                                   op0=ALU.add, op1=ALU.subtract)
                ins.then_inc(x_ready, 1)
                dve.wait_ge(x_ready, tally.next("x_ready"))

            for m in range(KC):
                if final is not None:
                    dve.scalar_tensor_tensor(out=H[:, m, 0:n], in0=H[:, m, 0:n], scalar=final[:, m:m + 1],
                                             in1=rstd[:, 0:n], op0=ALU.mult, op1=ALU.mult).then_inc(final_ready, 1)
                    tally.passed("final_ready")
                    continue
                ins = dve.scalar_tensor_tensor(out=xt[:, m % 2, 0:NX], in0=H[:, m, 0:NX], scalar=scv[:, m, 0:1],
                                               in1=rstd[:, 0:NX], op0=ALU.mult, op1=ALU.mult)
                if with_ctx:
                    ins = dve.scalar_tensor_tensor(out=xt[:, m % 2, NX:NT], in0=H[:, m, NX:NT],
                                                   scalar=scv[:, m, 1:2], in1=rstd[:, NX:NT],
                                                   op0=ALU.mult, op1=ALU.mult)
                ins.then_inc(xt_ready, 1)
                dve.wait_ge(xt_ready, tally.next("xt_ready"))
                if m:
                    low(m - 1)
            if final is None:
                low(KC - 1)
            else:
                dve.wait_ge(final_ready, tally.now("final_ready"))



        def pe_ffn(pe, tally, with_ctx, with_mod=False):
            x_before = tally.n.get("x_ready", 0)
            tally.passed("x_ready", KC)
            if with_mod:
                pe.wait_ge(c_ready, tally.now("c_ready"))
            for third, F in enumerate(F_THIRDS):
                mod = with_mod and third < 2
                n_tile, n_misc = (8, 2) if mod else (4, 0)
                with pe.Fori(0, F // 2) as i, tally.turns(i, F // 2, tile_used=n_tile, group=4, misc_done=n_misc):
                    rows_place = pe_mod_place(pe, tally) if mod else None
                    for q in range(4):
                        if mod:
                            pe_mod_tile(pe, tally, rows_place, q)
                        pe_x_tiles(pe, tally, 1, with_ctx, (x_ready, x_before) if q == third == 0 else None)
                    if mod:
                        tally.passed("misc_done")
                        pe_mod_columns(pe, tally, rows[1])
                before = tally.n.get("hid_ready", 0)
                tally.passed("hid_ready", F)
                with pe.Fori(0, 2) as i, tally.turns(i, 2, tile_used=n_tile, group=4, misc_done=n_misc):
                    rows_place = pe_mod_place(pe, tally) if mod else None
                    for q in range(4):
                        if mod:
                            pe_mod_tile(pe, tally, rows_place, q)
                        pe_tile(pe, tally, [[(k, wide_spans(hid, k, with_ctx)) for k in range(F)]],
                                (hid_ready, before) if q == 0 else None)
                    if mod:
                        tally.passed("misc_done")
                        pe_mod_columns(pe, tally, rows[1])

        def act_ffn(act, tally, with_ctx, with_mod=False, last=False):
            n = NT if with_ctx else NX
            for third, F in enumerate(F_THIRDS):
                mod = with_mod and third < 2
                n_tile, n_misc = (8, 2) if mod else (4, 0)
                with act.Fori(0, F // 2) as i, tally.turns(i, F // 2, tile_used=n_tile, group=4, tile_hi=n_tile,
                                                           hhi_ready=2, misc_done=n_misc):
                    for q in range(2):
                        act_mod_tiles(act, tally, mod)
                        tally.passed("tile_used")
                        slot = tally.take("group")
                        act.wait_ge(slot_free[tally.place("group", 4)], tally.read("group", 4))
                        act.wait_ge(tile_used, tally.now("tile_used"))
                        act.activation(ff_gate[:, q, 0:n], gslot(slot)[:, 0:n], ACT.Silu).then_inc(slot_free[slot], 1)
                        act.wait_ge(slot_free[slot], tally.read("group"))
                        split_tile(act, tally)
                        act_mod_tiles(act, tally, mod)
                        tally.passed("tile_used")
                        tally.take("group")
                        act.wait_ge(slot_free[tally.place("group", 1)], tally.read("group", 1))
                        act.activation(hid[0][:, bass.ds(i * 2 + q, 1), 0:n], ff_raw[:, q:q + 1, 0:n],
                                       ACT.Copy).then_inc(hhi_ready, 1)
                        act.wait_ge(hhi_ready, tally.next("hhi_ready"))
                        split_tile(act, tally)
                    tally.passed("misc_done", n_misc)
                final_third = third == len(F_THIRDS) - 1
                if last and final_third:
                    for m in range(8):
                        skip_tiles(tally, 1)
                        split_tile(act, tally)
                        act_square(act, tally, m, m % 2, n)
                else:
                    with act.Fori(0, 2) as i, tally.turns(i, 2, tile_used=n_tile, group=4, tile_hi=n_tile,
                                                          misc_done=n_misc, ssq_step=4 * final_third,
                                                          sq_ready=4 * final_third):
                        for q in range(4):
                            act_mod_tiles(act, tally, mod)
                            skip_tiles(tally, 1)
                            split_tile(act, tally)
                            if final_third:
                                act_square(act, tally, i * 4 + q, q % 2, n)
                        tally.passed("misc_done", n_misc)
            tally.passed("ssq_step", 2)

        def dve_ffn(dve, tally, with_ctx, gate, factor, mod_bias=None):
            n = NT if with_ctx else NX
            dve.tensor_scalar(hgv[:, :, :], mods[:, 8 * gate:8 * gate + 8, :], factor, None, ALU.mult
                ).then_inc(dve_step, 1)
            dve.wait_ge(dve_step, tally.next("dve_step"))
            for third, F in enumerate(F_THIRDS):
                mod = mod_bias is not None and third < 2
                n_tile, n_misc = (8, 2) if mod else (4, 0)
                with dve.Fori(0, F // 2) as i, tally.turns(i, F // 2, tile_used=n_tile, group=4, hhi_ready=2,
                                                           hid_ready=2, misc_done=n_misc):
                    for q in range(2):
                        tally.passed("tile_used", int(mod))
                        skip_tiles(tally, 1)
                        tally.passed("tile_used", int(mod))
                        if mod and q == 1:
                            dve_mod_rows(dve, tally, rows[1])
                        tally.passed("tile_used")
                        slot = tally.take("group")
                        dve.wait_ge(slot_free[tally.place("group", 2)], tally.read("group", 2))
                        dve.wait_ge(tile_used, tally.now("tile_used"))
                        dve.tensor_tensor(ff_raw[:, q, 0:n], gslot(slot)[:, 0:n], ff_gate[:, q, 0:n],
                                          ALU.mult).then_inc(slot_free[slot], 1)
                        dve.wait_ge(slot_free[slot], tally.read("group"))
                        dve.wait_ge(hhi_ready, tally.next("hhi_ready"))
                        dve.tensor_tensor(hid[1][:, bass.ds(i * 2 + q, 1), 0:n], ff_raw[:, q:q + 1, 0:n],
                                          hid[0][:, bass.ds(i * 2 + q, 1), 0:n], ALU.subtract).then_inc(hid_ready, 1)
                        dve.wait_ge(hid_ready, tally.next("hid_ready"))
                    if mod:
                        dve_mod_columns(dve, tally, mod_bias, i * 4 + 24 * third)
                final_third = third == len(F_THIRDS) - 1
                if final_third:
                    dve_sum_start(dve, tally)
                with dve.Fori(0, 2) as i, tally.turns(i, 2, tile_used=n_tile, group=4, misc_done=n_misc,
                                                      ssq_step=4 * final_third, sq_ready=4 * final_third):
                    for q in range(4):
                        tally.passed("tile_used", int(mod))
                        if mod and q == 3:
                            dve_mod_rows(dve, tally, rows[1])
                        tally.passed("tile_used")
                        slot = tally.take("group")
                        dve.wait_ge(tile_used, tally.now("tile_used"))
                        dve_residual(dve, tally, slot, i * 4 + q, with_ctx)
                        if final_third:
                            dve_sum(dve, tally, q % 2, n)
                    if mod:
                        dve_mod_columns(dve, tally, mod_bias, i * 4 + (24 * third + 16))

        def dve_residual(dve, tally, slot, m, with_ctx):
            for v, (a, b) in enumerate(((0, NX), (NX, NT))[:2 if with_ctx else 1]):
                ins = dve.scalar_tensor_tensor(out=H[:, bass.ds(m, 1), a:b], in0=gslot(slot)[:, a:b].unsqueeze(1),
                                               scalar=hgv[:, bass.ds(m, 1), v], in1=H[:, bass.ds(m, 1), a:b],
                                               op0=ALU.mult, op1=ALU.add)
            ins.then_inc(slot_free[slot], 1)
            dve.wait_ge(slot_free[slot], tally.read("group"))


        def halves(ap, b):
            return ap.rearrange("p (n h b) -> p n h b", h=2, b=b)

        def chunks(ap):
            return ap.rearrange("p (c t) -> p c t", t=CH)

        def unit(space, u, per_direction):
            two = (space["eq"], space["lf"]), (space["ek"], space["ktok"])
            U = dict(space)
            U["lf"] = U["eq"] = two[0][u % 2]
            U["ek"], U["ktok"] = two[1][u % 2], two[1][(u + 1) % 2]
            U["dec"] = dec[:, u % 2, :]
            U["bw"] = u >= per_direction
            return U

        def chunk_order(bw):
            return (5, 4, 3, 2, 1, 0) if bw else (4, 5, 0, 1, 2, 3)

        def pe_unit_head(pe, tally, U):
            pe.wait_ge(ke_ready, tally.next("ke_ready"))
            place = tally.place("misc_done")
            pe.wait_ge(misc_free[place], tally.free("misc_done"))
            m = mslot(place)
            for c in range(ALLCH):
                last = pe.transpose(m[:, c * P:(c + 1) * P], U["ek"][:, c * CH:(c + 1) * CH], ident[:, :])
            last.then_inc(misc_done, 1)
            tally.passed("misc_done")
            return misc_free[place], tally.read("misc_done")

        def pe_unit(pe, tally, U, q, k, vt, nsub, toks, ktok_ready, ahead, head):
            nch = toks // CH
            bw = U["bw"]
            order = chunk_order(bw)
            items = [(0, j) for j in range(nsub)]
            for j in range(nsub):
                r = slice(j * HD, (j + 1) * HD) if nsub == 2 else slice(0, P)
                place = tally.place("misc_done")
                pe.wait_ge(misc_free[place], tally.free("misc_done"))
                m = mslot(place)
                for c in range(nch):
                    cc = slice(c * CH, (c + 1) * CH)
                    last = pe.matmul(m[:, cc], k[r, cc], q[r, cc], start=True, stop=True)
                last.then_inc(misc_done, 1)
                tally.passed("misc_done")
            pe.wait_ge(*ktok_ready)
            place = tally.place("misc_done")
            pe.wait_ge(misc_free[place], tally.free("misc_done"))
            m = mslot(place)
            for c in order[:5]:
                last = pe.matmul(m[:, c * P:(c + 1) * P], U["ktok"][:, c * P:(c + 1) * P], vt(c),
                                 start=True, stop=True)
            last.then_inc(misc_done, 1)
            tally.passed("misc_done")
            for li in range(len(LEVELS)):
                pe.wait_ge(z_ready, tally.next("z_ready", 2))
                Z = U["Z"][:, li % 2, :]
                for j in range(nsub):
                    r = slice(j * HD, (j + 1) * HD) if nsub == 2 else slice(0, P)
                    place = tally.place("misc_done")
                    pe.wait_ge(misc_free[place], tally.free("misc_done"))
                    m = mslot(place)
                    for c in range(nch):
                        cc = slice(c * CH, (c + 1) * CH)
                        last = pe.matmul(m[:, cc], Z[r, cc], Z[r, cc], start=True, stop=True)
                    last.then_inc(misc_done, 1)
                    tally.passed("misc_done")
                ahead(li)
            place, pairs_read = tally.place("misc_done", 1), tally.read("misc_done")
            ktok_next = head()
            pe.wait_ge(misc_free[place], pairs_read)
            place = tally.place("misc_done")
            pe.wait_ge(misc_free[place], tally.free("misc_done"))
            m = mslot(place)
            for c in range(nch):
                cc = slice(c * CH, (c + 1) * CH)
                at_order = order.index(c)
                for j in range(nsub):
                    f = slice(j * HD, (j + 1) * HD) if nsub == 2 else slice(0, P)
                    last = pe.matmul(m[f, cc], vt(c)[:, f], U["P"][:, j, cc], start=True, stop=False,
                                     skip_group_check=True)
                    if at_order > 0:
                        last = pe.matmul(m[f, cc], U["S"][:, at_order, f], U["eq"][:, cc], start=False, stop=True,
                                         skip_group_check=True)
            last.then_inc(misc_done, 1)
            tally.passed("misc_done")
            return ktok_next

        def act_decays(act, tally, U, scale):
            end = 0 if U["bw"] else CH - 1
            act.wait_ge(decay_in, tally.next("decay_in"))
            act.activation(U["eq"][:, :], U["cum"][:, :], ACT.Exp, scale=scale).then_inc(act_step, 1)
            act.wait_ge(act_step, tally.next("act_step"))
            act.activation(U["ek"][:, :], U["ek"][:, :], ACT.Exp, scale=scale).then_inc(act_step, 1)
            act.wait_ge(act_step, tally.next("act_step"))
            act.activation(U["dec"][:, 0:ALLCH], chunks(U["cum"][:, :])[:, :, end], ACT.Exp, scale=scale
                ).then_inc(decay_ready, 1)
            act.wait_ge(decay_ready, tally.next("decay_ready"))

        def act_level(act, tally, U, li, toks, scale):
            act.wait_ge(ex_in, tally.next("ex_in", 2))
            x = U["ex"][:, li % 2, 0:toks]
            act.activation(x, x, ACT.Exp, scale=scale).then_inc(ex_out, 1)
            act.wait_ge(ex_out, tally.next("ex_out"))

        def act_unit_head(act, tally, U, toks, scale):
            act_decays(act, tally, U, scale)
            act_level(act, tally, U, 0, toks, scale)
            ms = tally.take("misc_done")
            act.wait_ge(misc_done, tally.now("misc_done"))
            act.activation(U["ktok"][:, :], mslot(ms)[:, 0:NT], ACT.Copy).then_inc(misc_free[ms], 1)
            act.wait_ge(misc_free[ms], tally.read("misc_done"))

        def act_unit(act, tally, U, nsub, toks, scale, ahead):
            tally.passed("misc_done", nsub + 1)
            for li in range(len(LEVELS)):
                if li:
                    act_level(act, tally, U, li, toks, scale)
                tally.passed("misc_done", nsub)
                ahead(li)
            tally.passed("misc_done")

        def dve_cum(dve, tally, U):
            bw = U["bw"]
            cum, lf = U["cum"][:, :], U["lf"][:, :]
            if not bw:
                dve.tensor_tensor_scan(cum, reset[:, :], lf, 0.0, ALU.mult, ALU.add).then_inc(dve_step, 1)
                dve.wait_ge(dve_step, tally.next("dve_step"))
                last = chunks(cum)[:, :, CH - 1:CH].broadcast_to([P, ALLCH, CH])
                dve.tensor_tensor(chunks(U["ek"][:, :]), last, chunks(cum), ALU.subtract).then_inc(decay_in, 1)
                dve.wait_ge(decay_in, tally.next("decay_in"))
            else:
                fwd = U["ktok"][:, :]
                dve.tensor_tensor_scan(fwd, reset[:, :], lf, 0.0, ALU.mult, ALU.add).then_inc(dve_step, 1)
                dve.wait_ge(dve_step, tally.next("dve_step"))
                dve.tensor_tensor(U["ek"][:, :], fwd, lf, ALU.subtract).then_inc(dve_step, 1)
                dve.wait_ge(dve_step, tally.next("dve_step"))
                total = chunks(fwd)[:, :, CH - 1:CH].broadcast_to([P, ALLCH, CH])
                dve.tensor_tensor(chunks(cum), total, chunks(U["ek"][:, :]), ALU.subtract).then_inc(decay_in, 1)
                dve.wait_ge(decay_in, tally.next("decay_in"))

        def dve_seam(dve, tally, U, li, toks):
            b = LEVELS[li]
            x = halves(U["ex"][:, li % 2, 0:toks], b)
            cum = halves(U["cum"][:, 0:toks], b)
            n = toks // (2 * b)
            a = cum[:, :, 1, 0:1] if U["bw"] else cum[:, :, 0, b - 1:b]
            a = a.broadcast_to([P, n, b])
            first, second = cum[:, :, 0, :], cum[:, :, 1, :]
            if U["bw"]:
                upper, lower = (first, a), (a, second)
            else:
                upper, lower = (a, first), (second, a)
            dve.tensor_tensor(x[:, :, 0, :], *upper, ALU.subtract).then_inc(ex_in, 1)
            dve.tensor_tensor(x[:, :, 1, :], *lower, ALU.subtract).then_inc(ex_in, 1)
            tally.passed("ex_in", 2)

        def dve_unit_head(dve, tally, U, q, k, toks):
            dve_seam(dve, tally, U, 0, toks)
            dve.wait_ge(decay_ready, tally.next("decay_ready"))
            dve.tensor_tensor(U["ek"][:, :], U["ek"][:, :], k[:, :], ALU.mult).then_inc(ke_ready, 1)
            dve.wait_ge(ke_ready, tally.next("ke_ready"))
            dve.tensor_tensor(U["eq"][:, 0:toks], U["eq"][:, 0:toks], q[:, 0:toks], ALU.mult).then_inc(dve_step, 1)
            dve.wait_ge(dve_step, tally.next("dve_step"))

        def dve_unit(dve, tally, U, q, k, nsub, toks, oacc, ahead, head):
            bw = U["bw"]
            d = 1 if bw else 0
            nch = toks // CH
            order = chunk_order(bw)

            def make_z(li):
                b = LEVELS[li]
                dve.wait_ge(ex_out, tally.next("ex_out"))
                x, z = halves(U["ex"][:, li % 2, 0:toks], b), halves(U["Z"][:, li % 2, 0:toks], b)
                qh, kh = halves(q[:, 0:toks], b), halves(k[:, 0:toks], b)
                left, right = (qh, kh) if bw else (kh, qh)
                dve.tensor_tensor(z[:, :, 0, :], x[:, :, 0, :], left[:, :, 0, :], ALU.mult).then_inc(z_ready, 1)
                dve.tensor_tensor(z[:, :, 1, :], x[:, :, 1, :], right[:, :, 1, :], ALU.mult).then_inc(z_ready, 1)
                tally.passed("z_ready", 2)

            def put(li):
                for j in range(nsub):
                    ms = tally.take("misc_done")
                    dve.wait_ge(misc_done, tally.now("misc_done"))
                    mk = masks[:, d, li, :].unsqueeze(1).broadcast_to([P, nch, CH])
                    dve.copy_predicated(chunks(U["P"][:, j, 0:toks]), mk, chunks(mslot(ms)[:, 0:toks])
                        ).then_inc(misc_free[ms], 1)
                    dve.wait_ge(misc_free[ms], tally.read("misc_done"))

            for j in range(nsub):
                ms = tally.take("misc_done")
                dve.wait_ge(misc_done, tally.now("misc_done"))
                dve.tensor_tensor(chunks(U["P"][:, j, 0:toks]), chunks(mslot(ms)[:, 0:toks]),
                                  ident[:, :].unsqueeze(1).broadcast_to([P, nch, CH]), ALU.mult
                                                ).then_inc(misc_free[ms], 1)
                dve.wait_ge(misc_free[ms], tally.read("misc_done"))
            make_z(0)
            dve_seam(dve, tally, U, 1, toks)
            ms = tally.take("misc_done")
            dve.wait_ge(misc_done, tally.now("misc_done"))
            add = mslot(ms)
            for n_, c in enumerate(order[:5]):
                src = add[:, c * P:(c + 1) * P]
                if nsub == 2:
                    src = U["Z"][:, 1, c * P:(c + 1) * P]
                    dve.tensor_tensor(src, add[:, c * P:(c + 1) * P], blk[:, :], ALU.mult).then_inc(dve_step, 1)
                    dve.wait_ge(dve_step, tally.next("dve_step"))
                dst = U["S"][:, n_ + 1, :]
                if n_ == 0:
                    ins = dve.tensor_copy(dst, src)
                else:
                    ins = dve.scalar_tensor_tensor(out=dst, in0=U["S"][:, n_, :], scalar=U["dec"][:, c:c + 1], in1=src,
                                                   op0=ALU.mult, op1=ALU.add)
                if n_ < 4:
                    ins.then_inc(dve_step, 1)
                    dve.wait_ge(dve_step, tally.next("dve_step"))
                else:
                    ins.then_inc(misc_free[ms], 1)
                    dve.wait_ge(misc_free[ms], tally.read("misc_done"))
            nl = len(LEVELS)
            for li in range(1, nl):
                make_z(li)
                if li + 1 < nl:
                    dve_seam(dve, tally, U, li + 1, toks)
                ahead(li)
                put(li - 1)
            if head is not None:
                head()
            put(nl - 1)
            if head is not None:
                tally.take("misc_done")
            ms = tally.take("misc_done")
            dve.wait_ge(misc_done, tally.now("misc_done"))
            if not bw:
                ins = dve.tensor_copy(oacc, mslot(ms)[:, 0:toks])
            else:
                ins = dve.tensor_tensor(oacc, mslot(ms)[:, 0:toks], oacc, ALU.add)
            ins.then_inc(misc_free[ms], 1)
            dve.wait_ge(misc_free[ms], tally.read("misc_done"))


        def pe_head_norm(pe, tally, count, n, groups, columns, squares, between):
            pe.wait_ge(nsq_ready, tally.next("nsq_ready", count))
            pe_token_sums(pe, tally, [(squares[:, h, :], n) for h in range(count)], columns)
            between()
            pe.wait_ge(inv_ready, tally.next("inv_ready"))
            for h in range(count):
                pe_spread(pe, tally, h * n // P, n, groups)

        def act_head_norm(act, tally, count, n, squares, oacc, gates, out_pair, first, before, between):
            act.wait_ge(misc_free[tally.place("misc_done", 1)], tally.read("misc_done"))
            for h in range(count):
                act.activation(squares[:, h, 0:n], oacc[:, h, 0:n], ACT.Square).then_inc(nsq_ready, 1)
                act.wait_ge(nsq_ready, tally.next("nsq_ready"))
            before()
            act_root(act, tally, 2 * count * n // P)
            between()
            for h in range(count):
                ms = tally.take("misc_done")
                act.wait_ge(misc_free[ms], tally.read("misc_done"))
                act.activation(out_pair[0][:, first + h, 0:n], gates[:, h, 0:n], ACT.Copy).then_inc(ohi_ready, 1)
                act.wait_ge(ohi_ready, tally.next("ohi_ready"))

        def dve_head_norm(dve, tally, count, n, width, oacc, gates, w, out_pair, first, gates_ready):
            dve_inverse(dve, tally, 2 * count * n // P, width)
            gates_ready()
            for h in range(count):
                dve.scalar_tensor_tensor(out=gates[:, h, 0:n], in0=oacc[:, h, 0:n], scalar=w, in1=gates[:, h, 0:n],
                                         op0=ALU.mult, op1=ALU.mult).then_inc(dve_step, 1)
                dve.wait_ge(dve_step, tally.next("dve_step"))

            def low(h):
                dve.wait_ge(ohi_ready, tally.next("ohi_ready"))
                dve.tensor_tensor(out_pair[1][:, first + h, 0:n], gates[:, h, 0:n], out_pair[0][:, first + h, 0:n],
                                  ALU.subtract).then_inc(mix_ready, 1)
                dve.wait_ge(mix_ready, tally.next("mix_ready"))

            for h in range(count):
                ms = tally.take("misc_done")
                dve.wait_ge(misc_done, tally.now("misc_done"))
                dve.tensor_tensor(gates[:, h, 0:n], gates[:, h, 0:n], mslot(ms)[:, 0:n], ALU.mult
                    ).then_inc(misc_free[ms], 1)
                dve.wait_ge(misc_free[ms], tally.read("misc_done"))
                if h:
                    low(h - 1)
            low(count - 1)



        def pe_mod_group(pe, tally):
            rows_place = pe_mod_place(pe, tally)
            for kk in range(4):
                pe_mod_tile(pe, tally, rows_place, kk)
            tally.passed("misc_done")
            pe_mod_columns(pe, tally, rows[0])

        def pe_filters(pe, tally):
            place = tally.place("misc_done")
            pe.wait_ge(misc_free[place], tally.free("misc_done"))
            m = mslot(place)
            for h in range(2):
                last = pe.matmul(m[0:64, h * NX:(h + 1) * NX], fw1[:, :], fz[:, h * NX:(h + 1) * NX],
                                 start=True, stop=True)
            last.then_inc(misc_done, 1)
            tally.passed("misc_done")
            pe.wait_ge(c_ready, tally.next("c_ready"))
            pe_mod_group(pe, tally)
            pe.wait_ge(sin_ready, tally.next("sin_ready"))
            place = tally.place("misc_done")
            pe.wait_ge(misc_free[place], tally.free("misc_done"))
            m = mslot(place)
            for h in range(2):
                last = pe.matmul(m[0:64, h * NX:(h + 1) * NX], fw2[:, :], fh[:, 0, h * NX:(h + 1) * NX],
                                 start=True, stop=True)
            last.then_inc(misc_done, 1)
            tally.passed("misc_done")
            pe_mod_group(pe, tally)
            pe.wait_ge(sin_ready, tally.next("sin_ready"))
            for o in range(2):
                norm = tally.take("group")
                pe.wait_ge(slot_free[norm], tally.free("group", 1))
                for t in range(5):
                    if t < 4:
                        place = tally.place("misc_done")
                        pe.wait_ge(misc_free[place], tally.free("misc_done"))
                        m = mslot(place)
                        for h in range(2):
                            last = pe.matmul(m[:, h * NX:(h + 1) * NX], fh[:, 1, h * NX + t * P:h * NX + (t + 1) * P],
                                             fw3[:, 2 * o + h, :], start=True, stop=True)
                        last.then_inc(misc_done, 1)
                        tally.passed("misc_done")
                    if t:
                        pe.wait_ge(abs_ready, tally.next("abs_ready"))
                        for h in range(2):
                            last = pe.matmul(gslot(norm)[:, 0:NX], ones[:, :], fabs[:, (t - 1) % 2, h, :],
                                             start=(t == 1 and h == 0), stop=(t == 4 and h == 1))
                        last.then_inc(abs_summed, 1)
                        tally.passed("abs_summed")
                pe.wait_ge(e_ready, tally.next("e_ready", 4))
                pe.wait_ge(second_landed, 16 * len(second))
                for c in range(NFREQ):
                    src = fe if c % 4 < 2 else fd
                    rows_place = pe_mod_place(pe, tally)
                    tally.passed("misc_done")
                    place = tally.place("misc_done")
                    pe.wait_ge(misc_free[place], tally.free("misc_done"))
                    m = mslot(place)
                    for t in range(4):
                        pe_mod_tile(pe, tally, rows_place, t)
                        last = pe.matmul(m[:, 0:NX], dft0[:, t, c * P:(c + 1) * P], src[:, t, :],
                                         start=(t == 0), stop=(t == 3))
                    last.then_inc(misc_done, 1)
                    tally.passed("misc_done")
                    pe_mod_columns(pe, tally, rows[0], 2)

        def act_filters(act, tally):
            act_mod_input(act, tally, "cvec")
            for layer in range(2):
                tally.take("misc_done")
                act_mod_tiles(act, tally, 4)
                tally.take("misc_done")
                tally.take("misc_done")
                act.wait_ge(arg_ready, tally.next("arg_ready"))
                act.activation(fh[:, layer, :], fh[:, layer, :], ACT.Sin).then_inc(sin_ready, 1)
                act.wait_ge(sin_ready, tally.next("sin_ready"))
            for dst, src in third:
                act.dma_start(dst, src).then_inc(third_landed, 16)
            for o in range(2):
                tally.take("group")
                for t in range(4):
                    tally.take("misc_done")
                    if t >= 2 or o:
                        act.wait_ge(abs_summed, tally.next("abs_summed"))
                    act.wait_ge(misc_free[tally.place("misc_done", 1)], tally.read("misc_done"))
                    act.activation(fabs[:, t % 2, :, :], fa[:, t % 2, :, :], ACT.Abs).then_inc(abs_ready, 1)
                    act.wait_ge(abs_ready, tally.next("abs_ready"))
                for c in range(NFREQ):
                    act_mod_tiles(act, tally, 4)
                    tally.take("misc_done")
                    tally.take("misc_done")
                    act.wait_ge(misc_free[tally.place("misc_done", 1)], tally.read("misc_done"))
                    tally.take("misc_done")
                    st = fst[:, c % 4, :]
                    n = tally.n.setdefault(f"k_stored{c % 4}", 0)

                    def store(dst, src):
                        act.dma_start(dst, src).then_inc(k_stored[c % 4], 16)
                        tally.n[f"k_stored{c % 4}"] += 16

                    if c == 0:
                        store(kdram[2 * 0 + o, :, :], st)
                        store(kdram[2 * 8 + o, 1:P, :], st[1:P, :])
                    elif c == 4:
                        store(kdram[2 * 4 + o, 1:P, :], st[1:P, :])
                        store(kdram[2 * 4 + o, 0:1, :], fzero[0:1, :])
                        store(kdram[2 * 8 + o, 0:1, :], st[0:1, :])
                    else:
                        store(kdram[2 * c + o, :, :], st)

        def dve_filters(dve, tally):
            dve.memset(fzero[0:1, :], 0.0).then_inc(dve_step, 1)
            dve.wait_ge(dve_step, tally.next("dve_step"))
            hy0, bias = VEC_AT["hyv"][0], VEC_AT["mod_b"][0]
            dve_mod_input(dve, tally)
            for layer in range(2):
                x = fh[:, layer, :]
                ms = tally.take("misc_done")
                dve.wait_ge(misc_done, tally.now("misc_done"))
                ins = dve.tensor_scalar(x, mslot(ms)[0:64, 0:2 * NX], vecs[0:64, hy0 + 2 * layer:hy0 + 2 * layer + 1],
                                        vecs[0:64, hy0 + 2 * layer + 1:hy0 + 2 * layer + 2], ALU.add, ALU.mult)
                ins.then_inc(misc_free[ms], 1)
                dve.wait_ge(misc_free[ms], tally.read("misc_done"))
                dve.wait_ge(misc_free[tally.place("misc_done", 1)], tally.read("misc_done"))
                dve.tensor_scalar(fk[:, :], x, 1.0 / (2 * np.pi), MAGIC, ALU.mult, ALU.add).then_inc(dve_step, 1)
                dve.wait_ge(dve_step, tally.next("dve_step"))
                dve.tensor_scalar(fk[:, :], fk[:, :], MAGIC, None, ALU.subtract).then_inc(dve_step, 1)
                dve.wait_ge(dve_step, tally.next("dve_step"))
                for part in (TWO_PI_HI, 2 * np.pi - TWO_PI_HI):
                    dve.scalar_tensor_tensor(out=x, in0=fk[:, :], scalar=-float(part), in1=x,
                                             op0=ALU.mult, op1=ALU.add).then_inc(dve_step, 1)
                    dve.wait_ge(dve_step, tally.next("dve_step"))
                dve.tensor_scalar(x, x, PI_F, -PI_F, ALU.min, ALU.max).then_inc(arg_ready, 1)
                dve.wait_ge(arg_ready, tally.next("arg_ready"))
                tally.passed("tile_used", 4)
                dve_mod_rows(dve, tally, rows[0])
                dve_mod_columns(dve, tally, bias, 4 * layer)
            dve.wait_ge(second_landed, 16 * len(second))
            for o in range(2):
                norm = tally.take("group")
                for t in range(5):
                    if t < 4:
                        ms = tally.take("misc_done")
                        dve.wait_ge(misc_done, tally.now("misc_done"))
                        dve.tensor_tensor(fa[:, t % 2, 0, :], mslot(ms)[:, 0:NX], fwin[:, 0, t, :],
                                          ALU.mult).then_inc(dve_step, 1)
                        dve.wait_ge(dve_step, tally.next("dve_step"))
                        dve.tensor_tensor(fa[:, t % 2, 1, :], mslot(ms)[:, NX:2 * NX], fwin[:, 1, t, :],
                                          ALU.mult).then_inc(misc_free[ms], 1)
                        dve.wait_ge(misc_free[ms], tally.read("misc_done"))
                    if t:
                        dve.wait_ge(abs_ready, tally.next("abs_ready"))
                        dve.tensor_tensor(fe[:, t - 1, :], fa[:, (t - 1) % 2, 0, :],
                                          fa[:, (t - 1) % 2, 1, :], ALU.add).then_inc(dve_step, 1)
                        dve.wait_ge(dve_step, tally.next("dve_step"))
                        dve.tensor_tensor(fd[:, t - 1, :], fa[:, (t - 1) % 2, 0, :],
                                          fa[:, (t - 1) % 2, 1, :], ALU.subtract).then_inc(e_ready, 1)
                        dve.wait_ge(e_ready, tally.next("e_ready"))
                dve.wait_ge(abs_summed, tally.next("abs_summed", 4))
                dve.tensor_scalar(fnorm[:, :], gslot(norm)[:, 0:NX], 1e-6, None, ALU.add).then_inc(slot_free[norm], 1)
                dve.wait_ge(slot_free[norm], tally.read("group"))
                dve.wait_ge(slot_free[tally.place("group", 1)], tally.read("group", 1))
                dve.reciprocal(fnorm[:, :], fnorm[:, :]).then_inc(dve_step, 1)
                dve.wait_ge(dve_step, tally.next("dve_step"))
                for c in range(NFREQ):
                    tally.passed("tile_used", 4)
                    dve_mod_rows(dve, tally, rows[0])
                    ms = tally.take("misc_done")
                    dve.wait_ge(misc_done, tally.now("misc_done"))
                    stored = K_STORES[c % 4]
                    times = o * 2 + (c >= 4)
                    want = 16 * (sum(stored) * (times // 2) + (stored[0] if times % 2 else 0))
                    if want:
                        dve.wait_ge(k_stored[c % 4], want)
                    dve.tensor_tensor(fst[:, c % 4, :], mslot(ms)[:, 0:NX], fnorm[:, :], ALU.mult
                        ).then_inc(misc_free[ms], 1)
                    dve.wait_ge(misc_free[ms], tally.read("misc_done"))
                    dve_mod_columns(dve, tally, bias, 4 * (2 + o * NFREQ + c))


        def pe_values(pe, tally, count, vt, order=None):
            for h in range(count + 1):
                if h < count:
                    pe_x_tiles(pe, tally, 1, True, order if h == 0 else None)
                if h:
                    back = 2 if h < count else 1
                    pe.wait_ge(slot_free[tally.place("group", back)], tally.read("group", back))
                    place = tally.place("misc_done")
                    pe.wait_ge(misc_free[place], tally.free("misc_done"))
                    m = mslot(place)
                    for c in range(ALLCH):
                        last = pe.transpose(m[:, c * P:(c + 1) * P], vt[:, (h - 1) % 2, c * P:(c + 1) * P],
                                            ident[:, :])
                    last.then_inc(misc_done, 1)
                    tally.passed("misc_done")

        def act_values(act, tally, count, vt):
            m0 = tally.n.get("misc_done", 0)
            for h in range(count):
                if h >= 2:
                    act.wait_ge(misc_free[(m0 + h - 2) % 2], (m0 + h - 2) // 2 + 2)
                act_proj(act, tally, vt[:, h % 2, :], NT)
            tally.passed("misc_done", count)

        def dve_values(dve, tally, count, vtok):
            skip_tiles(tally, count)
            for h in range(count):
                ms = tally.take("misc_done")
                dve.wait_ge(misc_done, tally.now("misc_done"))
                dve.tensor_copy(vtok[:, :, h * P:(h + 1) * P],
                                mslot(ms)[:, 0:NT].rearrange("p (c f) -> p c f", f=P)).then_inc(misc_free[ms], 1)
                dve.wait_ge(misc_free[ms], tally.read("misc_done"))

        def pe_hgrn(pe, tally):
            x_before = tally.n["x_ready"]
            tally.passed("x_ready", KC)
            pe_values(pe, tally, 4, vt1, (x_ready, x_before))
            pe_x_tiles(pe, tally, 4, False)
            pe_x_tiles(pe, tally, 2, True)
            ktok_ready = pe_unit_head(pe, tally, unit(u1, 0, 4))
            for u in range(8):
                h = u % 4

                def ahead(li, nxt=u + 1):
                    if nxt < 7:
                        pe_x_part(pe, tally, li, li + 1 if li < 6 else KC)

                def head(nxt=u + 1):
                    return pe_unit_head(pe, tally, unit(u1, nxt, 4)) if nxt < 8 else None

                ktok_ready = pe_unit(pe, tally, unit(u1, u, 4), q1[:, h, :], k1[u % 2][:, :],
                                     lambda c, h=h: vtok1[:, c, h * P:(h + 1) * P], 1, NX, ktok_ready, ahead, head)
            pe_x_tiles(pe, tally, 1, False)
            pe_head_norm(pe, tally, 4, NX, 1, ones[:, 0:2], hsq1, lambda: pe_x_tiles(pe, tally, 3, False))

        def act_gates(act, tally, heads):
            for h in heads:
                act_proj(act, tally, g1s[:, h, :], NX, ACT.Silu)

        def act_forget(act, tally, u):
            tally.passed("tile_used")
            slot = tally.take("group")
            act.wait_ge(tile_used, tally.now("tile_used"))
            act.activation(unit(u1, u, 4)["lf"][:, :], gslot(slot)[:, 0:NT], ACT.Sigmoid).then_inc(slot_free[slot], 1)
            act.wait_ge(slot_free[slot], tally.read("group"))

        def act_log_forget(act, tally, u):
            lf = unit(u1, u, 4)["lf"][:, :]
            act.wait_ge(f_ready, tally.next("f_ready"))
            act.activation(lf, lf, ACT.Ln).then_inc(lf_ready, 1)
            act.wait_ge(lf_ready, tally.next("lf_ready"))

        def act_hgrn(act, tally):
            act.wait_ge(lb_in, tally.next("lb_in"))
            act.dma_start(masks32[:, :, :, :], ins["masks"]).then_inc(masks_landed, 16)
            act_values(act, tally, 4, vt1)
            for h in range(4):
                act_proj(act, tally, q1[:, h, :], NX, ACT.Silu)
            act.activation(lb[:, 0:2, :], lb[:, 0:2, :], ACT.Exp).then_inc(lb_exp, 1)
            act.wait_ge(lb_exp, tally.next("lb_exp"))
            act_forget(act, tally, 0)
            split_tile(act, tally)
            act_log_forget(act, tally, 0)
            act_unit_head(act, tally, unit(u1, 0, 4), NX, 1.0)
            for u in range(8):
                def ahead(li, nxt=u + 1):
                    if nxt < 8 and li == 1:
                        act_forget(act, tally, nxt)
                    elif nxt < 8 and li == 2:
                        split_tile(act, tally)
                    elif nxt < 8 and li == 4:
                        act_log_forget(act, tally, nxt)
                    elif nxt < 8 and li == 6:
                        act_unit_head(act, tally, unit(u1, nxt, 4), NX, 1.0)

                act_unit(act, tally, unit(u1, u, 4), 1, NX, 1.0, ahead)
            act.wait_ge(misc_free[tally.place("misc_done", 1)], tally.read("misc_done"))
            act.dma_start(dft[:, :, :], ins["dft"]).then_inc(dft_landed, 16)
            act.dma_start(idft[:, :, :], ins["idft"]).then_inc(dft_landed, 16)
            act_head_norm(act, tally, 4, NX, hsq1, oacc1, g1s, oab, 0,
                          lambda: act_gates(act, tally, range(1)), lambda: act_gates(act, tally, range(1, 4)))

        def dve_forget(dve, tally, u):
            skip_tiles(tally, 1)
            f = unit(u1, u, 4)["lf"][:, :]
            dve.wait_ge(slot_free[tally.place("group", 1)], tally.read("group"))
            dve.tensor_scalar(f, f, lb[:, 3, u:u + 1], lb[:, 2, u:u + 1], ALU.mult, ALU.add).then_inc(dve_step, 1)
            dve.wait_ge(dve_step, tally.next("dve_step"))
            dve.tensor_scalar(k1[u % 2][:, :], f, -1.0, 1.0, ALU.mult, ALU.add).then_inc(f_ready, 1)
            dve.wait_ge(f_ready, tally.next("f_ready"))

        def dve_hgrn(dve, tally):
            a = vec("lbl", 0, 8)
            b = vec("lbl", 8, 8)
            dve.tensor_tensor(lb[:, 2, :], a, b, ALU.max).then_inc(dve_step, 1)
            dve.wait_ge(dve_step, tally.next("dve_step"))
            dve.tensor_tensor(lb[:, 0, :], a, lb[:, 2, :], ALU.subtract).then_inc(dve_step, 1)
            dve.wait_ge(dve_step, tally.next("dve_step"))
            dve.tensor_tensor(lb[:, 1, :], b, lb[:, 2, :], ALU.subtract).then_inc(lb_in, 1)
            dve.wait_ge(lb_in, tally.next("lb_in"))
            dve.wait_ge(masks_landed, 16)
            dve.tensor_copy(masks[:, :, :, :], masks32[:, :, :, :]).then_inc(dve_step, 1)
            dve.wait_ge(dve_step, tally.next("dve_step"))
            dve_values(dve, tally, 4, vtok1)
            skip_tiles(tally, 4)
            dve.wait_ge(lb_exp, tally.next("lb_exp"))
            dve.tensor_tensor(lb[:, 1, :], lb[:, 0, :], lb[:, 1, :], ALU.add).then_inc(dve_step, 1)
            dve.wait_ge(dve_step, tally.next("dve_step"))
            dve.reciprocal(lb[:, 1, :], lb[:, 1, :]).then_inc(dve_step, 1)
            dve.wait_ge(dve_step, tally.next("dve_step"))
            dve.tensor_tensor(lb[:, 2, :], lb[:, 0, :], lb[:, 1, :], ALU.mult).then_inc(dve_step, 1)
            dve.wait_ge(dve_step, tally.next("dve_step"))
            dve.tensor_scalar(lb[:, 3, :], lb[:, 2, :], -1.0, 1.0, ALU.mult, ALU.add).then_inc(dve_step, 1)
            dve.wait_ge(dve_step, tally.next("dve_step"))
            dve_forget(dve, tally, 0)
            dve.wait_ge(lf_ready, tally.next("lf_ready"))
            dve_cum(dve, tally, unit(u1, 0, 4))
            dve_unit_head(dve, tally, unit(u1, 0, 4), q1[:, 0, :], k1[0], NX)
            tally.take("misc_done")
            for u in range(8):
                def ahead(li, nxt=u + 1):
                    if nxt < 8 and li == 2:
                        dve_forget(dve, tally, nxt)
                    elif nxt < 8 and li == 6:
                        dve.wait_ge(lf_ready, tally.next("lf_ready"))
                        dve_cum(dve, tally, unit(u1, nxt, 4))

                def head(nxt=u + 1):
                    dve_unit_head(dve, tally, unit(u1, nxt, 4), q1[:, nxt % 4, :], k1[nxt % 2], NX)

                dve_unit(dve, tally, unit(u1, u, 4), q1[:, u % 4, :], k1[u % 2][:, :], 1, NX, oacc1[:, u % 4, :],
                         ahead, head if u < 7 else None)

            def gates_ready():
                skip_tiles(tally, 4)
                for back in (1, 2):
                    dve.wait_ge(slot_free[tally.place("group", back)], tally.read("group", back))

            dve_head_norm(dve, tally, 4, NX, P, oacc1, g1s, vec("hgrn_w"), oab, 0, gates_ready)


        def pe_hyena(pe, tally):
            pe.wait_ge(dft_landed, 32)
            pe_x_tiles(pe, tally, 3, False)
            for g in range(4):
                for o in range(2):
                    pe.wait_ge(hv_ready, tally.next("hv_ready"))
                    place = tally.place("misc_done")
                    pe.wait_ge(misc_free[place], tally.free("misc_done"))
                    m = mslot(place)
                    for t in range(4):
                        last = pe.transpose(m[:, t * P:(t + 1) * P], hv[:, 0, t * P:(t + 1) * P], ident[:, :])
                    last.then_inc(misc_done, 1)
                    tally.passed("misc_done")
                    pe.wait_ge(misc_free[tally.place("misc_done", 1)], tally.read("misc_done"))
                    place = tally.place("misc_done")
                    pe.wait_ge(misc_free[place], tally.free("misc_done"))
                    m = mslot(place)
                    for c in range(NFREQ):
                        for t in range(4):
                            last = pe.matmul(m[:, c * P:(c + 1) * P], dft[:, t, c * P:(c + 1) * P], hu[:, t, :],
                                             start=(t == 0), stop=(t == 3))
                    last.then_inc(misc_done, 1)
                    tally.passed("misc_done")
                    if g < 3:
                        pe_x_tiles(pe, tally, 1, False)
                    pe.wait_ge(freq_ready, tally.next("freq_ready"))
                    place = tally.place("misc_done")
                    pe.wait_ge(misc_free[place], tally.free("misc_done"))
                    m = mslot(place)
                    for c in range(NFREQ):
                        last = pe.matmul(m[:, 0:NX], hY[:, c, :], idft[:, c, :], start=(c == 0),
                                         stop=(c == NFREQ - 1))
                    last.then_inc(misc_done, 1)
                    tally.passed("misc_done")
                    if g < 3 and o == 0:
                        pe_x_tiles(pe, tally, 1, False)

        def act_hyena(act, tally):
            for s in range(4):
                act.wait_ge(k_stored[s], 2 * 16 * sum(K_STORES[s]))
            act.wait_ge(edge_ready, 1)
            for j in range(3):
                act_proj(act, tally, hp[:, j, 1:513], NX)
            for g in range(4):
                act.dma_start(hK[:, :, :, :].rearrange("p c o f -> p (c o) f"),
                              kdram[:, :, g * P:(g + 1) * P].rearrange("q p f -> p q f")).then_inc(k_landed, 16)
                for j in range(3 if g < 3 else 0):
                    if j == 0:
                        act.wait_ge(conv_done, tally.next("conv_done"))
                    act_proj(act, tally, hp[:, j, 1:513], NX)
                tally.passed("misc_done", 6)
                act.wait_ge(z_done, tally.next("z_done"))
                act.activation(oab[0][:, 4 + g, :], hv[:, 0, :], ACT.Copy).then_inc(ohi_ready, 1)
                act.wait_ge(ohi_ready, tally.next("ohi_ready"))

        def dve_hyena(dve, tally):
            def conv(g, j):
                c = 4 * j + g
                dve.tensor_scalar(hv[:, j, :], hp[:, j, 0:NX], vec("conv_w", c), vec("conv_b", c), ALU.mult, ALU.add
                    ).then_inc(dve_step, 1)
                dve.wait_ge(dve_step, tally.next("dve_step"))
                for tap in (1, 2):
                    dve.scalar_tensor_tensor(out=hv[:, j, :], in0=hp[:, j, tap:tap + NX],
                                             scalar=vec("conv_w", 12 * tap + c), in1=hv[:, j, :],
                                             op0=ALU.mult, op1=ALU.add).then_inc(dve_step, 1)
                    dve.wait_ge(dve_step, tally.next("dve_step"))

            dve.memset(hp[:, :, 0:514:513], 0.0).then_inc(edge_ready, 1)
            dve.wait_ge(edge_ready, 1)
            for g in range(4):
                skip_tiles(tally, 3)
                dve.wait_ge(slot_free[tally.place("group", 1)], tally.read("group"))
                conv(g, 0)
                dve.tensor_copy(small[:, 60:61], vec("final_w")).then_inc(hv_ready, 1)
                dve.wait_ge(hv_ready, tally.next("hv_ready"))
                for o in range(2):
                    ms = tally.take("misc_done")
                    dve.wait_ge(misc_done, tally.now("misc_done"))
                    dve.tensor_copy(hu[:, :, :], mslot(ms)[:, 0:NX].rearrange("p (t f) -> p t f", f=P)
                        ).then_inc(misc_free[ms], 1)
                    dve.wait_ge(misc_free[ms], tally.read("misc_done"))
                    if o == 0:
                        conv(g, 1)
                        conv(g, 2)
                        if g < 3:
                            dve.memset(small[:, 61:62], 0.0).then_inc(conv_done, 1)
                            dve.wait_ge(conv_done, tally.next("conv_done"))
                        dve.wait_ge(k_landed, 16 * (g + 1))
                    ms = tally.take("misc_done")
                    dve.wait_ge(misc_done, tally.now("misc_done"))
                    Uf = mslot(ms).rearrange("p (c f) -> p c f", f=P)
                    K = hK[:, :, o, :]
                    dve.tensor_tensor(hY[:, 0:4, :], Uf[:, 0:4, :], K[:, 0:4, :], ALU.mult).then_inc(dve_step, 1)
                    dve.wait_ge(dve_step, tally.next("dve_step"))
                    dve.tensor_tensor(hY[:, 4:8, :], Uf[:, 0:4, :], K[:, 4:8, :], ALU.mult).then_inc(dve_step, 1)
                    dve.wait_ge(dve_step, tally.next("dve_step"))
                    dve.tensor_tensor(K[:, 4:8, :], Uf[:, 4:8, :], K[:, 4:8, :], ALU.mult).then_inc(dve_step, 1)
                    dve.wait_ge(dve_step, tally.next("dve_step"))
                    dve.tensor_tensor(K[:, 1:4, :], Uf[:, 5:8, :], K[:, 1:4, :], ALU.mult).then_inc(dve_step, 1)
                    dve.wait_ge(dve_step, tally.next("dve_step"))
                    dve.tensor_tensor(K[:, 8, :], Uf[:, 4, :], K[:, 8, :], ALU.mult).then_inc(misc_free[ms], 1)
                    dve.wait_ge(misc_free[ms], tally.read("misc_done"))
                    dve.wait_ge(misc_free[tally.place("misc_done", 1)], tally.read("misc_done"))
                    dve.tensor_tensor(hY[:, 0:4, :], hY[:, 0:4, :], K[:, 4:8, :], ALU.subtract).then_inc(dve_step, 1)
                    dve.wait_ge(dve_step, tally.next("dve_step"))
                    dve.tensor_tensor(hY[:, 5:8, :], hY[:, 5:8, :], K[:, 1:4, :], ALU.add).then_inc(dve_step, 1)
                    dve.wait_ge(dve_step, tally.next("dve_step"))
                    dve.tensor_tensor(hY[:, 4, :], hY[:, 4, :], K[:, 8, :], ALU.add).then_inc(freq_ready, 1)
                    dve.wait_ge(freq_ready, tally.next("freq_ready"))
                    ms = tally.take("misc_done")
                    dve.wait_ge(misc_done, tally.now("misc_done"))
                    dve.scalar_tensor_tensor(out=hv[:, 0, :], in0=hv[:, 0, :],
                                             scalar=vec("hy_bias", 4 * o + g), in1=mslot(ms)[:, 0:NX],
                                             op0=ALU.mult, op1=ALU.add).then_inc(misc_free[ms], 1)
                    dve.wait_ge(misc_free[ms], tally.read("misc_done"))
                    dve.wait_ge(misc_free[tally.place("misc_done", 1)], tally.read("misc_done"))
                    dve.tensor_tensor(hv[:, 0, :], hv[:, 0, :], hv[:, 1 + o, :], ALU.mult
                        ).then_inc(z_done if o else hv_ready, 1)
                    dve.wait_ge(z_done if o else hv_ready, tally.next("z_done" if o else "hv_ready"))
                    if not o:
                        dve.wait_ge(hv_ready, tally.now("hv_ready"))
                dve.wait_ge(ohi_ready, tally.next("ohi_ready"))
                dve.tensor_tensor(oab[1][:, 4 + g, :], hv[:, 0, :], oab[0][:, 4 + g, :], ALU.subtract
                    ).then_inc(mix_ready, 1)
                dve.wait_ge(mix_ready, tally.next("mix_ready"))


        def pe_merge(pe, tally):
            pe.wait_ge(mix_ready, tally.next("mix_ready", 8))

            def spans(pair, k):
                return [((pair[0][:, k, :], pair[1][:, k, :]), 0, NX)]

            with pe.Fori(0, 2) as i, tally.turns(i, 2, tile_used=12, group=16):
                for m in range(4):
                    pe_x_tiles(pe, tally, 2, False)
                    pe_tile(pe, tally, [[(k, spans(oab, k)) for k in range(4)],
                                        [(k, spans(oab, k)) for k in range(4, 8)]])
            before = tally.n.get("y_ready", 0)
            tally.passed("y_ready", KC)
            with pe.Fori(0, 2) as i, tally.turns(i, 2, tile_used=4, group=4):
                for q in range(4):
                    pe_tile(pe, tally, [[(k, spans(yy, k)) for k in range(KC)]], (y_ready, before) if q == 0 else None)

        def act_merge(act, tally):
            with act.Fori(0, 2) as i, tally.turns(i, 2, tile_used=12, group=16, tile_hi=12, yraw_ready=4, yhi_ready=4):
                for m in range(4):
                    for half in range(2):
                        tally.passed("tile_used")
                        slot = tally.take("group")
                        act.wait_ge(slot_free[tally.place("group", 3 + half)], tally.read("group", 3 + half))
                        act.wait_ge(tile_used, tally.now("tile_used"))
                        act.activation(mg[:, 2 * (m % 2) + half, :], gslot(slot)[:, 0:NX], ACT.Sigmoid
                            ).then_inc(slot_free[slot], 1)
                        act.wait_ge(slot_free[slot], tally.read("group"))
                        split_tile(act, tally)
                    skip_tiles(tally, 1, 2)
                    split_tile(act, tally)
                    act.wait_ge(yraw_ready, tally.next("yraw_ready"))
                    act.activation(yy[0][:, bass.ds(i * 4 + m, 1), :], mg[:, 2 * (m % 2):2 * (m % 2) + 1, :],
                                   ACT.Copy).then_inc(yhi_ready, 1)
                    act.wait_ge(yhi_ready, tally.next("yhi_ready"))
            with act.Fori(0, 2) as i, tally.turns(i, 2, tile_used=4, group=4, tile_hi=4, ssq_step=4, sq_ready=4):
                for q in range(4):
                    skip_tiles(tally, 1)
                    split_tile(act, tally)
                    act_square(act, tally, i * 4 + q, q % 2, NX)
            tally.passed("ssq_step", 2)

        def dve_merge(dve, tally):
            dve.tensor_copy(hgv[:, :, :], mods[:, 40:48, :]).then_inc(dve_step, 1)
            dve.wait_ge(dve_step, tally.next("dve_step"))
            with dve.Fori(0, 2) as i, tally.turns(i, 2, tile_used=12, group=16, yraw_ready=4, yhi_ready=4, y_ready=4):
                for m in range(4):
                    a, b = mg[:, 2 * (m % 2), :], mg[:, 2 * (m % 2) + 1, :]
                    skip_tiles(tally, 2)
                    dve.wait_ge(slot_free[tally.place("group", 2)], tally.read("group", 2))
                    dve.wait_ge(slot_free[tally.place("group", 1)], tally.read("group", 1))
                    tally.passed("tile_used")
                    for half, t in enumerate((a, b)):
                        slot = tally.take("group")
                        if not half:
                            dve.wait_ge(tile_used, tally.now("tile_used"))
                        dve.tensor_tensor(t, gslot(slot)[:, 0:NX], t, ALU.mult).then_inc(slot_free[slot], 1)
                        dve.wait_ge(slot_free[slot], tally.read("group"))
                    dve.wait_ge(slot_free[tally.place("group", 1)], tally.read("group"))
                    dve.tensor_tensor(a, a, b, ALU.add).then_inc(yraw_ready, 1)
                    dve.wait_ge(yraw_ready, tally.next("yraw_ready"))
                    dve.wait_ge(yhi_ready, tally.next("yhi_ready"))
                    dve.tensor_tensor(yy[1][:, bass.ds(i * 4 + m, 1), :],
                                      mg[:, 2 * (m % 2):2 * (m % 2) + 1, :],
                                      yy[0][:, bass.ds(i * 4 + m, 1), :], ALU.subtract).then_inc(y_ready, 1)
                    dve.wait_ge(y_ready, tally.next("y_ready"))
            dve_sum_start(dve, tally)
            with dve.Fori(0, 2) as i, tally.turns(i, 2, tile_used=4, group=4, ssq_step=4, sq_ready=4):
                for q in range(4):
                    tally.passed("tile_used")
                    slot = tally.take("group")
                    dve.wait_ge(tile_used, tally.now("tile_used"))
                    dve_residual(dve, tally, slot, i * 4 + q, False)
                    dve_sum(dve, tally, q % 2, NX)


        def pe_gate(pe, tally, u):
            place = tally.place("misc_done")
            pe.wait_ge(misc_free[place], tally.free("misc_done"))
            m = mslot(place)
            for a, b in ((0, NX), (NX, NT)):
                last = pe.matmul(m[:, a:b], gatew[:, u, :], lr[:, a:b], start=True, stop=True)
            last.then_inc(misc_done, 1)
            tally.passed("misc_done")

        def pe_gla(pe, tally, toks):
            with_ctx = toks == NT
            x_before = tally.n["x_ready"]
            tally.passed("x_ready", KC)
            pe_values(pe, tally, 2, vt2, (x_ready, x_before))
            pe.wait_ge(lrw_ready, tally.next("lrw_ready"))
            place = tally.place("misc_done")
            pe.wait_ge(misc_free[place], tally.free("misc_done"))
            m = mslot(place)
            for k in range(KC):
                for pi, (w, part) in enumerate(((0, 0), (0, 1), (1, 0))):
                    for rhs, col, n in x_spans(k, True):
                        last = pe.matmul(m[0:32, col:col + n], lrs[w][:, k, :], rhs[part],
                                         start=(k == 0 and pi == 0), stop=(k == KC - 1 and pi == 2))
            last.then_inc(misc_done, 1)
            tally.passed("misc_done")
            pe_x_tiles(pe, tally, 2, True)
            pe.wait_ge(lr_ready, tally.next("lr_ready"))
            pe_gate(pe, tally, 0)
            pe_x_tiles(pe, tally, 2, True)
            pe_x_tiles(pe, tally, 2, with_ctx)
            ktok_ready = pe_unit_head(pe, tally, unit(u2, 0, 2))
            for u in range(4):
                t = u % 2

                def ahead(li, nxt=u + 1):
                    if nxt < 4 and li == 1:
                        pe_gate(pe, tally, nxt)

                def head(nxt=u + 1):
                    return pe_unit_head(pe, tally, unit(u2, nxt, 2)) if nxt < 4 else None

                ktok_ready = pe_unit(pe, tally, unit(u2, u, 2), gq[:, t, :], gk[:, t, :],
                                     lambda c, t=t: vtok2[:, c, t * P:(t + 1) * P], 2, toks, ktok_ready, ahead, head)
            pe_head_norm(pe, tally, 2, toks, 2, blk[:, 0:P:HD], hsq2,
                         lambda: pe_x_tiles(pe, tally, 2, with_ctx))

        def act_gla(act, tally, layer, toks):
            with_ctx = toks == NT
            act.wait_ge(arena_free, tally.next("arena_free"))
            act.dma_start(gatew[:, :, :], ins["gatew"][layer]).then_inc(gate_landed, 16)
            act.dma_start(lrw[:, :, :], ins["lrw"][layer]).then_inc(lrw_landed, 16)
            act.wait_ge(lrw_landed, 16 * (layer + 1))
            act.activation(lrs[0][:, :, :], lrw[:, :, :], ACT.Copy).then_inc(lrw_hi, 1)
            act.wait_ge(lrw_hi, tally.next("lrw_hi"))
            act_values(act, tally, 2, vt2)
            tally.take("misc_done")
            for t in range(2):
                tally.passed("tile_used")
                slot = tally.take("group")
                act.wait_ge(tile_used, tally.now("tile_used"))
                act.activation(gq[:, t, :], gslot(slot)[:, 0:NT], ACT.Copy, scale=HD ** -0.5
                    ).then_inc(slot_free[slot], 1)
                act.wait_ge(slot_free[slot], tally.read("group"))
                split_tile(act, tally)
            def soft(u, place, count):
                U = unit(u2, u, 2)
                x = U["ek"][:, :]
                act.wait_ge(misc_free[place], count)
                act.activation(x, U["lf"][:, :], ACT.Abs).then_inc(act_step, 1)
                act.wait_ge(act_step, tally.next("act_step"))
                act.activation(x, x, ACT.Exp, scale=-1.0).then_inc(act_step, 1)
                act.wait_ge(act_step, tally.next("act_step"))
                act.activation(x, x, ACT.Ln, bias=1.0).then_inc(ge_ready, 1)
                act.wait_ge(ge_ready, tally.next("ge_ready"))

            soft(0, tally.take("misc_done"), tally.read("misc_done"))
            for t in range(2):
                act_proj(act, tally, gk[:, t, :], NT)
            for t in range(2):
                act_proj(act, tally, gg[:, t, 0:toks], toks, ACT.Silu)
            act_unit_head(act, tally, unit(u2, 0, 2), toks, 1.0 / 16.0)
            for u in range(4):
                gate = []

                def ahead(li, nxt=u + 1):
                    if nxt < 4 and li == 1:
                        gate.extend((tally.take("misc_done"), tally.read("misc_done")))
                    elif nxt < 4 and li == 4:
                        soft(nxt, *gate)
                    elif nxt < 4 and li == 6:
                        act_unit_head(act, tally, unit(u2, nxt, 2), toks, 1.0 / 16.0)

                act_unit(act, tally, unit(u2, u, 2), 2, toks, 1.0 / 16.0, ahead)
            act_head_norm(act, tally, 2, toks, hsq2, oacc2, gg, mo, 6, lambda: None,
                          lambda: act_conv_inputs(act, tally, layer, toks, 0))

        def dve_gla(dve, tally, layer, toks):
            dve.tensor_copy(small[:, 0:1], vec("final_w")).then_inc(arena_free, 1)
            dve.wait_ge(arena_free, tally.next("arena_free"))
            dve.wait_ge(lrw_hi, tally.next("lrw_hi"))
            dve.tensor_tensor(lrs[1][:, :, :], lrw[:, :, :], lrs[0][:, :, :], ALU.subtract).then_inc(lrw_ready, 1)
            dve.wait_ge(lrw_ready, tally.next("lrw_ready"))
            dve_values(dve, tally, 2, vtok2)
            ms = tally.take("misc_done")
            dve.wait_ge(misc_done, tally.now("misc_done"))
            dve.tensor_copy(lr[:, :], mslot(ms)[0:32, 0:NT]).then_inc(misc_free[ms], 1)
            dve.wait_ge(misc_free[ms], tally.read("misc_done"))
            dve.wait_ge(gate_landed, 16 * (layer + 1))
            dve.tensor_copy(small[:, 0:1], vec("final_w")).then_inc(lr_ready, 1)
            dve.wait_ge(lr_ready, tally.next("lr_ready"))
            def gate(u):
                ms = tally.take("misc_done")
                dve.wait_ge(misc_done, tally.now("misc_done"))
                dve.tensor_scalar(unit(u2, u, 2)["lf"][:, :], mslot(ms)[:, 0:NT], vec("gate_b", 4 * layer + u), None,
                                  ALU.add).then_inc(misc_free[ms], 1)
                dve.wait_ge(misc_free[ms], tally.read("misc_done"))

            def log_gate(u):
                U = unit(u2, u, 2)
                dve.wait_ge(ge_ready, tally.next("ge_ready"))
                dve.scalar_tensor_tensor(out=U["lf"][:, :], in0=U["lf"][:, :], scalar=0.0, in1=U["ek"][:, :],
                                         op0=ALU.min, op1=ALU.subtract).then_inc(dve_step, 1)
                dve.wait_ge(dve_step, tally.next("dve_step"))

            gate(0)
            log_gate(0)
            dve_cum(dve, tally, unit(u2, 0, 2))
            skip_tiles(tally, 6)
            for back in (1, 2):
                dve.wait_ge(slot_free[tally.place("group", back)], tally.read("group", back))
            dve_unit_head(dve, tally, unit(u2, 0, 2), gq[:, 0, :], gk[:, 0, :], toks)
            tally.take("misc_done")
            for u in range(4):
                def ahead(li, nxt=u + 1):
                    if nxt < 4 and li == 3:
                        gate(nxt)
                    elif nxt < 4 and li == 5:
                        log_gate(nxt)
                    elif nxt < 4 and li == 6:
                        dve_cum(dve, tally, unit(u2, nxt, 2))

                def head(nxt=u + 1):
                    dve_unit_head(dve, tally, unit(u2, nxt, 2), gq[:, nxt % 2, :], gk[:, nxt % 2, :], toks)

                dve_unit(dve, tally, unit(u2, u, 2), gq[:, u % 2, :], gk[:, u % 2, :], 2, toks,
                         oacc2[:, u % 2, 0:toks], ahead, head if u < 3 else None)
            dve_head_norm(dve, tally, 2, toks, HD, oacc2, gg, vec("gla_w", layer), mo, 6, lambda: None)


        def act_conv_inputs(act, tally, layer, toks, j):
            if j == 2:
                act.wait_ge(mix_ready, 8 + 8 * layer + 2)
            for t in range(2):
                act_proj(act, tally, cv[:, j, t, 0:toks], toks)

        def act_conv2(act, tally, layer, toks):
            for j in (1, 2):
                act_conv_inputs(act, tally, layer, toks, j)
            for t in range(2):
                act.wait_ge(conv_ready, tally.next("conv_ready"))
                act.activation(mo[0][:, t, 0:toks], cy[:, 0:toks], ACT.Copy).then_inc(ohi_ready, 1)
                act.wait_ge(ohi_ready, tally.next("ohi_ready"))

        def dve_conv2(dve, tally, layer, toks):
            parts = ((0, NX, 1), (NX, NT, 3))[:2 if toks == NT else 1]
            dve.memset(cu[:, :], 0.0).then_inc(dve_step, 1)
            dve.wait_ge(dve_step, tally.next("dve_step"))
            skip_tiles(tally, 6)
            for back in (1, 2):
                dve.wait_ge(slot_free[tally.place("group", back)], tally.read("group", back))
            for t in range(2):
                for a, b, sh in parts:
                    ins = dve.tensor_tensor(cu[:, a + sh:b + sh], cv[:, 0, t, a:b], cv[:, 1, t, a:b], ALU.mult)
                    ins.then_inc(dve_step, 1)
                    dve.wait_ge(dve_step, tally.next("dve_step"))
                for a, b, sh in parts:
                    w = 6 * layer
                    dve.tensor_scalar(cy[:, a:b], cu[:, a + sh - 1:b + sh - 1], vec("conv2_w", w + t), None,
                                      ALU.mult).then_inc(dve_step, 1)
                    dve.wait_ge(dve_step, tally.next("dve_step"))
                    for tap in (1, 2):
                        dve.scalar_tensor_tensor(out=cy[:, a:b], in0=cu[:, a + sh - 1 + tap:b + sh - 1 + tap],
                                                 scalar=vec("conv2_w", w + 2 * tap + t), in1=cy[:, a:b],
                                                 op0=ALU.mult, op1=ALU.add).then_inc(dve_step, 1)
                        dve.wait_ge(dve_step, tally.next("dve_step"))
                dve.tensor_tensor(cy[:, 0:toks], cy[:, 0:toks], cv[:, 2, t, 0:toks], ALU.mult).then_inc(conv_ready, 1)
                dve.wait_ge(conv_ready, tally.next("conv_ready"))
                dve.wait_ge(conv_ready, tally.now("conv_ready"))
                dve.wait_ge(ohi_ready, tally.next("ohi_ready"))
                dve.tensor_tensor(mo[1][:, t, 0:toks], cy[:, 0:toks], mo[0][:, t, 0:toks], ALU.subtract
                    ).then_inc(mix_ready, 1)
                dve.wait_ge(mix_ready, tally.next("mix_ready"))


        def att_items(toks):
            return [(c, s, qb) for c in range(4) for s in range(2) for qb in range(toks // P)]

        def local_keys(qb):
            return [] if qb >= XCH else [b for b in (qb - 1, qb, qb + 1) if 0 <= b < XCH]

        def pe_rope(pe, tally, src_slot, back):
            pe.wait_ge(slot_free[tally.place("group", back)], tally.read("group", back))
            place = tally.place("misc_done")
            pe.wait_ge(misc_free[place], tally.free("misc_done"))
            m = mslot(place)
            pe.matmul(m[:, 0:NX], rot[:, :], araw[:, src_slot, 0:NX], start=True, stop=True).then_inc(misc_done, 1)
            tally.passed("misc_done")

        def pe_attention(pe, tally, toks):
            with_ctx = toks == NT
            pe_x_tiles(pe, tally, 4, with_ctx)
            pe_x_tiles(pe, tally, 1, True)
            pe_rope(pe, tally, 0, 1)
            pe_x_tiles(pe, tally, 1, True)
            pe.wait_ge(slot_free[tally.place("group", 1)], tally.read("group"))
            place = tally.place("misc_done")
            pe.wait_ge(misc_free[place], tally.free("misc_done"))
            m = mslot(place)
            for c in range(ALLCH):
                last = pe.transpose(m[:, c * P:(c + 1) * P], araw[:, 1, c * P:(c + 1) * P], ident[:, :])
            last.then_inc(misc_done, 1)
            tally.passed("misc_done")
            for c in range(4):
                pe_x_tiles(pe, tally, 1, with_ctx)
                pe_rope(pe, tally, c % 2, 1)
            pe.wait_ge(slot_free[tally.place("group", 1)], tally.read("group", 1))
            pe.wait_ge(slot_free[tally.place("group", 2)], tally.read("group", 2))
            pe.wait_ge(rope_done, tally.next("rope_done", 5))
            items = att_items(toks)

            def scores(i):
                c, s, qb = items[i]
                place = tally.place("misc_done")
                pe.wait_ge(misc_free[place], tally.free("misc_done"))
                m = mslot(place)
                r = slice(s * HD, (s + 1) * HD)
                qq = aq[r, c, qb * P:(qb + 1) * P]
                last = pe.matmul(m[:, 0:NCTX], qq, akx[r, NX:NT], start=True, stop=True)
                lk = local_keys(qb)
                if lk:
                    last = pe.matmul(m[:, 512:512 + len(lk) * P], qq, akx[r, lk[0] * P:(lk[-1] + 1) * P],
                                     start=True, stop=True)
                last.then_inc(misc_done, 1)
                tally.passed("misc_done")

            def turn(i):
                n = 2 + len(local_keys(items[i][2]))
                pe.wait_ge(pn_ready, tally.next("pn_ready"))
                if i >= 1:
                    pe.wait_ge(pt_ready, tally.next("pt_ready"))
                for b in range(n):
                    last = pe.transpose(gslot(1)[:, b * P:(b + 1) * P], pr[:, i % 2, b * P:(b + 1) * P],
                                        ident[:, :])
                last.then_inc(pt_done, 1)
                tally.passed("pt_done")

            def values(i):
                c, s, qb = items[i]
                if i == len(items) - 1:
                    pe.wait_ge(pt_ready, tally.next("pt_ready"))
                if (s, qb) == (0, 0) and c:
                    pe.wait_ge(mix_ready, tally.next("mix_ready"))
                keys = [4, 5] + local_keys(qb)
                f = slice(s * HD, (s + 1) * HD)
                for n, kc in enumerate(keys):
                    last = pe.matmul(gslot(0)[f, qb * P:(qb + 1) * P], avt[:, kc, f],
                                     pT[:, i % 2, n * P:(n + 1) * P], start=(n == 0), stop=(n == len(keys) - 1),
                                     skip_group_check=True)
                if i == len(items) - 1 or items[i + 1][0] != c:
                    last.then_inc(ao_done, 1)
                    tally.passed("ao_done")

            pe.wait_ge(mix_ready, tally.next("mix_ready", 4))
            scores(0)
            scores(1)
            for i in range(len(items)):
                if i + 2 < len(items):
                    scores(i + 2)
                turn(i)
                if i:
                    values(i - 1)
            values(len(items) - 1)
            pe.wait_ge(mix_ready, tally.next("mix_ready"))

        def act_attention(act, tally, layer, toks):
            act.dma_start(rope[:, :, :], ins["rope"]).then_inc(rope_landed, 16)
            act_proj(act, tally, araw[:, 0, :], NT)
            tally.take("misc_done")
            act_proj(act, tally, araw[:, 1, :], NT)
            tally.take("misc_done")
            for c in range(4):
                if c == 0:
                    act.wait_ge(rope_done, tally.next("rope_done"))
                elif c == 1:
                    act.wait_ge(misc_free[tally.place("misc_done", 2)], tally.read("misc_done", 2))
                else:
                    act.wait_ge(rope_done, tally.next("rope_done"))
                act_proj(act, tally, araw[:, c % 2, 0:toks], toks)
                tally.take("misc_done")
            items = att_items(toks)
            act.wait_ge(rope_done, tally.next("rope_done", 2))

            def expo(i):
                c, s, qb = items[i]
                h = c + 4 * s
                w = 6 + 8 * (i % 2)
                act.wait_ge(m_ready, tally.next("m_ready"))
                lk = len(local_keys(qb))
                neg = small[:, w + 1:w + 2]
                sums = small[:, w + 2:w + 5]
                ms = tally.take("misc_done")
                act.activation(pr[:, i % 2, 0:NCTX], mslot(ms)[:, 0:NCTX], ACT.Exp, bias=neg, scale=ATT_SCALE,
                               accum_out=sums[:, 1:2]).then_inc(misc_free[ms], 1)
                act.wait_ge(misc_free[ms], tally.read("misc_done"))
                if lk:
                    act.activation(pr[:, i % 2, NCTX:NCTX + lk * P], sl[:, i % 2, 0:lk * P], ACT.Exp,
                                   bias=neg, scale=ATT_SCALE, accum_out=sums[:, 0:1]).then_inc(act_step, 1)
                    act.wait_ge(act_step, tally.next("act_step"))
                act.activation(sums[:, 2:3], mx[:, h, 2:3], ACT.Exp, bias=neg, scale=ATT_SCALE).then_inc(exp_ready, 1)
                act.wait_ge(exp_ready, tally.next("exp_ready"))

            def copy(i):
                n = 2 + len(local_keys(items[i][2]))
                act.wait_ge(pt_done, tally.next("pt_done"))
                act.activation(pT[:, i % 2, 0:n * P], gslot(1)[:, 0:n * P], ACT.Copy).then_inc(pt_ready, 1)
                act.wait_ge(pt_ready, tally.next("pt_ready"))

            def leave(c):
                act.wait_ge(ao_done, tally.next("ao_done"))
                act.activation(mo[0][:, 2 + c, 0:toks], gslot(0)[:, 0:toks], ACT.Copy).then_inc(ohi_ready, 1)
                act.wait_ge(ohi_ready, tally.next("ohi_ready"))

            per = len(items) // 4
            for i in range(len(items)):
                expo(i)
                if i:
                    copy(i - 1)
                if i > 1 and (i - 1) % per == 0:
                    leave((i - 1) // per - 1)
            copy(len(items) - 1)
            leave(3)

        def dve_attention(dve, tally, layer, toks):
            skip_tiles(tally, 1)
            dve.wait_ge(rope_landed, 16 * (layer + 1))

            def rotate(dst, src, n):
                dve.wait_ge(slot_free[tally.place("group", 1)], tally.read("group"))
                ms = tally.take("misc_done")
                dve.wait_ge(misc_done, tally.now("misc_done"))
                dve.tensor_tensor(arot[:, 0:NX], mslot(ms)[:, 0:NX], rope[:, 1, :], ALU.mult
                    ).then_inc(misc_free[ms], 1)
                dve.wait_ge(misc_free[ms], tally.read("misc_done"))
                dve.tensor_tensor(dst[:, 0:NX], src[:, 0:NX], rope[:, 0, :], ALU.mult).then_inc(dve_step, 1)
                dve.wait_ge(dve_step, tally.next("dve_step"))
                ins = dve.tensor_tensor(dst[:, 0:NX], dst[:, 0:NX], arot[:, 0:NX], ALU.add)
                if n > NX:
                    ins.then_inc(dve_step, 1)
                    dve.wait_ge(dve_step, tally.next("dve_step"))
                    ins = dve.tensor_copy(dst[:, NX:n], src[:, NX:n])
                ins.then_inc(rope_done, 1)
                dve.wait_ge(rope_done, tally.next("rope_done"))

            rotate(akx[:, :], araw[:, 0, :], NT)
            skip_tiles(tally, 1)
            ms = tally.take("misc_done")
            dve.wait_ge(misc_done, tally.now("misc_done"))
            dve.tensor_copy(avt[:, :, :], mslot(ms)[:, 0:NT].rearrange("p (c f) -> p c f", f=P)
                ).then_inc(misc_free[ms], 1)
            dve.wait_ge(misc_free[ms], tally.read("misc_done"))
            for c in range(4):
                skip_tiles(tally, 1)
                rotate(aq[:, c, :], araw[:, c % 2, :], toks)
            dve.tensor_scalar(mx[:, :, 2], vec("sink", 8 * layer, 8), 1.0 / ATT_SCALE, None, ALU.mult
                ).then_inc(dve_step, 1)
            dve.wait_ge(dve_step, tally.next("dve_step"))
            items = att_items(toks)
            per = len(items) // 4

            def top(i):
                c, s, qb = items[i]
                h = c + 4 * s
                w = 6 + 8 * (i % 2)
                ms = tally.take("misc_done")
                dve.wait_ge(misc_done, tally.now("misc_done"))
                lk = local_keys(qb)
                if lk:
                    a0 = P if qb == 0 else 0
                    dve.tensor_tensor(sl[:, i % 2, 0:len(lk) * P], mslot(ms)[:, 512:512 + len(lk) * P],
                                      amask[:, a0:a0 + len(lk) * P], ALU.add).then_inc(dve_step, 1)
                    dve.wait_ge(dve_step, tally.next("dve_step"))
                    dve.wait_ge(dve_step, tally.now("dve_step"))
                    dve.tensor_reduce(mx[:, h, 0:1], sl[:, i % 2, 0:len(lk) * P], AX.X, ALU.max).then_inc(dve_step, 1)
                    dve.wait_ge(dve_step, tally.next("dve_step"))
                dve.tensor_reduce(mx[:, h, 1:2], mslot(ms)[:, 0:NCTX], AX.X, ALU.max).then_inc(dve_step, 1)
                dve.wait_ge(dve_step, tally.next("dve_step"))
                dve.tensor_reduce(small[:, w:w + 1], mx[:, h, (0 if lk else 1):3], AX.X, ALU.max).then_inc(dve_step, 1)
                dve.wait_ge(dve_step, tally.next("dve_step"))
                dve.tensor_scalar(small[:, w + 1:w + 2], small[:, w:w + 1], -ATT_SCALE, None, ALU.mult
                    ).then_inc(m_ready, 1)
                dve.wait_ge(m_ready, tally.next("m_ready"))

            def norm(i):
                lk = len(local_keys(items[i][2]))
                w = 6 + 8 * (i % 2)
                dve.wait_ge(exp_ready, tally.next("exp_ready"))
                dve.tensor_reduce(small[:, w + 5:w + 6], small[:, w + (2 if lk else 3):w + 5], AX.X, ALU.add
                    ).then_inc(dve_step, 1)
                dve.wait_ge(dve_step, tally.next("dve_step"))
                dve.reciprocal(small[:, w + 5:w + 6], small[:, w + 5:w + 6]).then_inc(dve_step, 1)
                dve.wait_ge(dve_step, tally.next("dve_step"))
                n = NCTX + lk * P
                dve.tensor_scalar(pr[:, i % 2, 0:n], pr[:, i % 2, 0:n], small[:, w + 5:w + 6], None,
                                  ALU.mult).then_inc(pn_ready, 1)
                dve.wait_ge(pn_ready, tally.next("pn_ready"))

            def leave(c):
                dve.wait_ge(ohi_ready, tally.next("ohi_ready"))
                dve.tensor_tensor(mo[1][:, 2 + c, 0:toks], gslot(0)[:, 0:toks], mo[0][:, 2 + c, 0:toks],
                                  ALU.subtract).then_inc(mix_ready, 1)
                dve.wait_ge(mix_ready, tally.next("mix_ready"))

            top(0)
            for i in range(len(items)):
                if i + 1 < len(items):
                    top(i + 1)
                norm(i)
                if i > 1 and (i - 1) % per == 0:
                    leave((i - 1) // per - 1)
            leave(3)

        def pe_out2(pe, tally, with_ctx):
            with pe.Fori(0, 2) as i, tally.turns(i, 2, tile_used=4, group=4):
                for _ in range(4):
                    pe_tile(pe, tally, [[(k, wide_spans(mo, k, with_ctx)) for k in range(KC)]])

        def act_out2(act, tally, n):
            with act.Fori(0, 2) as i, tally.turns(i, 2, tile_used=4, group=4, tile_hi=4, ssq_step=4, sq_ready=4):
                for q in range(4):
                    skip_tiles(tally, 1)
                    split_tile(act, tally)
                    act_square(act, tally, i * 4 + q, q % 2, n)
            tally.passed("ssq_step", 2)

        def dve_out2(dve, tally, with_ctx):
            dve.tensor_copy(hgv[:, :, :], mods[:, 16:24, :]).then_inc(dve_step, 1)
            dve.wait_ge(dve_step, tally.next("dve_step"))
            dve_sum_start(dve, tally)
            with dve.Fori(0, 2) as i, tally.turns(i, 2, tile_used=4, group=4, ssq_step=4, sq_ready=4):
                for q in range(4):
                    tally.passed("tile_used")
                    slot = tally.take("group")
                    dve.wait_ge(tile_used, tally.now("tile_used"))
                    dve_residual(dve, tally, slot, i * 4 + q, with_ctx)
                    dve_sum(dve, tally, q % 2, NT if with_ctx else NX)


        block = ctx.enter_context(nc.Block())
        first = [(vecs[:, :], ins["vecs"]), (fz[:, :], ins["fz"]), (fw1[:, :], ins["fw1"]), (fw2[:, :], ins["fw2"]),
                 (fw3[:, :, :], ins["fw3"]), (ones[:, :], ins["ones"])]
        second = [(fwin[:, :, :, :], ins["fwin"]), (dft0[:, :, :], ins["dft"])]
        third = [(H[:, :, :], ins["h"]), (pos[:, :, :], ins["pos"]), (ident[:, :], ins["ident"]),
                 (blk[:, :], ins["blk"]), (rot[:, :], ins["rot"]), (reset[:, :], ins["reset"]),
                 (amask[:, :], ins["amask"])]

        @block.sync
        def _(sp):
            for dst, src in first:
                sp.dma_start(dst, src).then_inc(first_landed, 16)
            for s in range(RING):
                sp.dma_start(raw[:, s, :], ins["stream"][s]).then_inc(landed[s], 16)
            for dst, src in second:
                sp.dma_start(dst, src).then_inc(second_landed, 16)
            with sp.Fori(1, n_tiles // RING) as i:
                for s in range(RING):
                    sp.wait_ge(tile_lo, i * RING + (s + 1 - RING))
                    sp.dma_start(raw[:, s, :], ins["stream"][bass.ds(i * RING + s, 1)].rearrange("a p n -> (a p) n")
                                 ).then_inc(landed[s], 16)
            for m in range(KC):
                sp.wait_ge(final_ready, KC + m + 1)
                sp.dma_start(out[m], H[:, m, 0:NX]).then_inc(out_landed, 16)
            sp.wait_ge(out_landed, 16 * KC)
            for s in range(4):
                sp.wait_ge(k_stored[s], 2 * 16 * sum(K_STORES[s]))

        @block.gpsimd
        def _(pool):
            with pool.Fori(0, n_tiles // RING) as i:
                for s in range(RING):
                    pool.wait_ge(tile_hi, i * RING + s + 1)
                    nc.gpsimd.tensor_tensor(wr_lo[:, s, :], raw[:, s, :], wr_hi[:, s, :],
                                            ALU.subtract).then_inc(tile_lo, 1)

        @block.tensor
        def _(pe):
            tally = Tally()
            pe.wait_ge(first_landed, 16 * len(first))
            for stage in STAGES:
                if stage == "filters":
                    pe_filters(pe, tally)
                    pe.wait_ge(third_landed, 16 * len(third))
                elif stage == "block1_ffn1":
                    pe_norm(pe, tally, True)
                    pe_ffn(pe, tally, True)
                elif stage == "block1_mix":
                    pe_norm(pe, tally, True)
                    pe_hgrn(pe, tally)
                    pe_hyena(pe, tally)
                    pe_merge(pe, tally)
                elif stage == "block1_ffn2":
                    pe_norm(pe, tally, False)
                    tally.passed("c_ready")
                    pe_ffn(pe, tally, False, with_mod=True)
                    pe_norm(pe, tally, False)
                elif stage[:-1] == "block2_mix":
                    toks = NT if stage[-1] == "0" else NX
                    pe_norm(pe, tally, True)
                    pe_gla(pe, tally, toks)
                    pe_attention(pe, tally, toks)
                    pe_out2(pe, tally, toks == NT)
                elif stage[:-1] == "block2_ffn":
                    with_ctx = stage[-1] == "0"
                    pe_norm(pe, tally, with_ctx)
                    pe_ffn(pe, tally, with_ctx, with_mod=with_ctx)
                elif stage == "final":
                    pe_norm(pe, tally, False)

        @block.scalar
        def _(act):
            tally = Tally()
            act.wait_ge(first_landed, 16 * len(first))
            for s in range(RING):
                act.wait_ge(landed[s], 16)
                act.activation(wr_hi[:, s, :], raw[:, s, :], ACT.Copy).then_inc(tile_hi, 1)
                act.wait_ge(tile_hi, tally.next("tile_hi"))
            for stage in STAGES:
                if stage == "filters":
                    act_filters(act, tally)
                elif stage == "block1_ffn1":
                    act_norm(act, tally, True)
                    act_ffn(act, tally, True)
                elif stage == "block1_mix":
                    act_norm(act, tally, True, 3, summed=True)
                    act_hgrn(act, tally)
                    act_hyena(act, tally)
                    act_merge(act, tally)
                elif stage == "block1_ffn2":
                    act_mod_input(act, tally, "cvec2")
                    act_norm(act, tally, False, 6, summed=True)
                    act_ffn(act, tally, False, with_mod=True)
                    act.dma_start(H[:, :, NX:NT], ins["ctx2"]).then_inc(ctx2_landed, 16)
                    act_norm(act, tally, False, final=True, summed=True)
                elif stage[:-1] == "block2_mix":
                    toks = NT if stage[-1] == "0" else NX
                    layer = int(stage[-1])
                    if layer == 0:
                        act.wait_ge(ctx2_landed, 16)
                        act.wait_ge(final_ready, tally.next("final_ready", KC))
                    act_norm(act, tally, True, summed=layer == 1)
                    act_gla(act, tally, layer, toks)
                    act_conv2(act, tally, layer, toks)
                    act_attention(act, tally, layer, toks)
                    act_out2(act, tally, toks)
                elif stage[:-1] == "block2_ffn":
                    with_ctx = stage[-1] == "0"
                    act_norm(act, tally, with_ctx, 3, summed=True)
                    act_ffn(act, tally, with_ctx, with_mod=with_ctx, last=not with_ctx)
                elif stage == "final":
                    act_norm(act, tally, False, final=True, summed=True)

        @block.vector
        def _(dve):
            tally = Tally()
            for j, place in enumerate((*slot_free, *misc_free)):
                dve.memset(small[:, 56 + j:57 + j], 0.0).then_inc(place, 1)
            dve.wait_ge(first_landed, 16 * len(first))
            for stage in STAGES:
                if stage == "filters":
                    dve_filters(dve, tally)
                    dve.wait_ge(third_landed, 16 * len(third))
                    for m in range(KC):
                        dve.tensor_tensor(H[:, m, 0:NX], H[:, m, 0:NX], pos[:, m, :], ALU.add).then_inc(dve_step, 1)
                        dve.wait_ge(dve_step, tally.next("dve_step"))
                elif stage == "block1_ffn1":
                    for s in range(4):
                        dve.wait_ge(k_stored[s], 2 * 16 * sum(K_STORES[s]))
                    dve_norm(dve, tally, True, 0, 1)
                    dve_ffn(dve, tally, True, 2, 0.5)
                elif stage == "block1_mix":
                    dve_norm(dve, tally, True, 3, 4, summed=True)
                    dve_hgrn(dve, tally)
                    dve_hyena(dve, tally)
                    dve_merge(dve, tally)
                elif stage == "block1_ffn2":
                    dve_mod_input(dve, tally)
                    dve_norm(dve, tally, False, 6, 7, summed=True)
                    dve_ffn(dve, tally, False, 8, 0.5, mod_bias=VEC_AT["b_mod0"][0])
                    dve_norm(dve, tally, False, final=vec("final_w", 0, 8), summed=True)
                elif stage[:-1] == "block2_mix":
                    layer = int(stage[-1])
                    toks = NX if layer else NT
                    if layer == 0:
                        dve.wait_ge(ctx2_landed, 16)
                    dve_norm(dve, tally, True, 0, 1, gain=vec("n1g", 8 * layer, 8),
                             summed=layer == 1)
                    dve_gla(dve, tally, layer, toks)
                    dve_conv2(dve, tally, layer, toks)
                    dve_attention(dve, tally, layer, toks)
                    dve_out2(dve, tally, toks == NT)
                elif stage[:-1] == "block2_ffn":
                    layer = int(stage[-1])
                    dve_norm(dve, tally, layer == 0, 3, 4, gain=vec("n2g", 8 * layer, 8), summed=True)
                    dve_ffn(dve, tally, layer == 0, 5, 1.0, mod_bias=None if layer else VEC_AT["b_mod1"][0])
                elif stage == "final":
                    dve_norm(dve, tally, False, final=vec("final2", 0, 8), summed=True)


STAGES = ("filters", "block1_ffn1", "block1_mix", "block1_ffn2", "block2_mix0", "block2_ffn0", "block2_mix1",
          "block2_ffn1", "final")
MAGIC = 1.5 * 2.0 ** 23
TWO_PI_HI = 6.28125
PI_F = 3.14159250
K_STORES = ((2, 3), (1, 1), (1, 1), (1, 1))
ATT_SCALE = HD ** -0.5



def _tiles(w):
    n = w.shape[1] // P
    return w.reshape(KC, P, n, P).transpose(2, 1, 0, 3).reshape(n, P, D)


def _mod_tiles(w):
    n = w.shape[1] // 512
    return w.reshape(4, 2, P, n, 512).transpose(3, 0, 2, 1, 4).reshape(4 * n, P, D)


def _ffn_tiles(gate, up, down, mod=None):
    out = []
    at = 0
    g, u = _tiles(gate), _tiles(up)
    for third, F in enumerate(F_THIRDS):
        d = down[at * P:(at + F) * P].reshape(F, P, KC, P).transpose(2, 1, 0, 3).reshape(KC, P, F * P)
        t = np.concatenate([np.stack([g[at:at + F], u[at:at + F]], 1).reshape(2 * F, P, D),
                            np.pad(d, ((0, 0), (0, 0), (0, D - F * P)))], 0)
        if mod is not None and third < 2:
            t = np.stack([_mod_tiles(mod).reshape(2, 6, 4, P, D)[third], t.reshape(6, 4, P, D)], 2
                         ).reshape(48, P, D)
        out.append(t)
        at += F
    return out


def _cols(v):
    v = np.asarray(v)
    return v.reshape(-1, P).T


def _tables():
    t = {}
    eye = np.eye(P, dtype=np.float32)
    t["ident"], t["ones"] = eye, np.ones((P, P), np.float32)
    idx = np.arange(P)
    t["blk"] = (idx[:, None] // HD == idx[None, :] // HD).astype(np.float32)
    r = np.zeros((P, P), np.float32)
    for m in range(P):
        if m % 32 < 16:
            r[m + 16, m] = -1.0
        else:
            r[m - 16, m] = 1.0
    t["rot"] = r
    t["reset"] = np.broadcast_to((np.arange(NT) % CH != 0).astype(np.float32), (P, NT)).copy()
    mk = np.zeros((P, 2, 8, P), np.int32)
    s, q = idx[:, None], idx[None, :]
    for li, b in enumerate(LEVELS):
        same = s // (2 * b) == q // (2 * b)
        first_s, first_q = (s // b) % 2 == 0, (q // b) % 2 == 0
        mk[:, 0, li] = same & first_s & ~first_q
        mk[:, 1, li] = same & ~first_s & first_q
    t["masks"] = mk
    am = np.zeros((P, 3, P), np.float32)
    am[:, 0] = np.where(q >= s, 0.0, -1e30)
    am[:, 2] = np.where(q <= s, 0.0, -1e30)
    t["amask"] = am.reshape(P, 3 * P)
    grid = 64
    rows_ = NX // grid
    quarter = D // 4
    omega = (1.0 / (10000.0 ** (np.arange(quarter, dtype=np.float32) / quarter))).astype(np.float32)
    ar = np.arange(rows_, dtype=np.float32)[:, None] * omega
    ac = np.arange(grid, dtype=np.float32)[:, None] * omega
    er = np.concatenate([np.sin(ar), np.cos(ar)], -1)
    ec = np.concatenate([np.sin(ac), np.cos(ac)], -1)
    emb = np.concatenate([np.broadcast_to(er[:, None], (rows_, grid, D // 2)),
                          np.broadcast_to(ec[None], (rows_, grid, D // 2))], -1).reshape(NX, D)
    t["pos"] = emb.T.reshape(KC, P, NX).transpose(1, 0, 2).astype(np.float32).copy()
    p = np.arange(NX, dtype=np.float32)
    tt = p / (NX - 1)
    w = (2.0 * np.pi * p / NX).astype(np.float32)
    f = np.linspace(1e-4, 15, 16, dtype=np.float32)
    ang = w[:, None] * f[None]
    z = np.concatenate([tt[:, None], np.cos(ang), -np.sin(ang)], -1).astype(np.float32)
    t["fz"] = np.concatenate([z, z[::-1]], 0).T.copy()
    lo, hi = np.log(1e-2) / 1.5, np.log(1e-2) / 0.3
    deltas = np.abs(np.linspace(lo, hi, 512, dtype=np.float32))
    win = (np.exp(-tt[:, None] * deltas[None]) + 0.05).astype(np.float32)
    t["fwin"] = np.stack([win, win[::-1]]).reshape(2, 4, P, 512).transpose(2, 0, 1, 3).astype(np.float32).copy()
    fr = np.concatenate([np.arange(0, 512, 2), np.arange(1, 512, 2)])
    n = np.arange(NX)
    a = 2 * np.pi * ((n[:, None] * fr[None]) % 1024) / 1024.0
    C = np.cos(a)
    S = -np.sin(a)
    S[:, 0] = np.where(n % 2 == 0, 1.0, -1.0)
    t["dft"] = np.concatenate([C, S], 1).reshape(4, P, 1024).transpose(1, 0, 2).astype(np.float32).copy()
    inv = np.concatenate([2 * C, 2 * S], 1)
    inv[:, 0] = 1.0
    inv[:, 512] = S[:, 0]
    t["idft"] = (inv.T / 1024.0).reshape(8, P, NX).transpose(1, 0, 2).astype(np.float32).copy()
    tok = np.arange(NX)
    row, col = (tok // grid).astype(np.float32), (tok % grid).astype(np.float32)
    inv_freq = (10000.0 ** (-np.arange(16, dtype=np.float32) / 16)).astype(np.float32)
    h = idx % HD
    pos = np.where((h // 32 == 0)[:, None], row[None], col[None])
    an = pos * inv_freq[h % 16][:, None]
    t["rope"] = np.stack([np.cos(an), np.sin(an)], 1).astype(np.float32)
    return t


def _fm(a, n):
    return np.asarray(a).T.reshape(KC, P, n).transpose(1, 0, 2)


def kernel(**inputs):
    import concourse.bacc as _bacc
    from concourse.bass_utils import run_bass_kernel_spmd as _run

    x = {k: np.asarray(v) for k, v in inputs.items()}
    w = x["w_in"][0]
    v_, ffw, fbw, q_, g_ = (w[:, i * 512:(i + 1) * 512] for i in range(5))
    hy, mer = w[:, 2560:4096], w[:, 4096:6144]
    hyt = _tiles(hy)
    mt = _tiles(mer)
    pab = np.concatenate([x["w_proj_a"][0].reshape(4, P, KC, P), x["w_proj_b"][0].reshape(4, P, KC, P)], 0
                         ).transpose(2, 1, 0, 3).reshape(KC, P, D)
    s = [_mod_tiles(x["mod_w"][0])]
    s += _ffn_tiles(x["ffn_w_gate"][0, 0], x["ffn_w_up"][0, 0], x["ffn_w_down"][0, 0])
    s += [_tiles(v_), _tiles(q_), _tiles(ffw), _tiles(fbw), _tiles(g_)]
    s += [hyt.reshape(3, 4, P, D).transpose(1, 0, 2, 3).reshape(12, P, D)]
    s += [np.stack([mt[:KC], mt[KC:], pab], 1).reshape(3 * KC, P, D)]
    s += [_tiles(x["w_out"][0])]
    s += _ffn_tiles(x["ffn_w_gate"][0, 1], x["ffn_w_up"][0, 1], x["ffn_w_down"][0, 1],
                    x["w_mod_2"][0])
    heads = np.concatenate([np.concatenate([np.arange(c * HD, (c + 1) * HD), np.arange((c + 4) * HD, (c + 5) * HD)])
                            for c in range(4)])
    for layer in range(2):
        wi = x["w_in_2"][layer]
        ci, cb, cc = wi[:, 0:256], wi[:, 256:512], wi[:, 512:768]
        aq_, ak_, av_ = wi[:, 768:1280][:, heads], wi[:, 1280:1408], wi[:, 1408:1536]
        gq_, gk_, gv_, gg_ = (wi[:, 1536 + 256 * i:1792 + 256 * i] for i in range(4))
        s += [_tiles(a) for a in (gv_, gq_, gk_, gg_, ci, cc, cb, ak_, av_, aq_)]
        wo = x["w_out_2"][layer]
        s += [_tiles(np.concatenate([wo[:256], wo[256:768][heads], wo[768:]], 0))]
        up = x["w_up_2"][layer]
        s += _ffn_tiles(up[:, :DFF], up[:, DFF:], x["w_down_2"][layer],
                        x["w_mod_2"][1] if layer == 0 else None)
    lrw_ = np.stack([x["w_in_2"][l][:, 2560:2592].reshape(KC, P, 32).transpose(1, 0, 2) for l in range(2)])
    gw = np.zeros((2, 32, 4, P), np.float32)
    for d in range(2):
        gw[:, 16 * d:16 * d + 16, 2 * d:2 * d + 2] = x["gla_gate_w_2"][:, d].reshape(2, 16, 2, P)

    vecs = np.zeros((P, NVEC), np.float32)

    def put(name, v):
        a, n = VEC_AT[name]
        assert v.shape[1] == n, (name, v.shape)
        vecs[:v.shape[0], a:a + n] = v

    put("mod_b", _cols(x["mod_b"][0]))
    put("b_mod0", _cols(x["b_mod_2"][0]))
    put("b_mod1", _cols(x["b_mod_2"][1]))
    put("cvec", np.stack([_cols(x["c"]), _cols(x["c_ctx"])], -1).reshape(P, 16))
    put("cvec2", np.stack([_cols(x["c_2"]), _cols(x["c_ctx_2"])], -1).reshape(P, 16))
    put("lbl", _cols(x["hgrn_lb_logits"]))
    put("hgrn_w", _cols(x["hgrn_norm_w"]))
    put("conv_w", _cols(x["hyena_conv_w"]))
    put("conv_b", _cols(x["hyena_conv_b"]))
    put("hy_bias", _cols(x["hyena_bias"]))
    put("final_w", _cols(x["final_norm_w"]))
    put("n1g", _cols(x["norm1_g_2"]))
    put("n2g", _cols(x["norm2_g_2"]))
    put("conv2_w", _cols(x["conv_w_2"]))
    put("gate_b", _cols(x["gla_gate_b_2"]))
    put("gla_w", np.concatenate([x["gla_norm_g_2"].T] * 2, 0))
    put("final2", _cols(x["final_norm_g_2"]))
    put("sink", np.broadcast_to(x["attn_sink_2"].reshape(1, 16), (P, 16)))
    put("hyv", np.stack([x["hyena_b1"][0], x["hyena_freq1"][0], x["hyena_b2"][0], x["hyena_freq2"][0]], 1))
    put("s4", np.repeat(np.eye(2, dtype=np.float32), 2, 0))

    arrays = _tables()
    arrays["stream"] = np.concatenate(s, 0)
    arrays["vecs"] = vecs
    arrays["h"] = np.concatenate([_fm(x["x"][0], NX), _fm(x["ctx"][0], NCTX)], 2)
    arrays["ctx2"] = _fm(x["ctx_2"][0], NCTX)
    arrays["fw1"], arrays["fw2"] = x["hyena_w1"][0], x["hyena_w2"][0]
    arrays["fw3"] = x["hyena_w3"][0].reshape(64, 4, 512)
    arrays["lrw"], arrays["gatew"] = lrw_, gw
    arrays = {k: np.ascontiguousarray(v) for k, v in arrays.items()}

    nc = _bacc.Bacc("TRN2", target_bir_lowering=False, num_devices=1)
    aps = {}
    for name, a in arrays.items():
        aps[name] = nc.dram_tensor(f"in_{name}", a.shape, mybir.dt.from_np(a.dtype), kind="ExternalInput").ap()
    out = nc.dram_tensor("out_t", (KC, P, NX), F32, kind="ExternalOutput").ap()
    build(nc, aps, out)
    r = _run(nc, [{f"in_{k}": v for k, v in arrays.items()}], core_ids=[0])
    y = r.results[0]["out_t"]
    return y.reshape(1, D, NX).transpose(0, 2, 1)
```
